# Optimizing a Trainium2 kernel written in Bass

```python
import math
import jax, jax.numpy as jnp
from jax import lax
import numpy as np

D_MODEL = 1024
BATCH = 1
SEQ = 256
DEPTH = 4

N_MIXERS = 3
EPS = 1e-6
N_GLA = (DEPTH + 2) // 3
N_SGU = (DEPTH + 1) // 3
N_FOX = DEPTH // 3

GLA_HEADS = 4
GLA_DK = D_MODEL // (2 * GLA_HEADS)
GLA_DV = D_MODEL // GLA_HEADS
GLA_KD = GLA_HEADS * GLA_DK
GLA_VD = GLA_HEADS * GLA_DV
GLA_RANK = 16
GLA_NORMALIZER = 16.0
GLA_CHUNK = 64
GLA_IN = 2 * GLA_KD + 2 * GLA_VD + GLA_RANK

SGU_WIDTH = D_MODEL
SGU_GROUPS = 4
SGU_GDIM = SGU_WIDTH // SGU_GROUPS
SGU_CHUNK = 128
SGU_IN = 3 * SGU_WIDTH

FOX_HEADS = 16
FOX_DH = 64
FOX_AD = FOX_HEADS * FOX_DH
FOX_BLOCK = 128
FOX_IN = 4 * FOX_AD + FOX_HEADS
FORGET_BIAS_INIT = 2.0


def rms_norm(x, g):
    xf = x.astype(jnp.float32)
    xf = xf * lax.rsqrt(jnp.mean(xf * xf, axis=-1, keepdims=True) + EPS)
    return xf.astype(x.dtype) * g

def layer_norm(x, g, b):
    xf = x.astype(jnp.float32)
    mu = jnp.mean(xf, axis=-1, keepdims=True)
    var = jnp.mean(jnp.square(xf - mu), axis=-1, keepdims=True)
    return ((xf - mu) * lax.rsqrt(var + EPS)).astype(x.dtype) * g + b

def gla_mixer(h, w_in, w_a2, b_a, g_head, w_out):
    B, S, _ = h.shape
    H, DK, DV, C = GLA_HEADS, GLA_DK, GLA_DV, GLA_CHUNK
    N = S // C
    q, k, v, z, a_low = jnp.split(h @ w_in, [GLA_KD, 2 * GLA_KD, 2 * GLA_KD + GLA_VD,
                                             2 * GLA_KD + 2 * GLA_VD], axis=-1)
    log_a = jax.nn.log_sigmoid((a_low @ w_a2 + b_a).astype(jnp.float32)) / GLA_NORMALIZER
    q = q.astype(jnp.float32) * (DK ** -0.5)

    def to_chunks(t, d):
        return t.astype(jnp.float32).reshape(B, N, C, H, d).transpose(1, 0, 3, 2, 4)

    qc, kc, vc, gc = to_chunks(q, DK), to_chunks(k, DK), to_chunks(v, DV), to_chunks(log_a, DK)
    causal = jnp.tril(jnp.ones((C, C), dtype=bool))

    def step(state, xs):
        qb, kb, vb, gb = xs
        b = jnp.cumsum(gb, axis=2)
        o_inter = jnp.einsum('bhik,bhkv->bhiv', qb * jnp.exp(b), state)
        diff = b[:, :, :, None, :] - b[:, :, None, :, :]
        decay = jnp.exp(jnp.where(causal[:, :, None], diff, -jnp.inf))
        attn = jnp.einsum('bhik,bhjk,bhijk->bhij', qb, kb, decay)
        o = o_inter + jnp.einsum('bhij,bhjv->bhiv', attn, vb)
        b_last = b[:, :, -1:, :]
        state = (jnp.exp(b_last[:, :, 0, :])[..., None] * state
                 + jnp.einsum('bhjk,bhjv->bhkv', kb * jnp.exp(b_last - b), vb))
        return state, o

    state0 = jnp.zeros((B, H, DK, DV), jnp.float32)
    _, o = lax.scan(step, state0, (qc, kc, vc, gc))
    o = o.transpose(1, 0, 3, 2, 4).reshape(B, S, H, DV)
    o = rms_norm(o, g_head).reshape(B, S, GLA_VD).astype(h.dtype)
    return (o * jax.nn.silu(z)) @ w_out

def sgu_mixer(h, w_in, ln_g, ln_b, w_s, b_s, w_out):
    B, S, _ = h.shape
    C, G, Dg = SGU_CHUNK, SGU_GROUPS, SGU_GDIM
    N = S // C
    u, v, z = jnp.split(h @ w_in, 3, axis=-1)
    u = jax.nn.gelu(u)
    v = layer_norm(jax.nn.gelu(v), ln_g, ln_b)
    w_causal = jnp.where(jnp.tril(jnp.ones((C, C), dtype=bool))[None], w_s, 0.0)
    vc = v.reshape(B, N, C, G, Dg)
    mixed = jnp.einsum('gts,bnsgd->bntgd', w_causal, vc) + b_s.T[None, None, :, :, None]
    sg = u * mixed.reshape(B, S, SGU_WIDTH)
    return (sg * jax.nn.silu(z)) @ w_out

def fox_mixer(h, w_in, b_f, g_q, g_k, w_out):
    B, S, _ = h.shape
    H, Dh, BLK = FOX_HEADS, FOX_DH, FOX_BLOCK
    q, k, v, z, f_logit = jnp.split(h @ w_in, [FOX_AD, 2 * FOX_AD, 3 * FOX_AD, 4 * FOX_AD], axis=-1)
    q = rms_norm(q.reshape(B, S, H, Dh), g_q).transpose(0, 2, 1, 3)
    k = rms_norm(k.reshape(B, S, H, Dh), g_k).transpose(0, 2, 1, 3)
    v = v.reshape(B, S, H, Dh).transpose(0, 2, 1, 3)
    log_f = jax.nn.log_sigmoid((f_logit + b_f).astype(jnp.float32))
    F = jnp.cumsum(log_f, axis=1).transpose(0, 2, 1)
    scale = Dh ** -0.5
    outs = []
    for i in range(S // BLK):
        lo, hi = i * BLK, (i + 1) * BLK
        s = jnp.einsum('bhqd,bhkd->bhqk', q[:, :, lo:hi], k[:, :, :hi]).astype(jnp.float32) * scale
        s = s + F[:, :, lo:hi, None] - F[:, :, None, :hi]
        causal = (lo + jnp.arange(BLK))[:, None] >= jnp.arange(hi)[None, :]
        p = jax.nn.softmax(jnp.where(causal, s, -jnp.inf), axis=-1).astype(v.dtype)
        outs.append(jnp.einsum('bhqk,bhkd->bhqd', p, v[:, :, :hi]))
    o = jnp.concatenate(outs, axis=2).transpose(0, 2, 1, 3).reshape(B, S, FOX_AD)
    return (o * jax.nn.silu(z)) @ w_out

def first_inputs(seed: int = 0) -> dict:
    key = jax.random.key(seed)
    ks = jax.random.split(key, 32)
    D = D_MODEL
    nrm = lambda k, shape, s: jax.random.normal(k, shape, jnp.float32) * s
    return {
        "x": nrm(ks[0], (BATCH, SEQ, D), 1.0),
        "c": nrm(ks[1], (BATCH, D), 1.0),
        "norm_pre_g": 1.0 + nrm(ks[2], (DEPTH, D), 0.1),
        "norm_post_g": 1.0 + nrm(ks[3], (DEPTH, D), 0.1),
        "w_mod": nrm(ks[4], (DEPTH, D, 3 * D), D ** -0.5),
        "b_mod": nrm(ks[5], (DEPTH, 3 * D), 0.01),
        "gla_w_in": nrm(ks[6], (N_GLA, D, GLA_IN), D ** -0.5),
        "gla_w_a2": nrm(ks[7], (N_GLA, GLA_RANK, GLA_KD), GLA_RANK ** -0.5),
        "gla_b_a": nrm(ks[8], (N_GLA, GLA_KD), 0.1),
        "gla_g_head": 1.0 + nrm(ks[9], (N_GLA, GLA_HEADS, GLA_DV), 0.1),
        "gla_w_out": nrm(ks[10], (N_GLA, GLA_VD, D), GLA_VD ** -0.5),
        "sgu_w_in": nrm(ks[11], (N_SGU, D, SGU_IN), D ** -0.5),
        "sgu_ln_g": 1.0 + nrm(ks[12], (N_SGU, SGU_WIDTH), 0.1),
        "sgu_ln_b": nrm(ks[13], (N_SGU, SGU_WIDTH), 0.1),
        "sgu_w_s": nrm(ks[14], (N_SGU, SGU_GROUPS, SGU_CHUNK, SGU_CHUNK), SGU_CHUNK ** -0.5),
        "sgu_b_s": 1.0 + nrm(ks[15], (N_SGU, SGU_GROUPS, SGU_CHUNK), 0.1),
        "sgu_w_out": nrm(ks[16], (N_SGU, SGU_WIDTH, D), SGU_WIDTH ** -0.5),
        "fox_w_in": nrm(ks[17], (N_FOX, D, FOX_IN), D ** -0.5),
        "fox_b_f": FORGET_BIAS_INIT + nrm(ks[18], (N_FOX, FOX_HEADS), 0.1),
        "fox_g_q": 1.0 + nrm(ks[19], (N_FOX, FOX_DH), 0.1),
        "fox_g_k": 1.0 + nrm(ks[20], (N_FOX, FOX_DH), 0.1),
        "fox_w_out": nrm(ks[21], (N_FOX, FOX_AD, D), FOX_AD ** -0.5),
    }

def first_block(x, c, norm_pre_g, norm_post_g, w_mod, b_mod,
              gla_w_in, gla_w_a2, gla_b_a, gla_g_head, gla_w_out,
              sgu_w_in, sgu_ln_g, sgu_ln_b, sgu_w_s, sgu_b_s, sgu_w_out,
              fox_w_in, fox_b_f, fox_g_q, fox_g_k, fox_w_out):
    cond = jax.nn.silu(c)
    for i in range(DEPTH):
        mod = (cond @ w_mod[i] + b_mod[i])[:, None, :]
        shift, scale, gate = jnp.split(mod, 3, axis=-1)
        h = rms_norm(x, norm_pre_g[i]) * (1.0 + scale) + shift
        kind, j = i % N_MIXERS, i // N_MIXERS
        if kind == 0:
            o = gla_mixer(h, gla_w_in[j], gla_w_a2[j], gla_b_a[j], gla_g_head[j], gla_w_out[j])
        elif kind == 1:
            o = sgu_mixer(h, sgu_w_in[j], sgu_ln_g[j], sgu_ln_b[j], sgu_w_s[j], sgu_b_s[j], sgu_w_out[j])
        else:
            o = fox_mixer(h, fox_w_in[j], fox_b_f[j], fox_g_q[j], fox_g_k[j], fox_w_out[j])
        x = x + gate * rms_norm(o, norm_post_g[i])
    return x


DEPTH_2 = 1

D_CONV = D_MODEL
CONV_WIDTH = 3
HEAD_DIM = 64
HEADS_PER_GROUP = 8
DILATED_GROUPS = ((128, 1), (512, 4), (2048, 16))
N_ATTN_HEADS = HEADS_PER_GROUP * len(DILATED_GROUPS)
D_ATTN = N_ATTN_HEADS * HEAD_DIM
D_ATTN_OUT = HEADS_PER_GROUP * HEAD_DIM
BLOCK = 128
ROT_DIM = HEAD_DIM // 4
ROPE_THETA = 500000.0
PEER_HEADS = 8
PEER_N_KEYS = 128
PEER_N_EXPERTS = PEER_N_KEYS * PEER_N_KEYS
PEER_TOPK = 16
PEER_D_HALF = 128
PEER_D_QUERY = 2 * PEER_D_HALF
PEER_CHUNK = 128
RMS_EPS = 1e-6


def rms_norm_2(x, g):
    xf = x.astype(jnp.float32)
    y = xf * lax.rsqrt(jnp.mean(xf * xf, axis=-1, keepdims=True) + RMS_EPS)
    return (y * g.astype(jnp.float32)).astype(x.dtype)

def partial_rotary(t, positions):
    half = ROT_DIM // 2
    inv_freq = ROPE_THETA ** (-jnp.arange(half, dtype=jnp.float32) * (2.0 / ROT_DIM))
    ang = positions.astype(jnp.float32)[..., None] * inv_freq
    cos = jnp.cos(ang)[:, :, None, :]
    sin = jnp.sin(ang)[:, :, None, :]
    tr = t[..., :ROT_DIM].astype(jnp.float32)
    t1, t2 = tr[..., :half], tr[..., half:]
    rot = jnp.concatenate([t1 * cos - t2 * sin, t2 * cos + t1 * sin], axis=-1).astype(t.dtype)
    return jnp.concatenate([rot, t[..., ROT_DIM:]], axis=-1)

def dilated_window_attention(q, k, v, window, dilation):
    B, S, H, Dh = q.shape
    steps = window // dilation
    span = dilation * BLOCK
    sp = -(-S // span) * span
    nb = sp // span

    def blocks(t):
        t = jnp.pad(t, ((0, 0), (0, sp - S), (0, 0), (0, 0)))
        return t.reshape(B, nb, BLOCK, dilation, H, Dh)

    def with_prev(t):
        prev = jnp.pad(t, ((0, 0), (1, 0), (0, 0), (0, 0), (0, 0), (0, 0)))[:, :-1]
        return jnp.concatenate([prev, t], axis=2)

    qb = blocks(q)
    kk = with_prev(blocks(k))
    vv = with_prev(blocks(v))
    s = jnp.einsum('bnqrhd,bnkrhd->bnrhqk', qb, kk,
                   preferred_element_type=jnp.float32) * (Dh ** -0.5)
    qi = np.arange(BLOCK)[:, None]
    ki = np.arange(2 * BLOCK)[None, :]
    dist = BLOCK + qi - ki
    band = (dist >= 0) & (dist <= steps)
    valid = band[None] & ((np.arange(nb)[:, None, None] > 0) | (ki >= BLOCK)[None])
    s = jnp.where(valid[None, :, None, None], s, -jnp.inf)
    m = jnp.max(s, axis=-1, keepdims=True)
    p = jnp.exp(s - m)
    l = jnp.sum(p, axis=-1, keepdims=True)
    o = jnp.einsum('bnrhqk,bnkrhd->bnqrhd', (p / l).astype(v.dtype), vv)
    o = o.reshape(B, sp, H, Dh)[:, :S]
    lse = (m + jnp.log(l))[..., 0]
    lse = lse.transpose(0, 1, 4, 2, 3).reshape(B, sp, H)[:, :S]
    return o, lse

def hybrid_mixer(u, positions, w_in, conv_w, w_conv_out, w_attn_out, gate_bias, w_out):
    B, S, _ = u.shape
    sizes = [D_CONV, D_CONV, D_CONV, D_ATTN, D_ATTN, D_ATTN, D_MODEL, D_MODEL]
    split_points = [int(c) for c in np.cumsum(sizes)[:-1]]
    proj = u @ w_in
    b_gate, c_gate, xc, q, k, v, g_conv, g_attn = jnp.split(proj, split_points, axis=-1)

    z = c_gate * xc
    zp = jnp.pad(z, ((0, 0), (CONV_WIDTH - 1, 0), (0, 0)))
    conv = sum(conv_w[i] * zp[:, i:i + S] for i in range(CONV_WIDTH))
    y_conv = (b_gate * conv) @ w_conv_out

    q = partial_rotary(q.reshape(B, S, N_ATTN_HEADS, HEAD_DIM), positions)
    k = partial_rotary(k.reshape(B, S, N_ATTN_HEADS, HEAD_DIM), positions)
    v = v.reshape(B, S, N_ATTN_HEADS, HEAD_DIM)
    outs, lses = [], []
    for g, (window, dilation) in enumerate(DILATED_GROUPS):
        sl = slice(g * HEADS_PER_GROUP, (g + 1) * HEADS_PER_GROUP)
        o_g, lse_g = dilated_window_attention(q[:, :, sl], k[:, :, sl], v[:, :, sl], window, dilation)
        outs.append(o_g)
        lses.append(lse_g)
    wts = jax.nn.softmax(jnp.stack(lses, axis=0), axis=0)
    o = jnp.einsum('gbsh,gbshd->bshd', wts.astype(v.dtype), jnp.stack(outs, axis=0))
    y_attn = o.reshape(B, S, D_ATTN_OUT) @ w_attn_out

    merged = (jax.nn.sigmoid(g_conv + gate_bias[0]) * y_conv
              + jax.nn.sigmoid(g_attn + gate_bias[1]) * y_attn)
    return merged @ w_out

def peer_ffn(u, w_query, sub_keys, expert_down, expert_up):
    B, S, D = u.shape
    T = B * S
    xf = u.reshape(T, D)
    q = (xf @ w_query).reshape(T, PEER_HEADS, 2, PEER_D_HALF)
    s = jnp.einsum('thcd,hckd->thck', q, sub_keys, preferred_element_type=jnp.float32)
    top_s, top_i = lax.top_k(s, PEER_TOPK)
    cand_s = (top_s[:, :, 0, :, None] + top_s[:, :, 1, None, :]).reshape(T, PEER_HEADS, PEER_TOPK * PEER_TOPK)
    cand_i = (top_i[:, :, 0, :, None] * PEER_N_KEYS + top_i[:, :, 1, None, :]).reshape(T, PEER_HEADS, PEER_TOPK * PEER_TOPK)
    best_s, pos = lax.top_k(cand_s, PEER_TOPK)
    idx = jnp.take_along_axis(cand_i, pos, axis=-1)
    gates = jax.nn.softmax(best_s, axis=-1).astype(u.dtype)
    hk = PEER_HEADS * PEER_TOPK
    xr = xf.reshape(-1, PEER_CHUNK, D)
    ir = idx.reshape(-1, PEER_CHUNK, hk)
    gr = gates.reshape(-1, PEER_CHUNK, hk)

    def chunk(args):
        xc, ic, gc = args
        a = jax.nn.gelu(jnp.einsum('cd,ced->ce', xc, expert_down[ic]), approximate=False)
        return jnp.einsum('ce,ced->cd', gc * a, expert_up[ic])

    return lax.map(chunk, (xr, ir, gr)).reshape(B, S, D)

def second_inputs(seed: int = 0) -> dict:
    key = jax.random.key(seed)
    ks = jax.random.split(key, 16)
    f32 = jnp.float32
    d_in = 3 * D_CONV + 3 * D_ATTN + 2 * D_MODEL
    x = jax.random.normal(ks[0], (BATCH, SEQ, D_MODEL), f32)
    offset = jax.random.randint(ks[1], (BATCH, 1), 0, 1024, dtype=jnp.int32)
    positions = (offset + jnp.arange(SEQ, dtype=jnp.int32)[None, :]).astype(jnp.int32)
    norm_mix = 1.0 + 0.01 * jax.random.normal(ks[2], (DEPTH_2, D_MODEL), f32)
    w_in = jax.random.normal(ks[3], (DEPTH_2, D_MODEL, d_in), f32) * D_MODEL ** -0.5
    conv_w = jax.random.normal(ks[4], (DEPTH_2, CONV_WIDTH, D_CONV), f32) * CONV_WIDTH ** -0.5
    w_conv_out = jax.random.normal(ks[5], (DEPTH_2, D_CONV, D_MODEL), f32) * D_CONV ** -0.5
    w_attn_out = jax.random.normal(ks[6], (DEPTH_2, D_ATTN_OUT, D_MODEL), f32) * D_ATTN_OUT ** -0.5
    gate_bias = 0.01 * jax.random.normal(ks[7], (DEPTH_2, 2, D_MODEL), f32)
    w_out = jax.random.normal(ks[8], (DEPTH_2, D_MODEL, D_MODEL), f32) * D_MODEL ** -0.5
    norm_ffn = 1.0 + 0.01 * jax.random.normal(ks[9], (DEPTH_2, D_MODEL), f32)
    peer_w_query = jax.random.normal(ks[10], (DEPTH_2, D_MODEL, PEER_HEADS * PEER_D_QUERY), f32) * D_MODEL ** -0.5
    peer_sub_keys = jax.random.normal(ks[11], (DEPTH_2, PEER_HEADS, 2, PEER_N_KEYS, PEER_D_HALF), f32) * PEER_D_HALF ** -0.5
    peer_down = jax.random.normal(ks[12], (DEPTH_2, PEER_N_EXPERTS, D_MODEL), f32) * D_MODEL ** -0.5
    peer_up = jax.random.normal(ks[13], (DEPTH_2, PEER_N_EXPERTS, D_MODEL), f32) * PEER_HEADS ** -0.5
    final_norm = 1.0 + 0.01 * jax.random.normal(ks[14], (D_MODEL,), f32)
    return {"x": x, "positions": positions, "norm_mix": norm_mix, "w_in": w_in,
            "conv_w": conv_w, "w_conv_out": w_conv_out, "w_attn_out": w_attn_out,
            "gate_bias": gate_bias, "w_out": w_out, "norm_ffn": norm_ffn,
            "peer_w_query": peer_w_query, "peer_sub_keys": peer_sub_keys,
            "peer_down": peer_down, "peer_up": peer_up, "final_norm": final_norm}

def second_block(x, positions, norm_mix, w_in, conv_w, w_conv_out, w_attn_out, gate_bias, w_out,
              norm_ffn, peer_w_query, peer_sub_keys, peer_down, peer_up, final_norm):
    h = x
    for layer in range(DEPTH_2):
        h = h + hybrid_mixer(rms_norm_2(h, norm_mix[layer]), positions, w_in[layer], conv_w[layer],
                             w_conv_out[layer], w_attn_out[layer], gate_bias[layer], w_out[layer])
        h = h + peer_ffn(rms_norm_2(h, norm_ffn[layer]), peer_w_query[layer], peer_sub_keys[layer],
                         peer_down[layer], peer_up[layer])
    return rms_norm_2(h, final_norm)


def setup_inputs(seed=0):
    out = dict(first_inputs(seed))
    for name, value in second_inputs(seed + 1).items():
        if name != "x":
            out[name + "_2"] = value
    return out


def reference(
    x, c, norm_pre_g, norm_post_g, w_mod, b_mod, gla_w_in, gla_w_a2, gla_b_a, gla_g_head,
    gla_w_out, sgu_w_in, sgu_ln_g, sgu_ln_b, sgu_w_s, sgu_b_s, sgu_w_out, fox_w_in, fox_b_f,
    fox_g_q, fox_g_k, fox_w_out, positions_2, norm_mix_2, w_in_2, conv_w_2, w_conv_out_2,
    w_attn_out_2, gate_bias_2, w_out_2, norm_ffn_2, peer_w_query_2, peer_sub_keys_2,
    peer_down_2, peer_up_2, final_norm_2,
):
    x = first_block(
        x, c, norm_pre_g, norm_post_g, w_mod, b_mod, gla_w_in, gla_w_a2, gla_b_a, gla_g_head,
        gla_w_out, sgu_w_in, sgu_ln_g, sgu_ln_b, sgu_w_s, sgu_b_s, sgu_w_out, fox_w_in, fox_b_f,
        fox_g_q, fox_g_k, fox_w_out,
    )
    return second_block(
        x, positions_2, norm_mix_2, w_in_2, conv_w_2, w_conv_out_2, w_attn_out_2, gate_bias_2,
        w_out_2, norm_ffn_2, peer_w_query_2, peer_sub_keys_2, peer_down_2, peer_up_2,
        final_norm_2,
    )


_drawn_inputs = setup_inputs


def setup_inputs(seed=0):
    import zlib

    import numpy as np

    out = dict(_drawn_inputs(seed))
    spreads = {}
    factors = {'fox_b_f': 2.865,
     'norm_mix_2': 15.166,
     'gate_bias_2': 33.517,
     'norm_ffn_2': 112.72,
     'final_norm_2': 185.467,
     'peer_w_query_2': 2.916,
     'peer_sub_keys_2': 2.883,
     'peer_down_2': 3.521,
     'peer_up_2': 2.864,
     'w_attn_out_2': 4.625}
    for name, (base, spread) in spreads.items():
        noise = np.random.default_rng([zlib.crc32(name.encode()), seed]).standard_normal(out[name].shape)
        drawn = base * np.exp(spread * noise) if base else spread * noise
        out[name] = __import__('jax').numpy.asarray(drawn.astype(out[name].dtype))
    for name, factor in factors.items():
        out[name] = (out[name] * factor).astype(out[name].dtype)
    return out
```

```python
from contextlib import ExitStack

import numpy as np
import concourse.bass as bass
from concourse import mybir

F32 = mybir.dt.float32
I32 = mybir.dt.int32
U32 = mybir.dt.uint32
ALU = mybir.AluOpType
ACT = mybir.ActivationFunctionType
X = mybir.AxisListType.X
ds = bass.ds

P = 128
T = 2
D = 1024
KC = D // P
N = 512
EPS = 1e-6
DEPTH = 4
GH, DK, DV = 4, 128, 256
RANK = 16
LEVELS = 7
SG = 4
AH, DH = 16, 64
NG, GHD = 3, 8
ROT = 8
PH, TOPK, NK = 8, 16, 128
SLOTS = 8
MAGIC = 1.5 * 2.0 ** 23
TWO_PI = (6.28125, 1.9340515136718750e-3, 1.2556659146e-6)
PI_SAFE = 3.1415925

BLOCKS = {}
_at = 0
for _name, _n in (("in0", 6), ("out0", 2), ("in1", 6), ("out1", 2), ("in2", 8), ("out2", 2),
                  ("in3", 6), ("out3", 2), ("hyb_a", 6), ("hyb_b", 13), ("conv", 2), ("attn", 1),
                  ("hyb_out", 2), ("query", 4)):
    BLOCKS[_name] = _at
    _at += _n


def constants():
    i = np.arange(P)
    row, col = i[:, None], i[None, :]
    ident = np.eye(P, dtype=np.float32)
    sum_mask = (row <= col).astype(np.float32)
    gla = np.zeros((P, LEVELS + 1, P), np.int32)
    gla[:, 0] = row == col
    for l in range(LEVELS):
        size = 1 << l
        same = row // (2 * size) == col // (2 * size)
        gla[:, l + 1] = same & (row // size % 2 == 0) & (col // size % 2 == 1)
    att = np.zeros((P, 4, 3, P), np.float32)
    for n, (steps, dil) in enumerate(((10 ** 6, 1), (128, 1), (128, 4), (128, 16))):
        own, back = row - col, row + P - col
        for part, dist in enumerate((own, back, own)):
            ok = (dist >= 0) & (dist <= steps * dil) & (dist % dil == 0)
            att[:, n, part] = np.where(ok, 0.0, -1e30)
    inv = (np.float32(500000.0) ** (-np.arange(ROT, dtype=np.float32) * np.float32(2.0 / 16)))
    return {
        "k_ident": ident, "k_sum": sum_mask, "k_gla": gla, "k_att": att.reshape(P, 4 * 3 * P),
        "k_freq": inv.astype(np.float32).reshape(1, ROT),
        "k_iota": np.arange(TOPK, dtype=np.float32).reshape(1, TOPK),
    }


def build(nc, A, out, stop=99):
    with ExitStack() as ctx:
        def sb(name, shape, dt=F32):
            return ctx.enter_context(nc.sbuf_tensor(name, shape, dt))

        sems = {}

        def S(name):
            if name not in sems:
                sems[name] = ctx.enter_context(nc.semaphore(name))
            return sems[name]

        ring = sb("ring", [P, 2, KC * N])
        mring = sb("mring", [P, 2, KC, N // 2])
        acc = sb("acc", [P, 3 * D])
        x = sb("x", [P, T, D])
        hT = sb("hT", [P, KC, T * P])
        gateb = sb("gateb", [P, 2, D])
        gpost = sb("gpost", [P, D])
        ghead = sb("ghead", [P, D])
        lng = sb("lng", [P, D])
        lnb = sb("lnb", [P, D])
        gbias = sb("gbias", [P, 2, D])
        nffn, fin = lng, lnb
        big = sb("big", [P, 19584])
        ident = sb("ident", [P, P])
        ones = sb("ones", [P, P])
        summ = sb("summ", [P, P])
        gmask = sb("gmask", [P, LEVELS + 1, P], I32)
        amask = sb("amask", [P, 4, 3 * P])
        rows = sb("rows", [72, P])
        cols = sb("cols", [P, 72])
        cond = sb("cond", [P, KC])
        modc = sb("modc", [P, 2, 2, KC])
        wlow = sb("wlow", [P, 3, KC, RANK])
        wa2 = sb("wa2", [RANK + 1, 2, GH * DK])
        alT = sb("alT", [RANK + 1, T * P])
        low = sb("low", [P, T, RANK])
        low2 = sb("low2", [P, T, RANK])
        bs = sb("bs", [P, SG])
        bf = sb("bf", [P, AH])
        gqk = sb("gqk", [P, 2, DH])
        freq = sb("freq", [P, ROT])
        iota = sb("iota", [P, TOPK])
        posi = sb("posi", [P, T], I32)
        posf = sb("posf", [P, T])
        ssq = sb("ssq", [P, 64])
        rstd = sb("rstd", [P, 64])
        newton = sb("newton", [P, 64])
        small = sb("small", [P, 8])
        trig = sb("trig", [P, 2, T * ROT])
        anm = sb("anm", [P, 10, 8])
        al = sb("al", [P, 10, 8])
        arl = sb("arl", [P, 8])
        lse = sb("lse", [P, 2, NG * 16])
        lsm = sb("lsm", [P, 16])
        pv = sb("pv", [P, 2, TOPK])
        pix = sb("pix", [P, 2, TOPK], U32)
        pixf = sb("pixf", [P, 2, TOPK])
        pbest = sb("pbest", [P, 2, TOPK])
        pneg = sb("pneg", [P, 2, 1])
        ppos = sb("ppos", [P, TOPK], U32)
        pab = sb("pab", [P, 2, TOPK], U32)
        pabf = sb("pabf", [P, 2, TOPK])
        psel = sb("psel", [P, 2, TOPK])
        pidf = sb("pidf", [P, TOPK])
        idx = sb("idx", [P, 2, TOPK], U32)

        pex = gpost[:, 0:32].rearrange("p (a b) -> p a b", a=2)
        pa = gpost[:, 32:64].rearrange("p (a b) -> p a b", a=2)
        pcoef = gpost[:, 64:96].rearrange("p (a b) -> p a b", a=2)
        psm = gpost[:, 96:98].rearrange("p (a b) -> p a b", a=2)
        sqf = gpost[:, 100:100 + 2 * T]

        bank = [ctx.enter_context(nc.psum_tensor(f"bank{i}", [P, N], F32)) for i in range(8)]

        def at(off, *shape):
            size = int(np.prod(shape))
            v = big[:, off:off + size]
            if len(shape) == 2:
                return v.rearrange("p (a b) -> p a b", b=shape[1])
            if len(shape) == 3:
                return v.rearrange("p (a b c) -> p a b c", b=shape[1], c=shape[2])
            if len(shape) == 4:
                return v.rearrange("p (a b c d) -> p a b c d", b=shape[1], c=shape[2], d=shape[3])
            return v

        ob = at(0, T, D)
        xn = at(2 * D, T, D)
        g_in = at(0, T, 3 * D)
        W0 = 6 * D
        b_ = at(W0, GH, T * P)
        qT = at(W0 + D, GH, T * P)
        kT = at(W0 + 2 * D, GH, T * P)
        Q = [at(W0 + 3 * D + i * D, GH * T * P) for i in (0, 1)]
        K = [at(W0 + 5 * D + i * D, GH * T * P) for i in (0, 1)]
        Dd = [at(W0 + 7 * D + i * D, GH * T * P) for i in (0, 1)]
        AT = at(W0 + 9 * D, T, GH * P)
        AX = at(W0 + 10 * D, GH, P)
        ws = at(W0, SG, P)
        wsT = at(W0 + N, SG, P)
        f_in = at(0, T, 4 * D)
        qa = at(8 * D, T, AH, DH + 2)
        ka = at(8 * D + T * AH * (DH + 2), T, AH, DH + 2)
        WF = 8 * D + 2 * T * AH * (DH + 2)
        fo = at(WF + 5 * D, T, D)
        sqs = at(WF, 2, T * D)
        ha = at(0, T, 3 * D)
        hb = at(6 * D, T, 6656)
        QO, KO, VO, GC, GA = 0, 1536, 3072, 4608, 5632
        zT = mring[:, :, :, :].rearrange("p a k n -> p (a k n)")[:, 0:KC * 258].rearrange(
            "p (k n) -> p k n", n=258)
        od = acc[:, :].rearrange("p (t g n) -> p t g n", t=T, g=NG)
        fox_bufs = (at(WF, 4, T * P), at(WF + D, 4, T * P), at(WF + 2 * D, 4, 3 * P),
                    at(WF + 2 * D + 12 * P, 3, 4, P))
        hyb_bufs = (at(D, 4, T * P), at(2 * D, 4, T * P), at(4 * D, 4, 3 * P),
                    mring[:, :, :, :].rearrange("p a k n -> p (a k n)")[:, 2064:2064 + 12 * P].rearrange(
                        "p (b h n) -> p b h n", b=3, h=4))

        def bufs(n):
            return fox_bufs if n < 4 else hyb_bufs
        pk = at(2 * D, 2 * P)
        pk2 = at(2 * D + 256, 2 * P)
        cand = at(2 * D + 512, TOPK, TOPK)
        cand2 = at(2 * D + 768, TOPK * TOPK)
        hot = at(3 * D, 2, TOPK, TOPK)
        diag = ghead[:, 0:4 * P].rearrange("p (s n) -> p s n", n=P)
        zero = ghead[:, 4 * P:5 * P]
        qq = at(0, T, 2 * D)
        u = at(4 * D, T, D)
        pqT = at(6 * D, 2 * PH, T * P)
        skT = at(10 * D, 2 * PH, P)
        skr = at(12 * D, 2 * PH, P)
        sc = at(14 * D, T, 2 * D)
        up = at(6 * D, SLOTS, D)
        dn = ring[:, :, :].rearrange("p a n -> p (a n)").rearrange("p (s d) -> p s d", d=D)

        block = ctx.enter_context(nc.Block())

        CONSTS = 10 + SG + T + 2
        LINKS, BEST = 20, 11
        ORDER = {}

        def orderer(eng, name):
            ORDER[name] = 0

            def link(ins, wait=True):
                ORDER[name] += 1
                ins.then_inc(S(name), 1)
                if wait:
                    eng.wait_ge(S(name), ORDER[name])
            return link

        NORMS = ["norm0", "head0", "post0", "norm1", "ln", "post1", "norm2", "qk", "post2", "norm3", "head3",
                 "post3", "mix", "ffn", "final"]

        def nth(tag):
            return NORMS.index(tag) + 1

        @block.sync
        def _(sp):
            def load(dst, src, sem):
                sp.dma_start(dst, src).then_inc(S(sem), 16)

            load(rows[0:32, :], A["norm_pre_g"].rearrange("l (k p) -> (l k) p", p=P), "rows_in")
            load(rows[32:40, :], A["norm_mix_2"].rearrange("l (k p) -> (l k) p", p=P), "rows_in")
            load(rows[40:64, :], A["conv_w_2"][0].rearrange("i (k p) -> (i k) p", p=P), "rows_in")
            load(rows[64:72, :], A["c"].rearrange("b (k p) -> (b k) p", p=P), "rows_in")
            load(ident[:, :], A["k_ident"], "rows_in")
            load(x[:, :, :], A["x"][0].rearrange("(t p) d -> p t d", p=P), "x_in")

            def src_of(w, col):
                return w.rearrange("(k p) n -> p k n", p=P)[:, :, ds(col, N)]

            def put(slot, src):
                sp.dma_start(ring[:, slot, :].rearrange("p (k n) -> p k n", n=src.shape[2]), src) \
                    .then_inc(S(f"w_landed{slot}"), 16)

            def stream(name, n, w):
                b0 = BLOCKS[name]
                start = 0
                if b0 == 0:
                    put(0, src_of(w, 0))
                    put(1, src_of(w, N))
                    start = 1

                def pair(i):
                    for slot in range(2):
                        sp.wait_ge(S("proj_done1"), b0 + 2 * i + slot - 1)
                        put(slot, src_of(w, i * (2 * N) + slot * N))

                if n // 2 - start > 1:
                    with sp.Fori(start, n // 2) as i:
                        pair(i)
                elif n // 2 - start == 1:
                    pair(start)

            def one(b, src):
                sp.wait_ge(S("proj_done1"), b - 1)
                put(b % 2, src)

            stream("in0", 6, A["gla_w_in"][0])
            for n, (name, w, c0) in enumerate((("gla_w_in", 0, 3072), ("gla_w_in", 1, 3072),
                                               ("fox_w_in", 0, 4096))):
                load(wlow[:, n, :, :], A[name][w].rearrange("(k p) n -> p k n", p=P)[:, :, c0:c0 + RANK],
                     "wlow_in")
            for j in range(2):
                load(wa2[0:RANK, j, :], A["gla_w_a2"][j], "wlow_in")
                load(wa2[RANK:RANK + 1, j, :], A["gla_b_a"][j:j + 1, :], "wlow_in")
            load(gmask[:, :, :], A["k_gla"], "consts_in")
            load(summ[:, :], A["k_sum"], "consts_in")
            load(amask[:, :, :], A["k_att"].rearrange("p (a b) -> p a b", a=4), "consts_in")
            load(ghead[:, :], A["gla_g_head"][0:1].rearrange("a h v -> a (h v)").to_broadcast([P, D]), "ghead_in")
            load(lng[:, :], A["sgu_ln_g"].to_broadcast([P, D]), "consts_in")
            load(lnb[:, :], A["sgu_ln_b"].to_broadcast([P, D]), "consts_in")
            load(gqk[:, 0, :], A["fox_g_q"].to_broadcast([P, DH]), "consts_in")
            load(gqk[:, 1, :], A["fox_g_k"].to_broadcast([P, DH]), "consts_in")
            load(bf[:, :], A["fox_b_f"].to_broadcast([P, AH]), "consts_in")
            load(freq[:, :], A["k_freq"].to_broadcast([P, ROT]), "consts_in")
            load(iota[:, :], A["k_iota"].to_broadcast([P, TOPK]), "consts_in")
            for g in range(SG):
                load(bs[:, g:g + 1], A["sgu_b_s"][0, g:g + 1, :].rearrange("a p -> p a"), "consts_in")
            for t in range(T):
                load(posi[:, t:t + 1], A["positions_2"][:, t * P:(t + 1) * P].rearrange("a p -> p a"),
                     "consts_in")
            for i in range(2):
                load(gbias[:, i, :], A["gate_bias_2"][0, i:i + 1, :].to_broadcast([P, D]), "consts_in")
            if stop < 1:
                return
            stream("out0", 2, A["gla_w_out"][0])
            if stop < 2:
                return
            stream("in1", 6, A["sgu_w_in"][0])
            sp.wait_ge(S("x_ready"), 1)
            load(ws, A["sgu_w_s"][0].rearrange("g t s -> t g s"), "ws_in")
            stream("out1", 2, A["sgu_w_out"][0])
            if stop < 3:
                return
            stream("in2", 8, A["fox_w_in"][0])
            sp.wait_ge(S("x_ready"), 2)
            load(nffn[:, :], A["norm_ffn_2"].to_broadcast([P, D]), "last_rows_in")
            load(fin[:, :], A["final_norm_2"].rearrange("(a d) -> a d", a=1).to_broadcast([P, D]), "last_rows_in")
            stream("out2", 2, A["fox_w_out"][0])
            if stop < 4:
                return
            sp.wait_ge(S("gated"), 1)
            load(ghead[:, :], A["gla_g_head"][1:2].rearrange("a h v -> a (h v)").to_broadcast([P, D]), "ghead_in")
            stream("in3", 6, A["gla_w_in"][1])
            stream("out3", 2, A["gla_w_out"][1])
            if stop < 5:
                return
            stream("hyb_a", 6, A["w_in_2"][0])
            b0 = BLOCKS["hyb_b"]
            with sp.Fori(0, 6) as i:
                for slot in range(2):
                    sp.wait_ge(S("proj_done1"), b0 + 2 * i + slot - 1)
                    put(slot, src_of(A["w_in_2"][0], i * (2 * N) + (3 * D + slot * N)))
            one(b0 + 12, src_of(A["w_in_2"][0], 3 * D + 12 * N))
            one(BLOCKS["conv"], src_of(A["w_conv_out_2"][0], 0))
            one(BLOCKS["conv"] + 1, src_of(A["w_conv_out_2"][0], N))
            one(BLOCKS["attn"], A["w_attn_out_2"][0].rearrange("(k p) n -> p k n", p=P))
            stream("hyb_out", 2, A["w_out_2"][0])
            if stop < 6:
                return
            stream("query", 4, A["peer_w_query_2"][0])
            sp.wait_ge(S("merged"), 1)
            load(skr, A["peer_sub_keys_2"][0].rearrange("h c k d -> k (h c) d"), "sk_in")
            if stop < 7:
                return
            for t in range(T):
                sp.wait_ge(S("out_ready"), t + 1)
                sp.dma_start(out[0, t * P:(t + 1) * P, :], at(t * D, D)).then_inc(S("out_stored"), 16)
            sp.wait_ge(S("out_stored"), 16 * T)

        @block.gpsimd
        def _(pool):
            link = orderer(pool, "pool_order")
            link(nc.gpsimd.memset(ones[:, :], 1.0), wait=False)
            nc.gpsimd.memset(alT[:, :], 1.0).then_inc(S("ones_set"), 1)

            def modulation(L):
                if L:
                    pool.wait_ge(S("mod_read"), L)
                link(nc.gpsimd.memset(acc[:, :], 0.0))
                pool.dma_start(acc[0:1, :], A["b_mod"][L:L + 1, :]).then_inc(S("acc_init"), 16)
                if L:
                    pool.wait_ge(S("mod_ready"), L)
                pool.dma_start(gpost[:, :], A["norm_post_g"][L:L + 1, :].to_broadcast([P, D])) \
                    .then_inc(S("gpost_in"), 16)
                w = A["w_mod"][L].rearrange("(k p) n -> p k n", p=P)

                def pair(i, first=False):
                    for s in range(2):
                        if not first:
                            pool.wait_ge(S("mod_sum"), (L * 6 + i - 1) * 16 + 8 * (s + 1))
                        pool.dma_start(mring[:, s, :, :], w[:, :, ds(i * N + s * (N // 2), N // 2)]) \
                            .then_inc(S(f"mod_landed{s}"), 16)
                if L == 0:
                    pair(0, first=True)
                with pool.Fori(1 if L == 0 else 0, 6) as i:
                    pair(i)

            modulation(0)
            if stop < 1:
                return
            for L in range(1, DEPTH):
                if stop < L:
                    return
                modulation(L)
            if stop < 7:
                return
            for t in range(T):
                def two_heads(i):
                    for half in range(2):
                        h = i * 2 + half + t * PH
                        pool.wait_ge(S("idx_ready"), h + 1)
                        for kind, buf, tab in (("dn", dn, "peer_down_2"), ("up", up, "peer_up_2")):
                            for e in range(TOPK):
                                s = e % SLOTS
                                use = h * 2 + e // SLOTS
                                pool.wait_ge(S(f"{kind}_used{s}"), use + 1)
                                pool.nop(nofuse=True)
                                pool.indirect_dma_start(
                                    out=buf[:, s, :], out_offset=None, in_=A[tab][0],
                                    in_offset=bass.IndirectOffsetOnAxis(ap=idx[:, half, e:e + 1], axis=0)
                                ).then_inc(S(f"{kind}_landed{s}"), 16)
                with pool.Fori(0, PH // 2) as i:
                    two_heads(i)

        @block.tensor
        def _(pe):
            mm, tr = nc.tensor.matmul, nc.tensor.transpose

            def transpose_in(src, tag, chunks=KC, banks=(2, 3, 4, 5)):
                for k in range(chunks):
                    for t in range(T):
                        last = tr(bank[banks[k // 2]][:, (k % 2) * 256 + t * P:(k % 2) * 256 + (t + 1) * P],
                                  src(t, k), ident[:, :])
                    if k % 2:
                        last.then_inc(S(tag), 1)

            def block_products(b, slot, rhs, banks=(0, 1)):
                pe.wait_ge(S(f"w_landed{slot}"), (b - slot) * 8 + 16)
                for t in range(T):
                    pe.wait_ge(S(f"evac{t}"), b + 1)
                    for k in range(KC):
                        last = mm(bank[t][:, :], hT[:, k, t * P:(t + 1) * P], rhs(k),
                                  start=(k == 0), stop=(k == KC - 1))
                    last.then_inc(S(f"proj_done{t}"), 1)

            def project(name, n):
                b0 = BLOCKS[name]

                def pair(i):
                    for slot in range(2):
                        block_products(b0 + 2 * i + slot, slot,
                                       lambda k: ring[:, slot, k * N:(k + 1) * N])
                if n > 2:
                    with pe.Fori(0, n // 2) as i:
                        pair(i)
                else:
                    pair(0)

            def low_columns(n, tag):
                pe.wait_ge(S("wlow_in"), 7 * 16)
                for t in range(T):
                    for k in range(KC):
                        last = mm(bank[6][:, t * RANK:(t + 1) * RANK], hT[:, k, t * P:(t + 1) * P],
                                  wlow[:, n, k, :], start=(k == 0), stop=(k == KC - 1))
                last.then_inc(S(tag), 1)

            def mod_reduce(L):
                pe.wait_ge(S("mod_sum"), (L + 1) * 96)
                for j in range(2 * KC):
                    mm(bank[7][:, j:j + 1], acc[:, j * P:(j + 1) * P], ones[:, 0:1], start=True, stop=True)
                for i in range(2):
                    last = mm(bank[5 + i][:, :], ones[:, :], acc[:, 2 * D + i * N:2 * D + (i + 1) * N],
                              start=True, stop=True)
                last.then_inc(S("mod_read"), 1)

            def quad(n, q, k, v, kd):
                aqT, akT, aS, aPT = bufs(n)
                for i, (src, bk) in enumerate(((q, 2), (k, 4))):
                    for h in range(4):
                        for t in range(T):
                            last = tr(bank[bk + h // 2][0:kd, (h % 2) * 256 + t * P:(h % 2) * 256 + (t + 1) * P],
                                      src(h, t), ident[:, :])
                    last.then_inc(S("att_T"), 1)
                pe.wait_ge(S("att_qT"), n + 1)
                pe.wait_ge(S("att_kT"), n + 1)
                if n:
                    pe.wait_ge(S("att_o"), n)
                for h in range(4):
                    mm(bank[6][:, h * P:(h + 1) * P], aqT[0:kd, h, 0:P], akT[0:kd, h, 0:P], start=True, stop=True)
                for h in range(4):
                    last = mm(bank[(7, 2)[h // 2]][:, (h % 2) * 256:(h % 2 + 1) * 256],
                              aqT[0:kd, h, P:2 * P], akT[0:kd, h, :], start=True, stop=True)
                last.then_inc(S("att_s"), 1)
                pe.wait_ge(S("att_p"), n + 1)
                for b in range(3):
                    for h in range(4):
                        last = tr(bank[3 + b][:, h * P:(h + 1) * P], aS[:, h, b * P:(b + 1) * P], ident[:, :])
                    last.then_inc(S("att_pt"), 1)
                pe.wait_ge(S("att_pta"), n + 1)
                pe.wait_ge(S("att_ptv"), n + 1)
                for h in range(4):
                    mm(bank[6][:, h * DH:(h + 1) * DH], aPT[:, 0, h, :], v(h, 0), start=True, stop=True)
                for h in range(4):
                    o = bank[6][:, 256 + h * DH:256 + (h + 1) * DH]
                    mm(o, aPT[:, 1, h, :], v(h, 0), start=True, stop=False)
                    last = mm(o, aPT[:, 2, h, :], v(h, 1), start=False, stop=True)
                last.then_inc(S("att_pv"), 1)

            def gla(L, j):
                low_columns(j, "low")
                pe.wait_ge(S("low_sb"), L // 3 + 1)
                for t in range(T):
                    last = tr(bank[7][0:RANK, t * P:(t + 1) * P], low[:, t, :], ident[:, :])
                last.then_inc(S("lowT"), 1)
                pe.wait_ge(S("alT"), L // 3 + 1)
                for h in range(GH):
                    last = mm(bank[6 + h // 2][:, (h % 2) * 256:(h % 2 + 1) * 256],
                              wa2[:, j, h * DK:(h + 1) * DK], alT[:, :], start=True, stop=True)
                last.then_inc(S("decay"), 1)
                for t in range(T):
                    pe.wait_ge(S(f"evac{t}"), BLOCKS[f"out{L}"] + 1)
                for i in range(2):
                    for h in range(GH):
                        for t in range(T):
                            last = tr(bank[2 + 2 * i + h // 2][:, (h % 2) * 256 + t * P:(h % 2) * 256 + (t + 1) * P],
                                      g_in[:, t, i * N + h * DK:i * N + (h + 1) * DK], ident[:, :])
                last.then_inc(S("qkT"), 1)
                pe.wait_ge(S("qkT_sb"), L // 3 + 1)
                pe.wait_ge(S("logd"), L // 3 + 1)
                for lv in range(LEVELS + 2):
                    q_, k_ = (qT, kT) if lv == 0 else (
                        Q[lv % 2].rearrange("p (h n) -> p h n", h=GH), K[lv % 2].rearrange("p (h n) -> p h n", h=GH))
                    if lv:
                        pe.wait_ge(S("lvl_qk"), L // 3 * (LEVELS + 1) + lv)
                    if lv >= 2:
                        pe.wait_ge(S("lvl_read"), L // 3 * (LEVELS + 1) + lv - 1)
                    b0 = (6, 2)[lv % 2]
                    if lv <= LEVELS:
                        for t in range(T):
                            for h in range(GH):
                                last = mm(bank[b0 + t][:, h * P:(h + 1) * P], k_[:, h, t * P:(t + 1) * P],
                                          q_[:, h, t * P:(t + 1) * P], start=True, stop=True)
                    else:
                        for h in range(GH):
                            last = mm(bank[b0][:, h * P:(h + 1) * P], k_[:, h, 0:P], q_[:, h, P:2 * P],
                                      start=True, stop=True)
                    last.then_inc(S("lvl"), 1)
                pe.wait_ge(S("attn_sb"), L // 3 + 1)
                for t in range(T):
                    for h in range(GH):
                        o = bank[2 + 2 * t + h // 2][:, (h % 2) * 256:(h % 2 + 1) * 256]
                        last = mm(o, AT[:, t, h * P:(h + 1) * P], g_in[:, t, D + h * DV:D + (h + 1) * DV],
                                  start=True, stop=(t == 0))
                        if t:
                            last = mm(o, AX[:, h, :], g_in[:, 0, D + h * DV:D + (h + 1) * DV],
                                      start=False, stop=True)
                last.then_inc(S("gla_o"), 1)

            def sgu():
                pe.wait_ge(S("ws_in"), 16)
                pe.wait_ge(S("hT"), 2)
                for g in range(SG):
                    last = tr(bank[2][:, g * P:(g + 1) * P], ws[:, g, :], ident[:, :])
                last.then_inc(S("wsT"), 1)
                pe.wait_ge(S("ln_done"), 1)
                for t in range(T):
                    for g in range(SG):
                        last = mm(bank[2 + 2 * t + g // 2][:, (g % 2) * 256:(g % 2 + 1) * 256],
                                  wsT[:, g, :], g_in[:, t, D + g * 256:D + (g + 1) * 256],
                                  start=True, stop=True)
                last.then_inc(S("mixed"), 1)

            def fox():
                low_columns(2, "low")
                pe.wait_ge(S("logf"), 1)
                pe.wait_ge(S("consts_in"), CONSTS * 16)
                mm(bank[7][:, 0:AH], summ[:, :], low2[:, 0, :], start=True, stop=True)
                mm(bank[7][:, AH:2 * AH], ones[:, :], low2[:, 0, :], start=True, stop=False)
                mm(bank[7][:, AH:2 * AH], summ[:, :], low2[:, 1, :], start=False, stop=True) \
                    .then_inc(S("fsum"), 1)
                pe.wait_ge(S("qka"), 1)
                for n in range(4):
                    quad(n, lambda h, t: qa[:, t, 4 * n + h, :], lambda h, t: ka[:, t, 4 * n + h, :],
                         lambda h, t: f_in[:, t, 2 * D + (4 * n + h) * DH:2 * D + (4 * n + h + 1) * DH],
                         DH + 2)

            pe.wait_ge(S("rows_in"), 5 * 16)
            tr(bank[7][:, 0:72], rows[:, :], ident[0:72, 0:72]).then_inc(S("colsT"), 1)
            pe.wait_ge(S("ones_set"), 1)
            pe.wait_ge(S("pool_order"), 1)
            mod_reduce(0)
            for L in range(DEPTH):
                if stop < L + 1:
                    return
                pe.wait_ge(S("xn"), L + 1)
                pe.wait_ge(S("mod_ready"), L + 1)
                transpose_in(lambda t, k: xn[:, t, k * P:(k + 1) * P], "xT")
                pe.wait_ge(S("hT"), L + 1)
                project(f"in{L}", 8 if L == 2 else 6)
                if L + 1 < DEPTH:
                    mod_reduce(L + 1)
                    pe.wait_ge(S("mod_ready"), L + 2)
                if L in (0, 3):
                    gla(L, L // 3)
                elif L == 1:
                    sgu()
                else:
                    fox()
                pe.wait_ge(S("gated"), L + 1)
                src = fo if L == 2 else g_in[:, :, 2 * D:3 * D]
                transpose_in(lambda t, k: src[:, t, k * P:(k + 1) * P], "gT")
                pe.wait_ge(S("ghT"), L + 1)
                project(f"out{L}", 2)
            if stop < 5:
                return
            pe.wait_ge(S("xn"), DEPTH + 1)
            transpose_in(lambda t, k: xn[:, t, k * P:(k + 1) * P], "xT")
            pe.wait_ge(S("hT"), DEPTH + 1)
            project("hyb_a", 6)
            project("hyb_b", 12)
            b = BLOCKS["hyb_b"] + 12
            block_products(b, b % 2, lambda k: ring[:, b % 2, k * N:(k + 1) * N])
            pe.wait_ge(S("z_conv"), 1)
            transpose_in(lambda t, k: ha[:, t, D + k * P:D + (k + 1) * P], "zT")
            pe.wait_ge(S("zT_sb"), 1)
            transpose_in(lambda t, k: ha[:, t, k * P:(k + 1) * P], "bT")
            pe.wait_ge(S("conv_hT"), 1)
            for i in range(2):
                b = BLOCKS["conv"] + i
                block_products(b, b % 2, lambda k: ring[:, b % 2, k * N:(k + 1) * N])
            pe.wait_ge(S("rotated"), 1)
            for n in range(6):
                c0 = n * 4 * DH
                quad(4 + n, lambda h, t: hb[:, t, QO + c0 + h * DH:QO + c0 + (h + 1) * DH],
                     lambda h, t: hb[:, t, KO + c0 + h * DH:KO + c0 + (h + 1) * DH],
                     lambda h, t: hb[:, t, VO + c0 + h * DH:VO + c0 + (h + 1) * DH], DH)
            pe.wait_ge(S("att_merged"), 1)
            transpose_in(lambda t, k: od[:, t, 0, k * P:(k + 1) * P], "oT", chunks=4)
            pe.wait_ge(S("oT_sb"), 1)
            b = BLOCKS["attn"]
            pe.wait_ge(S(f"w_landed{b % 2}"), (b // 2 + 1) * 16)
            wv = ring[:, b % 2, :].rearrange("p (k n) -> p k n", n=D)
            for half in (1, 0):
                for t in range(T):
                    if half == 0:
                        pe.wait_ge(S(f"evac{t}"), b + 1)
                    for k in range(4):
                        last = mm(bank[t + 6 * half][:, :], hT[:, k, t * P:(t + 1) * P],
                                  wv[:, k, half * N:(half + 1) * N], start=(k == 0), stop=(k == 3))
                    last.then_inc(S("attn_half") if half else S(f"proj_done{t}"), 1)
            pe.wait_ge(S("merged"), 1)
            transpose_in(lambda t, k: ha[:, t, k * P:(k + 1) * P], "mT")
            pe.wait_ge(S("mT_sb"), 1)
            project("hyb_out", 2)
            if stop < 6:
                return
            pe.wait_ge(S("u_ready"), 1)
            transpose_in(lambda t, k: u[:, t, k * P:(k + 1) * P], "uT")
            pe.wait_ge(S("uT_sb"), 1)
            project("query", 4)
            pe.wait_ge(S("sk_in"), 16)
            for g in range(4):
                for i in range(4):
                    last = tr(bank[2 + g][:, i * P:(i + 1) * P], skr[:, 4 * g + i, :], ident[:, :])
                last.then_inc(S("skT"), 1)
            for t in range(T):
                pe.wait_ge(S(f"evac{t}"), BLOCKS["query"] + 5)
            for r in range(2):
                pe.wait_ge(S("pq_sb"), r + 1)
                transpose_in(lambda t, k: qq[:, t, r * D + k * P:r * D + (k + 1) * P], "pqT")
            pe.wait_ge(S("pq_sb"), 3)
            for t in range(T):
                if t:
                    pe.wait_ge(S("sc_sb"), 1)
                for g in range(4):
                    for i in range(4):
                        hc = 4 * g + i
                        last = mm(bank[2 + g][:, i * P:(i + 1) * P], pqT[:, hc, t * P:(t + 1) * P],
                                  skT[:, hc, :], start=True, stop=True)
                    last.then_inc(S("sc_mm"), 1)
            if stop < 7:
                return
            for t in range(T):
                for i in range(2):
                    mm(bank[2 * t + i][:, :], ident[:, :], x[:, t, i * N:(i + 1) * N], start=True, stop=False,
                       skip_group_check=True)

                def two_heads(i):
                    for half in range(2):
                        h = i * 2 + half + t * PH
                        for e in range(TOPK):
                            s = e % SLOTS
                            pe.wait_ge(S("diag"), h * TOPK + e + 1)
                            pe.wait_ge(S(f"up_landed{s}"), (h * 2 + e // SLOTS + 1) * 16)
                            for c in range(2):
                                last = mm(bank[2 * t + c][:, :], diag[:, e % 4, :], up[:, s, c * N:(c + 1) * N],
                                          start=False, stop=False, skip_group_check=True)
                            last.then_inc(S(f"up_used{s}"), 1)
                with pe.Fori(0, PH // 2) as i:
                    two_heads(i)
                for c in range(2):
                    last = mm(bank[2 * t + c][:, :], zero[:, :], x[:, t, c * N:(c + 1) * N],
                              start=False, stop=True, skip_group_check=True)
                last.then_inc(S("peer_done"), 1)

        @block.scalar
        def _(act):
            link = orderer(act, "act_order")
            af = nc.scalar.activation

            def evac(b, slot, dst):
                for t in range(T):
                    act.wait_ge(S(f"proj_done{t}"), b + 1)
                    af(dst(t), bank[t][:, :], ACT.Copy).then_inc(S(f"evac{t}"), 1)

            def project(name, n, dst):
                b0 = BLOCKS[name]

                def pair(i):
                    for slot in range(2):
                        evac(b0 + 2 * i + slot, slot, lambda t: dst[:, t, ds(i * (2 * N) + slot * N, N)])
                if n > 2:
                    with act.Fori(0, n // 2) as i:
                        pair(i)
                else:
                    pair(0)

            def evac_done(b):
                for t in range(T):
                    act.wait_ge(S(f"evac{t}"), b + 1)

            def root(tag, n, width):
                act.wait_ge(S("ssq"), nth(tag))
                link(af(rstd[:, 0:n], ssq[:, 0:n], ACT.Ln, scale=1.0 / width, bias=EPS))
                af(rstd[:, 0:n], rstd[:, 0:n], ACT.Exp, scale=-0.5).then_inc(S("root"), 1)

            def squares(src, tag, wait=True):
                for t in range(T):
                    last = af(xn[:, t, :], src[:, t, :], ACT.Square, accum_out=ssq[:, t:t + 1])
                last.then_inc(S("ssq"), 1)
                root(tag, T, D)

            def quad(n, kd):
                aqT, akT, aS, aPT = bufs(n)
                act.wait_ge(S("att_T"), 2 * n + 1)
                for i in range(2):
                    last = af(aqT[0:kd, 2 * i:2 * i + 2, :].rearrange("p h n -> p (h n)"),
                              bank[2 + i][0:kd, :], ACT.Copy)
                last.then_inc(S("att_qT"), 1)
                act.wait_ge(S("att_m"), n + 1)
                for h in range(4):
                    for t in range(T):
                        part = aS[:, h, 0:P] if t == 0 else aS[:, h, P:3 * P]
                        last = af(part, part, ACT.Exp, bias=anm[:, n, 2 * h + t:2 * h + t + 1],
                                  accum_out=al[:, n, 2 * h + t:2 * h + t + 1])
                last.then_inc(S("att_p"), 1)
                act.wait_ge(S("att_pt"), 3 * n + 1)
                af(aPT[:, 0, :, :].rearrange("p h n -> p (h n)"), bank[3][:, :], ACT.Copy)
                act.wait_ge(S("att_pt"), 3 * n + 3)
                af(aPT[:, 2, :, :].rearrange("p h n -> p (h n)"), bank[5][:, :], ACT.Copy) \
                    .then_inc(S("att_pta"), 1)

            act.wait_ge(S("colsT_sb"), 1)
            af(cond[:, :], cols[:, 64:72], ACT.Silu).then_inc(S("cond"), 1)
            act.wait_ge(S("x_in"), 16)
            for L in range(DEPTH):
                if stop < L + 1:
                    return
                if L:
                    act.wait_ge(S("x_ready"), L)
                squares(x, f"norm{L}")
                project(f"in{L}", 8 if L == 2 else 6, f_in if L == 2 else g_in)
                evac_done(BLOCKS[f"out{L}"])
                if L in (0, 3):
                    act.wait_ge(S("decay"), L // 3 + 1)
                    ya = Dd[0]
                    for i in range(2):
                        link(af(ya[:, i * N:(i + 1) * N], bank[6 + i][:, :], ACT.Abs))
                    link(af(ya, ya, ACT.Exp, scale=-1.0))
                    af(ya, ya, ACT.Ln, bias=1.0).then_inc(S("lnd"), 1)
                    act.wait_ge(S("qkT"), L // 3 + 1)
                    for i in range(2):
                        af(qT[:, 2 * i:2 * i + 2, :].rearrange("p h n -> p (h n)"), bank[2 + i][:, :],
                           ACT.Copy, scale=DK ** -0.5)
                        last = af(kT[:, 2 * i:2 * i + 2, :].rearrange("p h n -> p (h n)"),
                                  bank[4 + i][:, :], ACT.Copy)
                    last.then_inc(S("qkT_sb"), 1)
                    for lv in range(1, LEVELS + 2):
                        act.wait_ge(S("lvl_d"), L // 3 * (LEVELS + 1) + lv)
                        af(Dd[lv % 2], Dd[lv % 2], ACT.Exp).then_inc(S("lvl_e"), 1)
                    af(g_in[:, :, 2 * D:3 * D], g_in[:, :, 2 * D:3 * D], ACT.Silu).then_inc(S("silu"), 1)
                    act.wait_ge(S("gla_o"), L // 3 + 1)
                    for t in range(T):
                        for h in range(GH):
                            last = af(at(W0 + 7 * D + (t * GH + h) * DV, DV), bank[2 + 2 * t + h // 2][:, (h % 2) * DV:(h % 2 + 1) * DV],
                                      ACT.Square, accum_out=ssq[:, t * GH + h:t * GH + h + 1])
                    last.then_inc(S("ssq"), 1)
                    root(f"head{L}", T * GH, DV)
                elif L == 1:
                    for t in range(T):
                        link(af(g_in[:, t, D:2 * D], g_in[:, t, D:2 * D], ACT.Gelu_apprx_tanh,
                                accum_out=small[:, t:t + 1]), wait=(t == T - 1))
                    act.wait_ge(S("act_order"), ORDER["act_order"])
                    link(af(small[:, 2:4], small[:, 0:2], ACT.Copy, scale=-1.0 / D))
                    for t in range(T):
                        link(af(g_in[:, t, D:2 * D], g_in[:, t, D:2 * D], ACT.Identity, bias=small[:, 2 + t:3 + t]))
                        last = af(at(W0 + (2 + t) * D, D), g_in[:, t, D:2 * D], ACT.Square, accum_out=ssq[:, t:t + 1])
                    last.then_inc(S("ssq"), 1)
                    root("ln", T, D)
                    af(g_in[:, :, 0:D], g_in[:, :, 0:D], ACT.Gelu_apprx_tanh)
                    af(g_in[:, :, 2 * D:3 * D], g_in[:, :, 2 * D:3 * D], ACT.Silu).then_inc(S("silu"), 1)
                else:
                    for i in range(2):
                        last = af(sqs[:, i, :].rearrange("p (t d) -> p t d", t=T), f_in[:, :, i * D:(i + 1) * D],
                                  ACT.Square)
                    last.then_inc(S("sq_qk"), 1)
                    act.wait_ge(S("f_sb"), 1)
                    link(af(low2[:, :, :], low[:, :, :], ACT.Abs))
                    link(af(low2[:, :, :], low2[:, :, :], ACT.Exp, scale=-1.0))
                    af(low2[:, :, :], low2[:, :, :], ACT.Ln, bias=1.0).then_inc(S("lnf"), 1)
                    af(f_in[:, :, 3 * D:4 * D], f_in[:, :, 3 * D:4 * D], ACT.Silu).then_inc(S("silu"), 1)
                    root("qk", 4 * AH, DH)
                    for n in range(4):
                        quad(n, DH + 2)
                project(f"out{L}", 2, ob)
                evac_done(BLOCKS[f"out{L}"] + 2)
                squares(ob, f"post{L}")
            if stop < 5:
                return
            act.wait_ge(S("angles"), 1)
            af(trig[:, :, :], trig[:, :, :], ACT.Sin).then_inc(S("trig"), 1)
            act.wait_ge(S("x_ready"), 4)
            squares(x, "mix")
            project("hyb_a", 6, ha)
            project("hyb_b", 12, hb)
            b = BLOCKS["hyb_b"] + 12
            evac(b, b % 2, lambda t: hb[:, t, 12 * N:13 * N])
            act.wait_ge(S("gates_in"), 1)
            af(hb[:, :, GC:GC + 2 * D], hb[:, :, GC:GC + 2 * D], ACT.Sigmoid).then_inc(S("gates"), 1)
            act.wait_ge(S("conv_hT"), 1)
            for i in range(2):
                b = BLOCKS["conv"] + i
                evac(b, b % 2, lambda t: ha[:, t, i * N:(i + 1) * N])
            for n in range(6):
                quad(4 + n, DH)
            act.wait_ge(S("lse_in"), 1)
            af(lse[:, 0, :], al[:, 4:10, :].rearrange("p n h -> p (n h)"), ACT.Ln).then_inc(S("lse_ln"), 1)
            act.wait_ge(S("lse_m"), 1)
            af(lse[:, 0, :], lse[:, 1, :], ACT.Exp).then_inc(S("lse_e"), 1)
            act.wait_ge(S("attn_half"), 2)
            for t in range(T):
                af(ha[:, t, D + N:2 * D], bank[6 + t][:, :], ACT.Copy)
            b = BLOCKS["attn"]
            evac(b, b % 2, lambda t: ha[:, t, D:D + N])
            project("hyb_out", 2, ha[:, :, 2 * D:3 * D])
            if stop < 6:
                return
            act.wait_ge(S("x_ready"), 5)
            squares(x, "ffn")
            project("query", 4, qq)
            for t in range(T):
                for g in range(4):
                    act.wait_ge(S("sc_mm"), 4 * t + g + 1)
                    last = af(sc[:, t, g * N:(g + 1) * N], bank[2 + g][:, :], ACT.Copy)
                last.then_inc(S("sc_sb"), 1)
            if stop < 7:
                return
            for t in range(T):
                def two_heads(i):
                    for half in range(2):
                        h = i * 2 + half + t * PH
                        act.wait_ge(S("choice"), h * LINKS + BEST)
                        af(pex[:, half, :], pbest[:, half, :], ACT.Exp, bias=pneg[:, half, :],
                           accum_out=psm[:, half, :]).then_inc(S("pexp"), 1)
                        act.wait_ge(S(f"dn_used{SLOTS - 1}"), h * 2 + 3)
                        af(pa[:, half, :], pa[:, half, :], ACT.Gelu).then_inc(S("gelu"), 1)
                        act.wait_ge(S("coef"), h + 1)
                        for e in range(TOPK):
                            act.wait_ge(S(f"up_used{(e - 4) % SLOTS}"),
                                        h * 2 + (e - 4) // SLOTS + 2)
                            af(diag[:, e % 4, :], ident[:, :], ACT.Copy, scale=pcoef[:, half, e:e + 1]) \
                                .then_inc(S("diag"), 1)
                with act.Fori(0, PH // 2) as i:
                    two_heads(i)
            for t in range(T):
                act.wait_ge(S("peer_done"), t + 1)
                for c in range(2):
                    last = af(at(t * D + c * N, N), bank[2 * t + c][:, :], ACT.Square,
                              accum_out=sqf[:, 2 * t + c:2 * t + c + 1])
                last.then_inc(S("sq_final"), 1)
            root("final", T, D)

        @block.vector
        def _(dve):
            v = nc.vector
            link = orderer(dve, "dve_order")

            def copy_banks(dst, tag, done, n=4, base=0):
                for i in range(n):
                    dve.wait_ge(S(tag), base + i + 1)
                    last = v.tensor_copy(dst[:, 2 * i:2 * i + 2, :].rearrange("p k n -> p (k n)"), bank[2 + i][:, :])
                last.then_inc(S(done), 1)

            def mod_sums(L):
                dve.wait_ge(S("acc_init"), (L + 1) * 16)
                if L == 0:
                    dve.wait_ge(S("cond"), 1)
                with dve.Fori(0, 6) as i:
                    for s in range(2):
                        dve.wait_ge(S(f"mod_landed{s}"), (L * 6 + i + 1) * 16)
                        for k in range(KC):
                            a = acc[:, ds(i * N + s * (N // 2), N // 2)]
                            v.scalar_tensor_tensor(out=a, in0=mring[:, s, k, :], scalar=cond[:, k:k + 1], in1=a,
                                                   op0=ALU.mult, op1=ALU.add).then_inc(S("mod_sum"), 1)
                            dve.wait_ge(S("mod_sum"), (L * 6 + i) * 16 + s * 8 + k + 1)

            def mod_finish(L):
                dve.wait_ge(S("mod_read"), L + 1)
                dve.wait_ge(S("gpost_in"), 16 * (L + 1))
                v.tensor_copy(modc[:, L % 2, 0, :], bank[7][:, 0:KC])
                v.scalar_tensor_tensor(out=modc[:, L % 2, 1, :], in0=bank[7][:, KC:2 * KC], scalar=1.0,
                                       in1=cols[:, L * KC:(L + 1) * KC], op0=ALU.add, op1=ALU.mult)
                for i in range(2):
                    last = v.tensor_tensor(gateb[:, L % 2, i * N:(i + 1) * N], bank[5 + i][:, :],
                                           gpost[:, i * N:(i + 1) * N], ALU.mult)
                last.then_inc(S("mod_ready"), 1)

            def root(tag, n, width, scale=None):
                dve.wait_ge(S("ssq"), nth(tag))
                var, y, w = ssq[:, 0:n], rstd[:, 0:n], newton[:, 0:n]
                dve.wait_ge(S("root"), nth(tag))
                v.tensor_scalar(var, var, 1.0 / width, EPS, ALU.mult, ALU.add)
                link(v.tensor_tensor(w, y, y, ALU.mult))
                link(v.tensor_tensor(w, w, var, ALU.mult))
                link(v.tensor_scalar(w, w, -0.5, 1.5, ALU.mult, ALU.add))
                link(v.tensor_tensor(y, y, w, ALU.mult))
                if scale is not None:
                    link(v.tensor_scalar(rstd[:, 0:scale[0]], rstd[:, 0:scale[0]], scale[1], None, ALU.mult))

            def normalize(tag, done):
                root(tag, T, D)
                for t in range(T):
                    last = v.tensor_scalar(xn[:, t, :], x[:, t, :], rstd[:, t:t + 1], None, ALU.mult)
                last.then_inc(S(done), 1)

            def quad(n, mask, o):
                aqT, akT, aS, aPT = bufs(n)
                kd = DH + 2 if n < 4 else DH
                dve.wait_ge(S("att_T"), 2 * n + 2)
                for i in range(2):
                    last = v.tensor_copy(akT[0:kd, 2 * i:2 * i + 2, :].rearrange("p h n -> p (h n)"), bank[4 + i][0:kd, :])
                last.then_inc(S("att_kT"), 1)
                dve.wait_ge(S("att_s"), n + 1)
                v.tensor_tensor(aS[:, :, 0:P], bank[6][:, :].rearrange("p (h n) -> p h n", h=4),
                                amask[:, mask, 0:P].unsqueeze(1).to_broadcast([P, 4, P]), ALU.add)
                for i in range(2):
                    last = v.tensor_tensor(aS[:, 2 * i:2 * i + 2, P:3 * P],
                                           bank[(7, 2)[i]][:, :].rearrange("p (h n) -> p h n", h=2),
                                           amask[:, mask, P:3 * P].unsqueeze(1).to_broadcast([P, 2, 2 * P]), ALU.add)
                link(last)
                nm = anm[:, n, :].rearrange("p (h t) -> p h t", t=T)
                v.tensor_reduce(nm[:, :, 0:1], aS[:, :, 0:P], X, ALU.max)
                link(v.tensor_reduce(nm[:, :, 1:2], aS[:, :, P:3 * P], X, ALU.max))
                v.tensor_scalar(anm[:, n, :], anm[:, n, :], -1.0, None, ALU.mult).then_inc(S("att_m"), 1)
                dve.wait_ge(S("att_pt"), 3 * n + 2)
                v.tensor_copy(aPT[:, 1, :, :].rearrange("p h n -> p (h n)"), bank[4][:, :]).then_inc(S("att_ptv"), 1)
                dve.wait_ge(S("att_pv"), n + 1)
                link(v.reciprocal(arl[:, :], al[:, n, :]))
                pv_ = bank[6][:, :].rearrange("p (t h d) -> p t h d", t=T, h=4)
                rl = arl[:, :].rearrange("p (h t) -> p t h", t=T)
                for t in range(T):
                    last = v.tensor_tensor(o[:, t, :].rearrange("p (h d) -> p h d", h=4), pv_[:, t, :, :],
                                           rl[:, t, :].unsqueeze(2).to_broadcast([P, 4, DH]), ALU.mult)
                last.then_inc(S("att_o"), 1)

            def gla(L):
                dve.wait_ge(S("low"), 3 if L else 1)
                v.tensor_copy(low[:, :, :].rearrange("p t n -> p (t n)"), bank[6][:, 0:T * RANK]) \
                    .then_inc(S("low_sb"), 1)
                dve.wait_ge(S("ones_set"), 1)
                dve.wait_ge(S("lowT"), L // 3 + 1)
                v.tensor_copy(alT[0:RANK, :], bank[7][0:RANK, 0:T * P]).then_inc(S("alT"), 1)
                for b in (Q[0], Q[1], K[0], K[1], AT[:, 0, :], AT[:, 1, :]):
                    link(v.memset(b, 0.0), wait=False)
                bfl = b_.rearrange("p h n -> p (h n)")
                dve.wait_ge(S("lnd"), L // 3 + 1)
                for i in range(2):
                    link(v.scalar_tensor_tensor(out=bfl[:, i * N:(i + 1) * N], in0=bank[6 + i][:, :], scalar=0.0,
                                                in1=Dd[0][:, i * N:(i + 1) * N], op0=ALU.min, op1=ALU.subtract))
                link(v.tensor_scalar(bfl, bfl, 1.0 / 16.0, None, ALU.mult))
                for h in range(GH):
                    last = v.tensor_tensor_scan(b_[:, h, :], ones[:, 0:1].to_broadcast([P, T * P]), b_[:, h, :], 0.0,
                                                ALU.mult, ALU.add)
                last.then_inc(S("logd"), 1)
                dve.wait_ge(S("logd"), L // 3 + 1)
                dve.wait_ge(S("qkT_sb"), L // 3 + 1)

                def halves(a, lv):
                    return a.rearrange("p (n two l) -> p n two l", two=2, l=1 << (lv - 1))

                def exponents(lv):
                    if lv >= 3:
                        dve.wait_ge(S("lvl_qk"), L // 3 * (LEVELS + 1) + lv - 2)
                    size = 1 << (lv - 1)
                    n = GH * T * P // (2 * size)
                    bv, dv = halves(bfl, lv), halves(Dd[lv % 2], lv)
                    ref = bv[:, :, 0, size - 1:size].to_broadcast([P, n, size])
                    v.tensor_tensor(dv[:, :, 1, :], bv[:, :, 1, :], ref, ALU.subtract)
                    v.tensor_tensor(dv[:, :, 0, :], ref, bv[:, :, 0, :], ALU.subtract).then_inc(S("lvl_d"), 1)

                def decayed(lv):
                    dve.wait_ge(S("lvl_e"), L // 3 * (LEVELS + 1) + lv)
                    if lv >= 2:
                        dve.wait_ge(S("lvl"), L // 3 * (LEVELS + 2) + lv - 1)
                    e = halves(Dd[lv % 2], lv)
                    v.tensor_tensor(halves(Q[lv % 2], lv)[:, :, 1, :],
                                    halves(qT.rearrange("p h n -> p (h n)"), lv)[:, :, 1, :], e[:, :, 1, :], ALU.mult)
                    v.tensor_tensor(halves(K[lv % 2], lv)[:, :, 0, :],
                                    halves(kT.rearrange("p h n -> p (h n)"), lv)[:, :, 0, :], e[:, :, 0, :], ALU.mult) \
                        .then_inc(S("lvl_qk"), 1)

                def take(lv):
                    dve.wait_ge(S("lvl"), L // 3 * (LEVELS + 2) + lv + 1)
                    if lv:
                        dve.wait_ge(S("lvl_read"), L // 3 * (LEVELS + 1) + lv)
                    b0 = (6, 2)[lv % 2]
                    if lv <= LEVELS:
                        for t in range(T):
                            last = v.copy_predicated(AT[:, t, :].rearrange("p (h n) -> p h n", h=GH),
                                                     gmask[:, lv, :].unsqueeze(1).to_broadcast([P, GH, P]),
                                                     bank[b0 + t][:, :].rearrange("p (h n) -> p h n", h=GH))
                        last.then_inc(S("lvl_read"), 1)
                    else:
                        v.tensor_copy(AX.rearrange("p h n -> p (h n)"), bank[b0][:, :]).then_inc(S("attn_sb"), 1)

                dve.wait_ge(S("consts_in"), CONSTS * 16)
                exponents(1)
                for lv in range(1, LEVELS + 2):
                    if lv <= LEVELS:
                        exponents(lv + 1)
                    decayed(lv)
                    take(lv - 1)
                take(LEVELS + 1)
                root(f"head{L}", T * GH, DV)
                dve.wait_ge(S("ghead_in"), 16 if L == 0 else 32)
                og = at(W0 + 3 * D, T, D)
                for t in range(T):
                    for h in range(GH):
                        last = v.scalar_tensor_tensor(
                            out=og[:, t, h * DV:(h + 1) * DV], in0=bank[2 + 2 * t + h // 2][:, (h % 2) * DV:(h % 2 + 1) * DV],
                            scalar=rstd[:, t * GH + h:t * GH + h + 1], in1=ghead[:, h * DV:(h + 1) * DV],
                            op0=ALU.mult, op1=ALU.mult)
                link(last)
                dve.wait_ge(S("silu"), L + 1)
                z = g_in[:, :, 2 * D:3 * D]
                v.tensor_tensor(z, z, og, ALU.mult).then_inc(S("gated"), 1)
                if L == 0:
                    pass

            def sgu():
                dve.wait_ge(S("wsT"), 1)
                link(v.tensor_tensor(wsT, bank[2][:, :].rearrange("p (g n) -> p g n", g=SG),
                                     summ[:, :].unsqueeze(1).to_broadcast([P, SG, P]), ALU.mult), wait=False)
                root("ln", T, D)
                for t in range(T):
                    vt = g_in[:, t, D:2 * D]
                    link(v.scalar_tensor_tensor(out=vt, in0=vt, scalar=rstd[:, t:t + 1], in1=lng[:, :],
                                                op0=ALU.mult, op1=ALU.mult))
                    last = v.tensor_tensor(vt, vt, lnb[:, :], ALU.add)
                last.then_inc(S("ln_done"), 1)
                dve.wait_ge(S("mixed"), 1)
                dve.wait_ge(S("silu"), 2)
                su = at(W0 + 2 * D, T, D)
                for t in range(T):
                    for g in range(SG):
                        last = v.scalar_tensor_tensor(
                            out=su[:, t, g * 256:(g + 1) * 256], in0=bank[2 + 2 * t + g // 2][:, (g % 2) * 256:(g % 2 + 1) * 256],
                            scalar=bs[:, g:g + 1], in1=g_in[:, t, g * 256:(g + 1) * 256], op0=ALU.add, op1=ALU.mult)
                link(last)
                z = g_in[:, :, 2 * D:3 * D]
                v.tensor_tensor(z, z, su, ALU.mult).then_inc(S("gated"), 1)

            def fox():
                dve.wait_ge(S("sq_qk"), 1)
                v.tensor_reduce(ssq[:, 0:64], sqs.rearrange("p i (h d) -> p (i h) d", d=DH), X, ALU.add) \
                    .then_inc(S("ssq"), 1)
                dve.wait_ge(S("low"), 2)
                v.tensor_tensor(low[:, :, :], bank[6][:, 0:T * AH].rearrange("p (t n) -> p t n", t=T),
                                bf[:, :].unsqueeze(1).to_broadcast([P, T, AH]), ALU.add).then_inc(S("f_sb"), 1)
                dve.wait_ge(S("lnf"), 1)
                v.scalar_tensor_tensor(out=low2[:, :, :], in0=low[:, :, :], scalar=0.0, in1=low2[:, :, :],
                                       op0=ALU.min, op1=ALU.subtract).then_inc(S("logf"), 1)
                v.memset(qa[:, :, :, DH:DH + 1], 1.0)
                v.memset(ka[:, :, :, DH + 1:DH + 2], 1.0)
                dve.wait_ge(S("fsum"), 1)
                F = bank[7][:, 0:T * AH].rearrange("p (t h) -> p t h", t=T).unsqueeze(3)
                v.tensor_copy(qa[:, :, :, DH + 1:DH + 2], F)
                v.tensor_scalar(ka[:, :, :, DH:DH + 1], F, -1.0, None, ALU.mult)
                root("qk", 4 * AH, DH, scale=(2 * AH, DH ** -0.5))
                for i, dst in ((0, qa), (1, ka)):
                    for t in range(T):
                        src = f_in[:, t, i * D:(i + 1) * D].rearrange("p (h d) -> p h d", d=DH)
                        r = rstd[:, (i * T + t) * AH:(i * T + t + 1) * AH].unsqueeze(2).to_broadcast([P, AH, DH])
                        link(v.tensor_tensor(src, src, r, ALU.mult))
                        last = v.tensor_tensor(dst[:, t, :, 0:DH], src, gqk[:, i, :].unsqueeze(1).to_broadcast([P, AH, DH]),
                                               ALU.mult)
                last.then_inc(S("qka"), 1)
                for n in range(4):
                    quad(n, 0, fo[:, :, n * 256:(n + 1) * 256])
                dve.wait_ge(S("att_o"), 4)
                dve.wait_ge(S("silu"), 3)
                v.tensor_tensor(fo, fo, f_in[:, :, 3 * D:4 * D], ALU.mult).then_inc(S("gated"), 1)

            for t in range(T):
                v.memset(bank[t][:, 0:1], 0.0).then_inc(S(f"evac{t}"), 1)
            dve.wait_ge(S("colsT"), 1)
            v.tensor_copy(cols[:, :], bank[7][:, 0:72]).then_inc(S("colsT_sb"), 1)
            dve.wait_ge(S("colsT_sb"), 1)
            mod_sums(0)
            mod_finish(0)
            for L in range(DEPTH):
                if stop < L + 1:
                    return
                normalize(f"norm{L}", "xn")
                dve.wait_ge(S("mod_ready"), L + 1)
                for k in range(KC):
                    dve.wait_ge(S("xT"), 4 * L + k // 2 + 1)
                    last = v.tensor_scalar(hT[:, k, :], bank[2 + k // 2][:, (k % 2) * 256:(k % 2 + 1) * 256],
                                           modc[:, L % 2, 1, k:k + 1], modc[:, L % 2, 0, k:k + 1], ALU.mult, ALU.add)
                last.then_inc(S("hT"), 1)
                if L + 1 < DEPTH:
                    mod_sums(L + 1)
                    mod_finish(L + 1)
                if L in (0, 3):
                    gla(L)
                elif L == 1:
                    sgu()
                else:
                    fox()
                copy_banks(hT, "gT", "ghT", base=4 * L)
                root(f"post{L}", T, D)
                for t in range(T):
                    link(v.scalar_tensor_tensor(out=ob[:, t, :], in0=ob[:, t, :], scalar=rstd[:, t:t + 1],
                                                in1=gateb[:, L % 2, :], op0=ALU.mult, op1=ALU.mult))
                v.tensor_tensor(x[:, :, :], x[:, :, :], ob, ALU.add).then_inc(S("x_ready"), 1)
                dve.wait_ge(S("x_ready"), L + 1)
            if stop < 5:
                return
            link(v.tensor_copy(posf[:, :], posi[:, :]))
            ang = acc[:, 0:16].rearrange("p (t r) -> p t r", t=T)
            for t in range(T):
                link(v.tensor_scalar(ang[:, t, :], freq[:, :], posf[:, t:t + 1], None, ALU.mult))
            for i, (turn, shift) in enumerate(((0.25, np.pi / 2), (0.0, 0.0))):
                a, r, n = acc[:, 0:16], trig[:, i, :], acc[:, 32:48]
                link(v.tensor_scalar(n, a, float(1 / (2 * np.pi)), turn, ALU.mult, ALU.add))
                link(v.tensor_scalar(n, n, MAGIC, None, ALU.add))
                link(v.tensor_scalar(n, n, MAGIC, None, ALU.subtract))
                link(v.scalar_tensor_tensor(out=r, in0=n, scalar=-TWO_PI[0], in1=a, op0=ALU.mult, op1=ALU.add))
                for c in TWO_PI[1:]:
                    link(v.scalar_tensor_tensor(out=r, in0=n, scalar=-c, in1=r, op0=ALU.mult, op1=ALU.add))
                link(v.tensor_scalar(r, r, float(shift), None, ALU.add))
                link(v.tensor_scalar(r, r, PI_SAFE, -PI_SAFE, ALU.min, ALU.max), wait=False)
            dve.wait_ge(S("dve_order"), ORDER["dve_order"])
            link(v.memset(zT[:, :, 0:2], 0.0), wait=False)
            v.memset(acc[:, 64:65], 0.0).then_inc(S("angles"), 1)
            normalize("mix", "xn")
            for k in range(KC):
                dve.wait_ge(S("xT"), 4 * DEPTH + k // 2 + 1)
                last = v.tensor_scalar(hT[:, k, :], bank[2 + k // 2][:, (k % 2) * 256:(k % 2 + 1) * 256],
                                       cols[:, 32 + k:33 + k], None, ALU.mult)
            last.then_inc(S("hT"), 1)
            for t in range(T):
                dve.wait_ge(S(f"evac{t}"), BLOCKS["hyb_b"] + 1)
            v.tensor_tensor(ha[:, :, D:2 * D], ha[:, :, D:2 * D], ha[:, :, 2 * D:3 * D], ALU.mult) \
                .then_inc(S("z_conv"), 1)
            for t in range(T):
                dve.wait_ge(S(f"evac{t}"), BLOCKS["conv"] + 1)
            for t in range(T):
                last = v.tensor_tensor(hb[:, t, GC:GC + 2 * D], hb[:, t, GC:GC + 2 * D],
                                       gbias[:, :, :].rearrange("p a d -> p (a d)"), ALU.add)
            last.then_inc(S("gates_in"), 1)
            dve.wait_ge(S("trig"), 1)
            HB = 2 * NG * GHD
            for t in range(T):
                qk = hb[:, t, 0:HB * DH].rearrange("p (h d) -> p h d", d=DH)
                t1, t2 = qk[:, :, 0:ROT], qk[:, :, ROT:2 * ROT]
                cs = trig[:, 0, t * ROT:(t + 1) * ROT].unsqueeze(1).to_broadcast([P, HB, ROT])
                sn = trig[:, 1, t * ROT:(t + 1) * ROT].unsqueeze(1).to_broadcast([P, HB, ROT])
                tmp = [acc[:, t * 1536 + i * 384:t * 1536 + (i + 1) * 384].rearrange("p (h r) -> p h r", r=ROT) for i in range(4)]
                for o, a, b in ((tmp[0], t1, cs), (tmp[1], t2, sn), (tmp[2], t2, cs), (tmp[3], t1, sn)):
                    last = v.tensor_tensor(o, a, b, ALU.mult)
                link(last)
                v.tensor_tensor(t1, tmp[0], tmp[1], ALU.subtract)
                last = v.tensor_tensor(t2, tmp[2], tmp[3], ALU.add)
            link(last)
            v.tensor_scalar(hb[:, :, 0:1536], hb[:, :, 0:1536], DH ** -0.5, None, ALU.mult).then_inc(S("rotated"), 1)
            for i in range(4):
                dve.wait_ge(S("zT"), i + 1)
                last = v.tensor_copy(zT[:, 2 * i:2 * i + 2, 2:258], bank[2 + i][:, :].rearrange("p (k n) -> p k n", k=2))
            last.then_inc(S("zT_sb"), 1)
            dve.wait_ge(S("zT_sb"), 1)
            for i in range(3):
                for k in range(KC):
                    w = cols[:, 40 + i * KC + k:41 + i * KC + k]
                    if i == 0:
                        last = v.tensor_scalar(hT[:, k, :], zT[:, k, 0:256], w, None, ALU.mult)
                    else:
                        last = v.scalar_tensor_tensor(out=hT[:, k, :], in0=zT[:, k, i:i + 256], scalar=w,
                                                      in1=hT[:, k, :], op0=ALU.mult, op1=ALU.add)
                link(last)
            for i in range(4):
                dve.wait_ge(S("bT"), i + 1)
                h2 = hT[:, 2 * i:2 * i + 2, :].rearrange("p k n -> p (k n)")
                last = v.tensor_tensor(h2, h2, bank[2 + i][:, :], ALU.mult)
            last.then_inc(S("conv_hT"), 1)
            for n in range(6):
                quad(4 + n, 1 + n // 2, od[:, :, n // 2, (n % 2) * 256:(n % 2 + 1) * 256])
            dve.wait_ge(S("att_o"), 10)
            v.memset(lsm[:, :], 0.0).then_inc(S("lse_in"), 1)
            dve.wait_ge(S("lse_ln"), 1)
            l0, l1 = lse[:, 0, :], lse[:, 1, :]
            link(v.tensor_tensor(l1, l0, anm[:, 4:10, :].rearrange("p n h -> p (n h)"), ALU.subtract))
            link(v.tensor_tensor(lsm[:, :], l1[:, 0:16], l1[:, 16:32], ALU.max))
            link(v.tensor_tensor(lsm[:, :], lsm[:, :], l1[:, 32:48], ALU.max))
            l3 = l1.rearrange("p (g h) -> p g h", g=NG)
            v.tensor_tensor(l3, l3, lsm[:, :].unsqueeze(1).to_broadcast([P, NG, 16]), ALU.subtract) \
                .then_inc(S("lse_m"), 1)
            dve.wait_ge(S("lse_e"), 1)
            link(v.tensor_tensor(lsm[:, :], l0[:, 0:16], l0[:, 16:32], ALU.add))
            link(v.tensor_tensor(lsm[:, :], lsm[:, :], l0[:, 32:48], ALU.add))
            link(v.reciprocal(lsm[:, :], lsm[:, :]))
            link(v.tensor_tensor(l3, l0.rearrange("p (g h) -> p g h", g=NG),
                                 lsm[:, :].unsqueeze(1).to_broadcast([P, NG, 16]), ALU.mult))
            for t in range(T):
                w = l1.rearrange("p (h t) -> p t h", t=T)[:, t, :].unsqueeze(2).to_broadcast([P, NG * GHD, DH])
                o = od[:, t, :, :].rearrange("p g (h d) -> p (g h) d", d=DH)
                last = v.tensor_tensor(o, o, w, ALU.mult)
            link(last)
            link(v.tensor_tensor(od[:, :, 0, :], od[:, :, 0, :], od[:, :, 1, :], ALU.add))
            v.tensor_tensor(od[:, :, 0, :], od[:, :, 0, :], od[:, :, 2, :], ALU.add).then_inc(S("att_merged"), 1)
            copy_banks(hT, "oT", "oT_sb", n=2)
            for t in range(T):
                dve.wait_ge(S(f"evac{t}"), BLOCKS["attn"] + 2)
            dve.wait_ge(S("gates"), 1)
            v.tensor_tensor(ha[:, :, 0:D], ha[:, :, 0:D], hb[:, :, GC:GC + D], ALU.mult)
            link(v.tensor_tensor(ha[:, :, D:2 * D], ha[:, :, D:2 * D], hb[:, :, GA:GA + D], ALU.mult))
            v.tensor_tensor(ha[:, :, 0:D], ha[:, :, 0:D], ha[:, :, D:2 * D], ALU.add).then_inc(S("merged"), 1)
            copy_banks(hT, "mT", "mT_sb")
            for t in range(T):
                dve.wait_ge(S(f"evac{t}"), BLOCKS["hyb_out"] + 3)
            v.tensor_tensor(x[:, :, :], x[:, :, :], ha[:, :, 2 * D:3 * D], ALU.add).then_inc(S("x_ready"), 1)
            if stop < 6:
                return
            root("ffn", T, D)
            dve.wait_ge(S("last_rows_in"), 32)
            for t in range(T):
                last = v.scalar_tensor_tensor(out=u[:, t, :], in0=x[:, t, :], scalar=rstd[:, t:t + 1], in1=nffn[:, :],
                                              op0=ALU.mult, op1=ALU.mult)
            last.then_inc(S("u_ready"), 1)
            copy_banks(hT, "uT", "uT_sb")
            for g in range(4):
                dve.wait_ge(S("skT"), g + 1)
                last = v.tensor_copy(skT[:, 4 * g:4 * g + 4, :].rearrange("p i n -> p (i n)"), bank[2 + g][:, :])
            last.then_inc(S("pq_sb"), 1)
            for r in range(2):
                for i in range(4):
                    dve.wait_ge(S("pqT"), 4 * r + i + 1)
                    last = v.tensor_copy(pqT[:, 8 * r + 2 * i:8 * r + 2 * i + 2, :].rearrange("p i n -> p (i n)"),
                                         bank[2 + i][:, :])
                last.then_inc(S("pq_sb"), 1)
            if stop < 7:
                return
            link(v.memset(zero, 0.0), wait=False)

            def best16(vals, pos, src, src2, put):
                dve.nop(nofuse=True)
                for w in range(len(src)):
                    last = v.max(vals[w][:, 0:8], src[w])
                put(last)
                dve.nop(nofuse=True)
                for w in range(len(src)):
                    v.max_index(pos[w][:, 0:8], vals[w][:, 0:8], src[w])
                    last = v.match_replace(src2[w], vals[w][:, 0:8], src[w], -3.0e38)
                put(last)
                dve.nop(nofuse=True)
                for w in range(len(src)):
                    last = v.max(vals[w][:, 8:16], src2[w])
                put(last)
                dve.nop(nofuse=True)
                for w in range(len(src)):
                    last = v.max_index(pos[w][:, 8:16], vals[w][:, 8:16], src2[w])
                put(last)

            def choose(h, par):
                n = [0]

                def put(ins):
                    n[0] += 1
                    ins.then_inc(S("choice"), 1)
                    dve.wait_ge(S("choice"), h * LINKS + n[0])

                put(v.tensor_copy(pk, sc.rearrange("p t n -> p (t n)")[:, ds(h * 256, 256)]))
                best16([pv[:, c, :] for c in range(2)], [pix[:, c, :] for c in range(2)],
                       [pk[:, c * P:(c + 1) * P] for c in range(2)], [pk2[:, c * P:(c + 1) * P] for c in range(2)], put)
                v.tensor_copy(pixf[:, :, :], pix[:, :, :])
                put(v.tensor_tensor(cand, pv[:, 0, :].unsqueeze(2).to_broadcast([P, TOPK, TOPK]),
                                    pv[:, 1, :].unsqueeze(1).to_broadcast([P, TOPK, TOPK]), ALU.add))
                best16([pbest[:, par, :]], [ppos[:, :]], [cand.rearrange("p a b -> p (a b)")], [cand2], put)
                put(v.tensor_scalar(pneg[:, par, :], pbest[:, par, 0:1], -1.0, None, ALU.mult))
                assert n[0] == BEST
                v.tensor_single_scalar(pab[:, 0, :], ppos[:, :], 4, ALU.logical_shift_right)
                put(v.tensor_single_scalar(pab[:, 1, :], ppos[:, :], 15, ALU.bitwise_and))
                put(v.tensor_copy(pabf[:, :, :], pab[:, :, :]))
                for c in range(2):
                    put(v.tensor_tensor(hot[:, c, :, :], iota[:, :].unsqueeze(1).to_broadcast([P, TOPK, TOPK]),
                                        pabf[:, c, :].unsqueeze(2).to_broadcast([P, TOPK, TOPK]), ALU.is_equal))
                for c in range(2):
                    put(v.tensor_tensor(hot[:, c, :, :], hot[:, c, :, :],
                                        pixf[:, c, :].unsqueeze(1).to_broadcast([P, TOPK, TOPK]), ALU.mult))
                for c in range(2):
                    put(v.tensor_reduce(psel[:, c, :], hot[:, c, :, :], X, ALU.add))
                put(v.scalar_tensor_tensor(out=pidf[:, :], in0=psel[:, 0, :], scalar=float(NK), in1=psel[:, 1, :],
                                           op0=ALU.mult, op1=ALU.add))
                assert n[0] == LINKS, n[0]

            def publish(h, par):
                v.tensor_copy(idx[:, par, :], pidf[:, :]).then_inc(S("idx_ready"), 1)

            dve.wait_ge(S("sc_sb"), 2)
            for s in range(SLOTS):
                v.memset(dn[:, s, 0:1], 0.0).then_inc(S(f"dn_used{s}"), 1)
                v.memset(up[:, s, 0:1], 0.0).then_inc(S(f"up_used{s}"), 1)
            choose(0, 0)
            publish(0, 0)
            for t in range(T):
                def two_heads(i, final=False):
                    for half in range(2):
                        h = i * 2 + half + t * PH
                        nxt = not (final and half)
                        if nxt:
                            choose(h + 1, 1 - half)
                        for e in range(TOPK):
                            s = e % SLOTS
                            dve.wait_ge(S(f"dn_landed{s}"), (h * 2 + e // SLOTS + 1) * 16)
                            v.tensor_tensor_reduce(out=dn[:, s, :], in0=dn[:, s, :], in1=u[:, t, :], scale=1.0, scalar=0.0,
                                                   op0=ALU.mult, op1=ALU.add, accum_out=pa[:, half, e:e + 1]) \
                                .then_inc(S(f"dn_used{s}"), 1)
                        if nxt:
                            dve.wait_ge(S(f"up_used{SLOTS - 1}"), h * 2 + 1)
                            publish(h + 1, 1 - half)
                        dve.wait_ge(S("pexp"), h + 1)
                        v.reciprocal(psm[:, half, :], psm[:, half, :]).then_inc(S("coef_step"), 1)
                        dve.wait_ge(S("gelu"), h + 1)
                        dve.wait_ge(S("coef_step"), h + 1)
                        v.scalar_tensor_tensor(out=pcoef[:, half, :], in0=pa[:, half, :], scalar=psm[:, half, :],
                                               in1=pex[:, half, :], op0=ALU.mult, op1=ALU.mult).then_inc(S("coef"), 1)
                rounds = PH // 2 - (t == T - 1)
                with dve.Fori(0, rounds) as i:
                    two_heads(i)
                if t == T - 1:
                    two_heads(rounds, final=True)
            for t in range(T):
                dve.wait_ge(S("sq_final"), t + 1)
                last = v.tensor_tensor(ssq[:, t:t + 1], sqf[:, 2 * t:2 * t + 1], sqf[:, 2 * t + 1:2 * t + 2], ALU.add)
            last.then_inc(S("ssq"), 1)
            root("final", T, D)
            for t in range(T):
                for c in range(2):
                    last = v.scalar_tensor_tensor(out=at(t * D + c * N, N), in0=bank[2 * t + c][:, :],
                                                  scalar=rstd[:, t:t + 1], in1=fin[:, c * N:(c + 1) * N],
                                                  op0=ALU.mult, op1=ALU.mult)
                last.then_inc(S("out_ready"), 1)


_INS = ["x", "c", "norm_pre_g", "norm_post_g", "w_mod", "b_mod", "gla_w_in", "gla_w_a2", "gla_b_a",
        "gla_g_head", "gla_w_out", "sgu_w_in", "sgu_ln_g", "sgu_ln_b", "sgu_w_s", "sgu_b_s",
        "sgu_w_out", "fox_w_in", "fox_b_f", "fox_g_q", "fox_g_k", "fox_w_out", "positions_2",
        "norm_mix_2", "w_in_2", "conv_w_2", "w_conv_out_2", "w_attn_out_2", "gate_bias_2", "w_out_2",
        "norm_ffn_2", "peer_w_query_2", "peer_sub_keys_2", "peer_down_2", "peer_up_2", "final_norm_2"]


def kernel(**inputs):
    import concourse.bacc as bacc
    from concourse.bass_utils import run_bass_kernel_spmd

    nc = bacc.Bacc("TRN2", target_bir_lowering=False, num_devices=1)
    data = {name: np.ascontiguousarray(inputs[name]) for name in _INS}
    data.update(constants())
    arrays, views = {}, {}
    for name, a in data.items():
        arrays[f"in_{name}"] = a
        views[name] = nc.dram_tensor(f"in_{name}", a.shape, mybir.dt.from_np(a.dtype), kind="ExternalInput").ap()
    out = nc.dram_tensor("out_0", (1, T * P, D), F32, kind="ExternalOutput").ap()
    build(nc, views, out)
    r = run_bass_kernel_spmd(nc, [arrays], core_ids=[0])
    return r.results[0]["out_0"]
```

```python
from contextlib import ExitStack

import numpy as np
import concourse.bass as bass
from concourse import mybir

F32 = mybir.dt.float32
I32 = mybir.dt.int32
U32 = mybir.dt.uint32
ALU = mybir.AluOpType
ACT = mybir.ActivationFunctionType
X = mybir.AxisListType.X
ds = bass.ds

P = 128
T = 2
D = 1024
KC = D // P
N = 512
EPS = 1e-6
DEPTH = 4
GH, DK, DV = 4, 128, 256
RANK = 16
LEVELS = 7
SG = 4
AH, DH = 16, 64
NG, GHD = 3, 8
ROT = 8
PH, TOPK, NK = 8, 16, 128
SLOTS = 8
MAGIC = 1.5 * 2.0 ** 23
TWO_PI = (6.28125, 1.9340515136718750e-3, 1.2556659146e-6)
PI_SAFE = 3.1415925

BLOCKS = {}
_at = 0
for _name, _n in (("in0", 6), ("out0", 2), ("in1", 6), ("out1", 2), ("in2", 8), ("out2", 2),
                  ("in3", 6), ("out3", 2), ("qkv", 9), ("conv_in", 6), ("gates", 4), ("conv", 2),
                  ("attn", 1), ("hyb_out", 2), ("query", 4)):
    BLOCKS[_name] = _at
    _at += _n


CONV_COLS = [D, 2 * D, D + N, 2 * D + N, 0, N]
GATE_COLS = [3 * D + 4608 + i * N for i in range(4)]


def constants():
    i = np.arange(P)
    row, col = i[:, None], i[None, :]
    ident = np.eye(P, dtype=np.float32)
    sum_mask = (row <= col).astype(np.float32)
    gla = np.zeros((P, LEVELS + 1, P), np.int32)
    gla[:, 0] = row == col
    for l in range(LEVELS):
        size = 1 << l
        same = row // (2 * size) == col // (2 * size)
        gla[:, l + 1] = same & (row // size % 2 == 0) & (col // size % 2 == 1)
    att = np.zeros((P, 4, 3, P), np.float32)
    for n, (steps, dil) in enumerate(((10 ** 6, 1), (128, 1), (128, 4), (128, 16))):
        own, back = row - col, row + P - col
        for part, dist in enumerate((own, back, own)):
            ok = (dist >= 0) & (dist <= steps * dil) & (dist % dil == 0)
            att[:, n, part] = np.where(ok, 0.0, -1e30)
    inv = (np.float32(500000.0) ** (-np.arange(ROT, dtype=np.float32) * np.float32(2.0 / 16)))
    return {
        "k_ident": ident, "k_sum": sum_mask, "k_gla": gla, "k_att": att.reshape(P, 4 * 3 * P),
        "k_freq": inv.astype(np.float32).reshape(1, ROT),
        "k_iota": np.arange(TOPK, dtype=np.float32).reshape(1, TOPK),
    }


def build(nc, A, out, stop=99):
    with ExitStack() as ctx:
        def sb(name, shape, dt=F32):
            return ctx.enter_context(nc.sbuf_tensor(name, shape, dt))

        sems = {}

        def S(name):
            if name not in sems:
                sems[name] = ctx.enter_context(nc.semaphore(name))
            return sems[name]

        ring = sb("ring", [P, 2, KC * N])
        mring = sb("mring", [P, 4, D])
        acc = sb("acc", [P, 3 * D])
        x = sb("x", [P, T, D])
        hT = sb("hT", [P, KC, T * P])
        gateb = sb("gateb", [P, 2, D])
        gpost = sb("gpost", [P, D])
        ghead = sb("ghead", [P, D])
        lng = sb("lng", [P, D])
        lnb = sb("lnb", [P, D])
        gbias = sb("gbias", [P, 2, D])
        nffn, fin = lng, lnb
        big = sb("big", [P, 19584])
        ident = sb("ident", [P, P])
        ones = sb("ones", [P, P])
        summ = sb("summ", [P, P])
        gmask = sb("gmask", [P, LEVELS + 1, P], I32)
        amask = sb("amask", [P, 4, 3 * P])
        rows = sb("rows", [64, P])
        cols = sb("cols", [P, 64])
        cond = sb("cond", [P, KC])
        modc = sb("modc", [P, 2, 2, KC])
        wlow = sb("wlow", [P, 3, KC, RANK])
        wa2 = sb("wa2", [RANK + 1, 2, GH * DK])
        alT = sb("alT", [RANK + 1, T * P])
        low = sb("low", [P, T, RANK])
        low2 = sb("low2", [P, T, RANK])
        bs = sb("bs", [P, SG])
        bf = sb("bf", [P, AH])
        gqk = sb("gqk", [P, 2, DH])
        freq = sb("freq", [P, ROT])
        iota = sb("iota", [P, TOPK])
        posi = sb("posi", [P, T], I32)
        posf = sb("posf", [P, T])
        ssq = sb("ssq", [P, 64])
        rstd = sb("rstd", [P, 64])
        newton = sb("newton", [P, 64])
        small = sb("small", [P, 8])
        trig = sb("trig", [P, 2, T * ROT])
        anm = sb("anm", [P, 10, 8])
        al = sb("al", [P, 10, 8])
        arl = sb("arl", [P, 8])
        lse = sb("lse", [P, 2, NG * 16])
        lsm = sb("lsm", [P, 16])
        pv = sb("pv", [P, 2, TOPK])
        pix = sb("pix", [P, 2, TOPK], U32)
        pixf = sb("pixf", [P, 2, TOPK])
        pbest = sb("pbest", [P, 2, TOPK])
        pneg = sb("pneg", [P, 2, 1])
        ppos = sb("ppos", [P, TOPK], U32)
        pab = sb("pab", [P, 2, TOPK], U32)
        pabf = sb("pabf", [P, 2, TOPK])
        psel = sb("psel", [P, 2, TOPK])
        pidf = sb("pidf", [P, TOPK])
        idx = sb("idx", [P, 2, TOPK], U32)
        idxu = sb("idxu", [P, 2, TOPK], U32)

        pex = gpost[:, 0:32].rearrange("p (a b) -> p a b", a=2)
        pa = gpost[:, 32:64].rearrange("p (a b) -> p a b", a=2)
        pcoef = gpost[:, 64:96].rearrange("p (a b) -> p a b", a=2)
        psm = gpost[:, 96:98].rearrange("p (a b) -> p a b", a=2)
        sqf = gpost[:, 100:100 + 2 * T]

        bank = [ctx.enter_context(nc.psum_tensor(f"bank{i}", [P, N], F32)) for i in range(8)]

        def at(off, *shape):
            size = int(np.prod(shape))
            v = big[:, off:off + size]
            if len(shape) == 2:
                return v.rearrange("p (a b) -> p a b", b=shape[1])
            if len(shape) == 3:
                return v.rearrange("p (a b c) -> p a b c", b=shape[1], c=shape[2])
            if len(shape) == 4:
                return v.rearrange("p (a b c d) -> p a b c d", b=shape[1], c=shape[2], d=shape[3])
            return v

        ob = at(0, T, D)
        xn = at(2 * D, T, D)
        g_in = at(0, T, 3 * D)
        W0 = 6 * D
        b_ = at(W0, GH, T * P)
        qT = at(W0 + D, GH, T * P)
        kT = at(W0 + 2 * D, GH, T * P)
        Q = [at(W0 + 3 * D + i * D, GH * T * P) for i in (0, 1)]
        K = [at(W0 + 5 * D + i * D, GH * T * P) for i in (0, 1)]
        Dd = [at(W0 + 7 * D + i * D, GH * T * P) for i in (0, 1)]
        AT = at(W0 + 9 * D, T, GH * P)
        AX = at(W0 + 10 * D, GH, P)
        ws = at(W0, SG, P)
        wsT = at(W0 + N, SG, P)
        f_in = at(0, T, 4 * D)
        qa = at(8 * D, T, AH, DH + 2)
        ka = at(8 * D + T * AH * (DH + 2), T, AH, DH + 2)
        WF = 8 * D + 2 * T * AH * (DH + 2)
        fo = at(WF + 5 * D, T, D)
        sqs = at(WF, 2, T * D)
        ha = at(0, T, 3 * D)
        hb = at(6 * D, T, 6656)
        QO, KO, VO, GC, GA = 0, 1536, 3072, 4608, 5632
        mflat = mring[:, :, :].rearrange("p a n -> p (a n)")
        zT = mflat[:, 0:KC * 258].rearrange("p (k n) -> p k n", n=258)
        cT = gateb[:, :, :].rearrange("p a (k n) -> p (a k) n", n=T * P)
        od = acc[:, :].rearrange("p (t g n) -> p t g n", t=T, g=NG)
        fox_bufs = (at(WF, 4, T * P), at(WF + D, 4, T * P), at(WF + 2 * D, 4, 3 * P),
                    at(WF + 2 * D + 12 * P, 3, 4, P))
        hyb_bufs = (mflat[:, 0:D].rearrange("p (h n) -> p h n", h=4),
                    mflat[:, D:2 * D].rearrange("p (h n) -> p h n", h=4),
                    gateb[:, :, :].rearrange("p a n -> p (a n)")[:, 0:12 * P].rearrange("p (h n) -> p h n", h=4),
                    mflat[:, 2 * D:2 * D + 12 * P].rearrange("p (b h n) -> p b h n", b=3, h=4))

        def bufs(n):
            return fox_bufs if n < 4 else hyb_bufs
        pk = at(2 * D, 2 * P)
        pk2 = at(2 * D + 256, 2 * P)
        cand = at(2 * D + 512, TOPK, TOPK)
        cand2 = at(2 * D + 768, TOPK * TOPK)
        hot = at(3 * D, 2, TOPK, TOPK)
        diag = ghead[:, 0:4 * P].rearrange("p (s n) -> p s n", n=P)
        zero = ghead[:, 4 * P:5 * P]
        u = at(4 * D, T, D)
        up = at(6 * D, SLOTS, D)
        qq = at(6 * D, 2, T, N)
        pqT = at(8 * D, 2, 4, T * P)
        skT = at(10 * D, 2 * PH, P)
        skr = at(12 * D, 2 * PH, P)
        sc = at(14 * D, T, 2 * D)
        dn = [mring[:, i, :] for i in range(4)] + [acc[:, i * D:(i + 1) * D] for i in range(3)] + [gateb[:, 0, :]]

        block = ctx.enter_context(nc.Block())

        CONSTS = 10 + SG + T + 2
        LINKS, BEST = 20, 11
        ORDER = {}

        def orderer(eng, name):
            ORDER[name] = 0

            def link(ins, wait=True):
                ORDER[name] += 1
                ins.then_inc(S(name), 1)
                if wait:
                    eng.wait_ge(S(name), ORDER[name])
            return link

        NORMS = ["norm0", "head0", "post0", "norm1", "ln", "post1", "norm2", "qk", "post2", "norm3", "head3",
                 "post3", "mix", "ffn", "final"]

        def nth(tag):
            return NORMS.index(tag) + 1

        @block.sync
        def _(sp):
            def load(dst, src, sem):
                sp.dma_start(dst, src).then_inc(S(sem), 16)

            load(rows[0:32, :], A["norm_pre_g"].rearrange("l (k p) -> (l k) p", p=P), "rows_in")
            load(rows[32:40, :], A["norm_mix_2"].rearrange("l (k p) -> (l k) p", p=P), "rows_in")
            load(rows[40:64, :], A["conv_w_2"][0].rearrange("i (k p) -> (i k) p", p=P), "rows_in")
            load(cond[:, :], A["c"].rearrange("b (p k) -> (b p) k", k=KC), "cond_in")
            load(ident[:, :], A["k_ident"], "rows_in")
            load(x[:, :, :], A["x"][0].rearrange("(t p) d -> p t d", p=P), "x_in")

            def src_of(w, col):
                return w.rearrange("(k p) n -> p k n", p=P)[:, :, ds(col, N)]

            def put(slot, src):
                sp.dma_start(ring[:, slot, :].rearrange("p (k n) -> p k n", n=src.shape[2]), src) \
                    .then_inc(S(f"w_landed{slot}"), 16)

            def stream(name, n, w):
                b0 = BLOCKS[name]
                start = 1 if b0 == 0 else 0

                def pair(i):
                    for slot in range(2):
                        sp.wait_ge(S("proj_done1"), b0 + 2 * i + slot - 1)
                        put(slot, src_of(w, i * (2 * N) + slot * N))

                if n // 2 - start > 1:
                    with sp.Fori(start, n // 2) as i:
                        pair(i)
                elif n // 2 - start == 1:
                    pair(start)

            def one(b, src):
                sp.wait_ge(S("proj_done1"), b - 1)
                put(b % 2, src)

            for i in range(2):
                put(i, src_of(A["gla_w_in"][0], i * N))
            for n, (name, w, c0) in enumerate((("gla_w_in", 0, 3072), ("gla_w_in", 1, 3072),
                                               ("fox_w_in", 0, 4096))):
                load(wlow[:, n, :, :], A[name][w].rearrange("(k p) n -> p k n", p=P)[:, :, c0:c0 + RANK],
                     "wlow_in")
            for j in range(2):
                load(wa2[0:RANK, j, :], A["gla_w_a2"][j], "wlow_in")
                load(wa2[RANK:RANK + 1, j, :], A["gla_b_a"][j:j + 1, :], "wlow_in")
            load(gmask[:, :, :], A["k_gla"], "consts_in")
            load(summ[:, :], A["k_sum"], "consts_in")
            load(amask[:, :, :], A["k_att"].rearrange("p (a b) -> p a b", a=4), "consts_in")
            load(ghead[:, :], A["gla_g_head"][0:1].rearrange("a h v -> a (h v)").to_broadcast([P, D]), "ghead_in")
            load(lng[:, :], A["sgu_ln_g"].to_broadcast([P, D]), "consts_in")
            load(lnb[:, :], A["sgu_ln_b"].to_broadcast([P, D]), "consts_in")
            load(gqk[:, 0, :], A["fox_g_q"].to_broadcast([P, DH]), "consts_in")
            load(gqk[:, 1, :], A["fox_g_k"].to_broadcast([P, DH]), "consts_in")
            load(bf[:, :], A["fox_b_f"].to_broadcast([P, AH]), "consts_in")
            load(freq[:, :], A["k_freq"].to_broadcast([P, ROT]), "consts_in")
            load(iota[:, :], A["k_iota"].to_broadcast([P, TOPK]), "consts_in")
            for g in range(SG):
                load(bs[:, g:g + 1], A["sgu_b_s"][0, g:g + 1, :].rearrange("a p -> p a"), "consts_in")
            for t in range(T):
                load(posi[:, t:t + 1], A["positions_2"][:, t * P:(t + 1) * P].rearrange("a p -> p a"),
                     "consts_in")
            for i in range(2):
                load(gbias[:, i, :], A["gate_bias_2"][0, i:i + 1, :].to_broadcast([P, D]), "consts_in")
            if stop < 1:
                return
            stream("in0", 6, A["gla_w_in"][0])
            stream("out0", 2, A["gla_w_out"][0])
            if stop < 2:
                return
            stream("in1", 6, A["sgu_w_in"][0])
            sp.wait_ge(S("x_ready"), 1)
            load(ws, A["sgu_w_s"][0].rearrange("g t s -> t g s"), "ws_in")
            stream("out1", 2, A["sgu_w_out"][0])
            if stop < 3:
                return
            stream("in2", 8, A["fox_w_in"][0])
            sp.wait_ge(S("x_ready"), 2)
            load(nffn[:, :], A["norm_ffn_2"].to_broadcast([P, D]), "last_rows_in")
            load(fin[:, :], A["final_norm_2"].rearrange("(a d) -> a d", a=1).to_broadcast([P, D]), "last_rows_in")
            stream("out2", 2, A["fox_w_out"][0])
            if stop < 4:
                return
            sp.wait_ge(S("gated"), 1)
            load(ghead[:, :], A["gla_g_head"][1:2].rearrange("a h v -> a (h v)").to_broadcast([P, D]), "ghead_in")
            stream("in3", 6, A["gla_w_in"][1])
            stream("out3", 2, A["gla_w_out"][1])
            if stop < 5:
                return
            b0 = BLOCKS["qkv"]
            with sp.Fori(0, 4) as i:
                for slot in range(2):
                    sp.wait_ge(S("proj_done1"), b0 + 2 * i + slot - 1)
                    put(slot, src_of(A["w_in_2"][0], i * (2 * N) + (3 * D + slot * N)))
            one(b0 + 8, src_of(A["w_in_2"][0], 3 * D + 8 * N))
            for i, col in enumerate(CONV_COLS + GATE_COLS):
                one(BLOCKS["conv_in"] + i, src_of(A["w_in_2"][0], col))
            one(BLOCKS["conv"], src_of(A["w_conv_out_2"][0], 0))
            one(BLOCKS["conv"] + 1, src_of(A["w_conv_out_2"][0], N))
            one(BLOCKS["attn"], A["w_attn_out_2"][0].rearrange("(k p) n -> p k n", p=P))
            stream("hyb_out", 2, A["w_out_2"][0])
            if stop < 6:
                return
            sp.wait_ge(S("merged"), 1)
            load(skr, A["peer_sub_keys_2"][0].rearrange("h c k d -> k (h c) d"), "sk_in")
            stream("query", 4, A["peer_w_query_2"][0])
            if stop < 7:
                return
            for t in range(T):
                sp.wait_ge(S("out_ready"), t + 1)
                sp.dma_start(out[0, t * P:(t + 1) * P, :], at(t * D, D)).then_inc(S("out_stored"), 16)
            sp.wait_ge(S("out_stored"), 16 * T)

        @block.gpsimd
        def _(pool):
            link = orderer(pool, "pool_order")
            link(nc.gpsimd.memset(ones[:, :], 1.0), wait=False)
            nc.gpsimd.memset(alT[:, :], 1.0).then_inc(S("ones_set"), 1)

            def modulation(L):
                if L:
                    pool.wait_ge(S("mod_read"), L)
                link(nc.gpsimd.memset(acc[:, :], 0.0))
                pool.dma_start(acc[0:1, :], A["b_mod"][L:L + 1, :]).then_inc(S("acc_init"), 16)
                if L:
                    pool.wait_ge(S("mod_ready"), L)
                pool.dma_start(gpost[:, :], A["norm_post_g"][L:L + 1, :].to_broadcast([P, D])) \
                    .then_inc(S("gpost_in"), 16)
                w = A["w_mod"][L].rearrange("(p k) n -> p k n", k=KC)
                for third in range(3):
                    def four(i, first=False):
                        for q in range(4):
                            if not first:
                                pool.wait_ge(S("mod_sum"), (L * 3 + third) * KC + 4 * i + q - 3)
                            pool.dma_start(mring[:, q, :],
                                           w[:, ds(4 * i + q, 1), third * D:(third + 1) * D]
                                           .rearrange("p a n -> p (a n)")) \
                                .then_inc(S(f"mod_landed{q}"), 16)
                    for i in range(2):
                        four(i, first=(L == 0 and third == 0 and i == 0))

            modulation(0)
            if stop < 1:
                return
            for L in range(1, DEPTH):
                if stop < L:
                    return
                modulation(L)
            if stop < 7:
                return
            def gather(h, par, kind, tab, index):
                pool.wait_ge(S(f"{kind}_picks"), h + 1)
                for e in range(TOPK):
                    s = e % SLOTS
                    pool.wait_ge(S(f"{kind}_used{s}"), h * 2 + e // SLOTS + 1)
                    pool.nop(nofuse=True)
                    pool.indirect_dma_start(
                        out=dn[s] if kind == "dn" else up[:, s, :], out_offset=None, in_=A[tab][0],
                        in_offset=bass.IndirectOffsetOnAxis(ap=index[:, par, e:e + 1], axis=0)
                    ).then_inc(S(f"{kind}_landed{s}"), 16)

            def two_heads(h, final=False):
                for half in range(2):
                    if not (final and half):
                        gather(h + half + 1, 1 - half, "dn", "peer_down_2", idx)
                    gather(h + half, half, "up", "peer_up_2", idxu)

            gather(0, 0, "dn", "peer_down_2", idx)
            pool.wait_ge(S("sc_sb"), 4)
            with pool.Fori(0, PH - 1) as i:
                two_heads(i * 2)
            two_heads(2 * PH - 2, final=True)

        @block.tensor
        def _(pe):
            mm, tr = nc.tensor.matmul, nc.tensor.transpose

            def transpose_in(src, tag, chunks=KC, banks=(2, 3, 4, 5)):
                for k in range(chunks):
                    for t in range(T):
                        last = tr(bank[banks[k // 2]][:, (k % 2) * 256 + t * P:(k % 2) * 256 + (t + 1) * P],
                                  src(t, k), ident[:, :])
                    if k % 2:
                        last.then_inc(S(tag), 1)

            def half_block(b, slot, t, rhs=None):
                if t == 0:
                    pe.wait_ge(S(f"w_landed{slot}"), (b - slot) * 8 + 16)
                pe.wait_ge(S(f"evac{t}"), b + 1)
                for k in range(KC):
                    last = mm(bank[t][:, :], hT[:, k, t * P:(t + 1) * P], ring[:, slot, k * N:(k + 1) * N],
                              start=(k == 0), stop=(k == KC - 1))
                last.then_inc(S(f"proj_done{t}"), 1)

            def block_products(b, slot):
                for t in range(T):
                    half_block(b, slot, t)

            def one_block(b):
                block_products(b, b % 2)

            def project(name, n):
                b0 = BLOCKS[name]

                def pair(i):
                    for slot in range(2):
                        block_products(b0 + 2 * i + slot, slot)
                if n > 2:
                    with pe.Fori(0, n // 2) as i:
                        pair(i)
                else:
                    pair(0)

            def low_columns(n, tag):
                pe.wait_ge(S("wlow_in"), 7 * 16)
                for t in range(T):
                    for k in range(KC):
                        last = mm(bank[6][:, t * RANK:(t + 1) * RANK], hT[:, k, t * P:(t + 1) * P],
                                  wlow[:, n, k, :], start=(k == 0), stop=(k == KC - 1))
                last.then_inc(S(tag), 1)

            def mod_reduce(L):
                pe.wait_ge(S("mod_sum"), L * 3 * KC + 2 * KC)
                for j in range(2 * KC):
                    last = mm(bank[2][:, j:j + 1], acc[:, j * P:(j + 1) * P], ones[:, 0:1], start=True, stop=True)
                last.then_inc(S("mod_cols"), 1)

            def gate_reduce(L):
                pe.wait_ge(S("mod_sum"), (L + 1) * 3 * KC)
                for i in range(2):
                    last = mm(bank[3 + i][:, :], ones[:, :], acc[:, 2 * D + i * N:2 * D + (i + 1) * N],
                              start=True, stop=True)
                last.then_inc(S("mod_read"), 1)

            def quads(first, count, q, k, v, kd, between):
                def transposed(n, src, bk):
                    for h in range(4):
                        for t in range(T):
                            last = tr(bank[bk + h // 2][0:kd, (h % 2) * 256 + t * P:(h % 2) * 256 + (t + 1) * P],
                                      src(n, h, t), ident[:, :])
                    last.then_inc(S("att_T"), 1)

                aqT, akT, aS, aPT = bufs(first)
                transposed(0, q, 6)
                transposed(0, k, 3)
                for i in range(count):
                    n = first + i
                    pe.wait_ge(S("att_qT"), n + 1)
                    pe.wait_ge(S("att_kT"), n + 1)
                    if n:
                        pe.wait_ge(S("att_o"), n)
                    for h in range(4):
                        mm(bank[5][:, h * P:(h + 1) * P], aqT[0:kd, h, 0:P], akT[0:kd, h, 0:P], start=True, stop=True)
                    for h in range(4):
                        last = mm(bank[6 + h // 2][:, (h % 2) * 256:(h % 2 + 1) * 256],
                                  aqT[0:kd, h, P:2 * P], akT[0:kd, h, :], start=True, stop=True)
                    last.then_inc(S("att_s"), 1)
                    between(i)
                    pe.wait_ge(S("att_p"), n + 1)
                    for b in range(3):
                        for h in range(4):
                            last = tr(bank[2 + b][:, h * P:(h + 1) * P], aS[:, h, b * P:(b + 1) * P], ident[:, :])
                        last.then_inc(S("att_pt"), 1)
                    if i + 1 < count:
                        transposed(i + 1, q, 6)
                    pe.wait_ge(S("att_pta"), n + 1)
                    pe.wait_ge(S("att_ptv"), n + 1)
                    if i + 1 < count:
                        transposed(i + 1, k, 3)
                    for h in range(4):
                        mm(bank[5][:, h * DH:(h + 1) * DH], aPT[:, 0, h, :], v(i, h, 0), start=True, stop=True)
                    for h in range(4):
                        o = bank[5][:, 256 + h * DH:256 + (h + 1) * DH]
                        mm(o, aPT[:, 1, h, :], v(i, h, 0), start=True, stop=False)
                        last = mm(o, aPT[:, 2, h, :], v(i, h, 1), start=False, stop=True)
                    last.then_inc(S("att_pv"), 1)

            def gla(L, j):
                b0 = BLOCKS[f"in{L}"]
                low_columns(j, "low")
                one_block(b0 + 2)
                if L + 1 < DEPTH:
                    mod_reduce(L + 1)
                    gate_reduce(L + 1)
                pe.wait_ge(S("low_sb"), L // 3 + 1)
                for t in range(T):
                    last = tr(bank[7][0:RANK, t * P:(t + 1) * P], low[:, t, :], ident[:, :])
                last.then_inc(S("lowT"), 1)
                pe.wait_ge(S("alT"), L // 3 + 1)
                for h in range(GH):
                    last = mm(bank[6 + h // 2][:, (h % 2) * 256:(h % 2 + 1) * 256],
                              wa2[:, j, h * DK:(h + 1) * DK], alT[:, :], start=True, stop=True)
                last.then_inc(S("decay"), 1)
                for t in range(T):
                    pe.wait_ge(S(f"evac{t}"), b0 + 3)
                if L + 1 < DEPTH:
                    pe.wait_ge(S("mod_ready"), L + 2)
                for i in range(2):
                    for h in range(GH):
                        for t in range(T):
                            last = tr(bank[2 + 2 * i + h // 2][:, (h % 2) * 256 + t * P:(h % 2) * 256 + (t + 1) * P],
                                      g_in[:, t, i * N + h * DK:i * N + (h + 1) * DK], ident[:, :])
                last.then_inc(S("qkT"), 1)
                one_block(b0 + 3)
                pe.wait_ge(S("qkT_sb"), L // 3 + 1)
                pe.wait_ge(S("logd"), L // 3 + 1)
                for lv in range(LEVELS + 2):
                    q_, k_ = (qT, kT) if lv == 0 else (
                        Q[lv % 2].rearrange("p (h n) -> p h n", h=GH), K[lv % 2].rearrange("p (h n) -> p h n", h=GH))
                    if lv:
                        pe.wait_ge(S("lvl_qk"), L // 3 * (LEVELS + 1) + lv)
                    if lv >= 2:
                        pe.wait_ge(S("lvl_read"), L // 3 * (LEVELS + 1) + lv - 1)
                    bk = (6, 2)[lv % 2]
                    if lv <= LEVELS:
                        for t in range(T):
                            for h in range(GH):
                                last = mm(bank[bk + t][:, h * P:(h + 1) * P], k_[:, h, t * P:(t + 1) * P],
                                          q_[:, h, t * P:(t + 1) * P], start=True, stop=True)
                    else:
                        for h in range(GH):
                            last = mm(bank[bk][:, h * P:(h + 1) * P], k_[:, h, 0:P], q_[:, h, P:2 * P],
                                      start=True, stop=True)
                    last.then_inc(S("lvl"), 1)
                    if lv % 2:
                        half_block(b0 + 4 + lv // 4, (b0 + lv // 4) % 2, lv // 2 % 2)
                pe.wait_ge(S("attn_sb"), L // 3 + 1)
                for t in range(T):
                    for h in range(GH):
                        o = bank[2 + 2 * t + h // 2][:, (h % 2) * 256:(h % 2 + 1) * 256]
                        last = mm(o, AT[:, t, h * P:(h + 1) * P], g_in[:, t, D + h * DV:D + (h + 1) * DV],
                                  start=True, stop=(t == 0))
                        if t:
                            last = mm(o, AX[:, h, :], g_in[:, 0, D + h * DV:D + (h + 1) * DV],
                                      start=False, stop=True)
                last.then_inc(S("gla_o"), 1)

            def sgu():
                pe.wait_ge(S("ws_in"), 16)
                pe.wait_ge(S("hT"), 2)
                for g in range(SG):
                    last = tr(bank[2][:, g * P:(g + 1) * P], ws[:, g, :], ident[:, :])
                last.then_inc(S("wsT"), 1)
                pe.wait_ge(S("ln_done"), 1)
                for t in range(T):
                    for g in range(SG):
                        last = mm(bank[2 + 2 * t + g // 2][:, (g % 2) * 256:(g % 2 + 1) * 256],
                                  wsT[:, g, :], g_in[:, t, D + g * 256:D + (g + 1) * 256],
                                  start=True, stop=True)
                last.then_inc(S("mixed"), 1)

            def fox():
                b0 = BLOCKS["in2"]
                low_columns(2, "low")
                one_block(b0 + 4)
                mod_reduce(3)
                gate_reduce(3)
                pe.wait_ge(S("logf"), 1)
                pe.wait_ge(S("consts_in"), CONSTS * 16)
                mm(bank[7][:, 0:AH], summ[:, :], low2[:, 0, :], start=True, stop=True)
                mm(bank[7][:, AH:2 * AH], ones[:, :], low2[:, 0, :], start=True, stop=False)
                mm(bank[7][:, AH:2 * AH], summ[:, :], low2[:, 1, :], start=False, stop=True) \
                    .then_inc(S("fsum"), 1)
                pe.wait_ge(S("mod_ready"), 4)
                pe.wait_ge(S("qka"), 1)

                def between(n):
                    if n < 3:
                        one_block(b0 + 5 + n)

                quads(0, 4, lambda n, h, t: qa[:, t, 4 * n + h, :], lambda n, h, t: ka[:, t, 4 * n + h, :],
                      lambda n, h, t: f_in[:, t, 2 * D + (4 * n + h) * DH:2 * D + (4 * n + h + 1) * DH],
                      DH + 2, between)

            pe.wait_ge(S("rows_in"), 4 * 16)
            tr(bank[7][:, 0:64], rows[:, :], ident[0:64, 0:64]).then_inc(S("colsT"), 1)
            pe.wait_ge(S("ones_set"), 1)
            pe.wait_ge(S("pool_order"), 1)
            mod_reduce(0)
            for L in range(DEPTH):
                if stop < L + 1:
                    return
                pe.wait_ge(S("xn"), L + 1)
                if L:
                    pe.wait_ge(S("mod_ready"), L + 1)
                else:
                    pe.wait_ge(S("mod_cols_sb"), 1)
                transpose_in(lambda t, k: xn[:, t, k * P:(k + 1) * P], "xT")
                pe.wait_ge(S("hT"), L + 1)
                project(f"in{L}", (2, 6, 4, 2)[L])
                if L == 0:
                    gate_reduce(0)
                    pe.wait_ge(S("mod_ready"), 1)
                if L == 1:
                    mod_reduce(2)
                    gate_reduce(2)
                    pe.wait_ge(S("mod_ready"), 3)
                if L in (0, 3):
                    gla(L, L // 3)
                elif L == 1:
                    sgu()
                else:
                    fox()
                pe.wait_ge(S("gated"), L + 1)
                src = fo if L == 2 else g_in[:, :, 2 * D:3 * D]
                transpose_in(lambda t, k: src[:, t, k * P:(k + 1) * P], "gT")
                pe.wait_ge(S("ghT"), L + 1)
                project(f"out{L}", 2)
            if stop < 5:
                return
            pe.wait_ge(S("xn"), DEPTH + 1)
            transpose_in(lambda t, k: xn[:, t, k * P:(k + 1) * P], "xT")
            pe.wait_ge(S("hT"), DEPTH + 1)
            b0 = BLOCKS["qkv"]
            project("qkv", 8)
            one_block(b0 + 8)
            pe.wait_ge(S("rotated"), 1)

            def head(c0):
                return lambda n, h, t: hb[:, t, c0 + (4 * n + h) * DH:c0 + (4 * n + h + 1) * DH]

            quads(4, 6, head(QO), head(KO), head(VO), DH, lambda n: one_block(BLOCKS["conv_in"] + n))
            pe.wait_ge(S("z_conv"), 1)
            one_block(BLOCKS["gates"])
            transpose_in(lambda t, k: ha[:, t, D + k * P:D + (k + 1) * P], "zT")
            one_block(BLOCKS["gates"] + 1)
            one_block(BLOCKS["gates"] + 2)
            one_block(BLOCKS["gates"] + 3)
            pe.wait_ge(S("zT_sb"), 1)
            transpose_in(lambda t, k: ha[:, t, k * P:(k + 1) * P], "bT")
            pe.wait_ge(S("conv_hT"), 1)
            for i in range(2):
                one_block(BLOCKS["conv"] + i)
            pe.wait_ge(S("att_merged"), 1)
            transpose_in(lambda t, k: od[:, t, 0, k * P:(k + 1) * P], "oT", chunks=4)
            pe.wait_ge(S("oT_sb"), 1)
            b = BLOCKS["attn"]
            pe.wait_ge(S(f"w_landed{b % 2}"), (b // 2 + 1) * 16)
            wv = ring[:, b % 2, :].rearrange("p (k n) -> p k n", n=D)
            for half in (1, 0):
                for t in range(T):
                    if half == 0:
                        pe.wait_ge(S(f"evac{t}"), b + 1)
                    for k in range(4):
                        last = mm(bank[t + 6 * half][:, :], hT[:, k, t * P:(t + 1) * P],
                                  wv[:, k, half * N:(half + 1) * N], start=(k == 0), stop=(k == 3))
                    last.then_inc(S("attn_half") if half else S(f"proj_done{t}"), 1)
            pe.wait_ge(S("merged"), 1)
            transpose_in(lambda t, k: ha[:, t, k * P:(k + 1) * P], "mT")
            pe.wait_ge(S("mT_sb"), 1)
            project("hyb_out", 2)
            if stop < 6:
                return
            pe.wait_ge(S("u_ready"), 1)
            transpose_in(lambda t, k: u[:, t, k * P:(k + 1) * P], "uT")
            pe.wait_ge(S("uT_sb"), 1)
            pe.wait_ge(S("sk_in"), 16)
            for g in range(4):
                for i in range(4):
                    last = tr(bank[2 + g][:, i * P:(i + 1) * P], skr[:, 4 * g + i, :], ident[:, :])
                last.then_inc(S("skT"), 1)
            for b in range(4):
                one_block(BLOCKS["query"] + b)
                for t in range(T):
                    pe.wait_ge(S(f"evac{t}"), BLOCKS["query"] + b + 2)
                pe.wait_ge(S("pq_sb"), b + 1)
                for i in range(4):
                    for t in range(T):
                        last = tr(bank[6 + i // 2][:, (i % 2) * 256 + t * P:(i % 2) * 256 + (t + 1) * P],
                                  qq[:, b % 2, t, i * P:(i + 1) * P], ident[:, :])
                last.then_inc(S("pqT"), 1)
                pe.wait_ge(S("pq_sb"), b + 2)
                if b:
                    pe.wait_ge(S("sc_sb"), b)
                for t in range(T):
                    for i in range(4):
                        last = mm(bank[4 + t][:, i * P:(i + 1) * P], pqT[:, b % 2, i, t * P:(t + 1) * P],
                                  skT[:, 4 * b + i, :], start=True, stop=True)
                last.then_inc(S("sc_mm"), 1)
            if stop < 7:
                return
            for t in range(T):
                for i in range(2):
                    mm(bank[2 * t + i][:, :], ident[:, :], x[:, t, i * N:(i + 1) * N], start=True, stop=False,
                       skip_group_check=True)

                def two_heads(i):
                    for half in range(2):
                        h = i * 2 + half + t * PH
                        for e in range(TOPK):
                            s = e % SLOTS
                            pe.wait_ge(S("diag"), h * TOPK + e + 1)
                            pe.wait_ge(S(f"up_landed{s}"), (h * 2 + e // SLOTS + 1) * 16)
                            for c in range(2):
                                last = mm(bank[2 * t + c][:, :], diag[:, e % 4, :], up[:, s, c * N:(c + 1) * N],
                                          start=False, stop=False, skip_group_check=True)
                            last.then_inc(S(f"up_used{s}"), 1)
                with pe.Fori(0, PH // 2) as i:
                    two_heads(i)
                for c in range(2):
                    last = mm(bank[2 * t + c][:, :], zero[:, :], x[:, t, c * N:(c + 1) * N],
                              start=False, stop=True, skip_group_check=True)
                last.then_inc(S("peer_done"), 1)

        @block.scalar
        def _(act):
            link = orderer(act, "act_order")
            af = nc.scalar.activation

            def half(b, t, dst):
                act.wait_ge(S(f"proj_done{t}"), b + 1)
                af(dst, bank[t][:, :], ACT.Copy).then_inc(S(f"evac{t}"), 1)

            def evac(b, slot, dst):
                for t in range(T):
                    half(b, t, dst(t))

            def one_block(b, buf, col):
                evac(b, b % 2, lambda t: buf[:, t, col:col + N])

            def project(name, n, dst):
                b0 = BLOCKS[name]

                def pair(i):
                    for slot in range(2):
                        evac(b0 + 2 * i + slot, slot, lambda t: dst[:, t, ds(i * (2 * N) + slot * N, N)])
                if n > 2:
                    with act.Fori(0, n // 2) as i:
                        pair(i)
                else:
                    pair(0)

            def evac_done(b):
                for t in range(T):
                    act.wait_ge(S(f"evac{t}"), b + 1)

            def root(tag, n, width):
                act.wait_ge(S("ssq"), nth(tag))
                link(af(rstd[:, 0:n], ssq[:, 0:n], ACT.Ln, scale=1.0 / width, bias=EPS))
                af(rstd[:, 0:n], rstd[:, 0:n], ACT.Exp, scale=-0.5).then_inc(S("root"), 1)

            def squares(src, tag, wait=True):
                for t in range(T):
                    last = af(xn[:, t, :], src[:, t, :], ACT.Square, accum_out=ssq[:, t:t + 1])
                last.then_inc(S("ssq"), 1)
                root(tag, T, D)

            def quads(first, count, kd, between):
                aqT, akT, aS, aPT = bufs(first)

                def q_in(n):
                    act.wait_ge(S("att_T"), 2 * n + 1)
                    for i in range(2):
                        last = af(aqT[0:kd, 2 * i:2 * i + 2, :].rearrange("p h n -> p (h n)"),
                                  bank[6 + i][0:kd, :], ACT.Copy)
                    last.then_inc(S("att_qT"), 1)

                q_in(first)
                for i in range(count):
                    n = first + i
                    act.wait_ge(S("att_m"), n + 1)
                    for h in range(4):
                        for t in range(T):
                            part = aS[:, h, 0:P] if t == 0 else aS[:, h, P:3 * P]
                            last = af(part, part, ACT.Exp, bias=anm[:, n, 2 * h + t:2 * h + t + 1],
                                      accum_out=al[:, n, 2 * h + t:2 * h + t + 1])
                    last.then_inc(S("att_p"), 1)
                    between(i)
                    act.wait_ge(S("att_pt"), 3 * n + 1)
                    af(aPT[:, 0, :, :].rearrange("p h n -> p (h n)"), bank[2][:, :], ACT.Copy)
                    act.wait_ge(S("att_pt"), 3 * n + 3)
                    af(aPT[:, 2, :, :].rearrange("p h n -> p (h n)"), bank[4][:, :], ACT.Copy) \
                        .then_inc(S("att_pta"), 1)
                    if i + 1 < count:
                        q_in(n + 1)

            act.wait_ge(S("cond_in"), 16)
            af(cond[:, :], cond[:, :], ACT.Silu).then_inc(S("cond"), 1)
            act.wait_ge(S("x_in"), 16)
            for L in range(DEPTH):
                if stop < L + 1:
                    return
                if L:
                    act.wait_ge(S("x_ready"), L)
                squares(x, f"norm{L}")
                b0 = BLOCKS[f"in{L}"]
                project(f"in{L}", (2, 6, 4, 2)[L], f_in if L == 2 else g_in)
                if L in (0, 3):
                    one_block(b0 + 2, g_in, 2 * N)
                    act.wait_ge(S("decay"), L // 3 + 1)
                    ya = Dd[0]
                    for i in range(2):
                        link(af(ya[:, i * N:(i + 1) * N], bank[6 + i][:, :], ACT.Abs))
                    link(af(ya, ya, ACT.Exp, scale=-1.0))
                    af(ya, ya, ACT.Ln, bias=1.0).then_inc(S("lnd"), 1)
                    act.wait_ge(S("qkT"), L // 3 + 1)
                    for i in range(2):
                        af(qT[:, 2 * i:2 * i + 2, :].rearrange("p h n -> p (h n)"), bank[2 + i][:, :],
                           ACT.Copy, scale=DK ** -0.5)
                        last = af(kT[:, 2 * i:2 * i + 2, :].rearrange("p h n -> p (h n)"),
                                  bank[4 + i][:, :], ACT.Copy)
                    last.then_inc(S("qkT_sb"), 1)
                    for lv in range(1, LEVELS + 2):
                        act.wait_ge(S("lvl_d"), L // 3 * (LEVELS + 1) + lv)
                        af(Dd[lv % 2], Dd[lv % 2], ACT.Exp).then_inc(S("lvl_e"), 1)
                        if lv == 2:
                            one_block(b0 + 3, g_in, 3 * N)
                        if lv % 2 == 0 and lv >= 4:
                            hf = lv // 2 - 2
                            half(b0 + 4 + hf // 2, hf % 2, g_in[:, hf % 2, (4 + hf // 2) * N:(5 + hf // 2) * N])
                    half(b0 + 5, 1, g_in[:, 1, 5 * N:6 * N])
                    evac_done(b0 + 6)
                    af(g_in[:, :, 2 * D:3 * D], g_in[:, :, 2 * D:3 * D], ACT.Silu).then_inc(S("silu"), 1)
                    act.wait_ge(S("gla_o"), L // 3 + 1)
                    for t in range(T):
                        for h in range(GH):
                            last = af(at(W0 + 7 * D + (t * GH + h) * DV, DV), bank[2 + 2 * t + h // 2][:, (h % 2) * DV:(h % 2 + 1) * DV],
                                      ACT.Square, accum_out=ssq[:, t * GH + h:t * GH + h + 1])
                    last.then_inc(S("ssq"), 1)
                    root(f"head{L}", T * GH, DV)
                elif L == 1:
                    evac_done(b0 + 6)
                    for t in range(T):
                        link(af(g_in[:, t, D:2 * D], g_in[:, t, D:2 * D], ACT.Gelu_apprx_tanh,
                                accum_out=small[:, t:t + 1]), wait=(t == T - 1))
                    act.wait_ge(S("act_order"), ORDER["act_order"])
                    link(af(small[:, 2:4], small[:, 0:2], ACT.Copy, scale=-1.0 / D))
                    for t in range(T):
                        link(af(g_in[:, t, D:2 * D], g_in[:, t, D:2 * D], ACT.Identity, bias=small[:, 2 + t:3 + t]))
                        last = af(at(W0 + (2 + t) * D, D), g_in[:, t, D:2 * D], ACT.Square, accum_out=ssq[:, t:t + 1])
                    last.then_inc(S("ssq"), 1)
                    root("ln", T, D)
                    af(g_in[:, :, 0:D], g_in[:, :, 0:D], ACT.Gelu_apprx_tanh)
                    af(g_in[:, :, 2 * D:3 * D], g_in[:, :, 2 * D:3 * D], ACT.Silu).then_inc(S("silu"), 1)
                else:
                    evac_done(b0 + 4)
                    for i in range(2):
                        last = af(sqs[:, i, :].rearrange("p (t d) -> p t d", t=T), f_in[:, :, i * D:(i + 1) * D],
                                  ACT.Square)
                    last.then_inc(S("sq_qk"), 1)
                    act.wait_ge(S("f_sb"), 1)
                    link(af(low2[:, :, :], low[:, :, :], ACT.Abs))
                    link(af(low2[:, :, :], low2[:, :, :], ACT.Exp, scale=-1.0))
                    af(low2[:, :, :], low2[:, :, :], ACT.Ln, bias=1.0).then_inc(S("lnf"), 1)
                    root("qk", 4 * AH, DH)
                    one_block(b0 + 4, f_in, 4 * N)
                    quads(0, 4, DH + 2, lambda n: one_block(b0 + 5 + n, f_in, (5 + n) * N) if n < 3 else None)
                    evac_done(b0 + 8)
                    af(f_in[:, :, 3 * D:4 * D], f_in[:, :, 3 * D:4 * D], ACT.Silu).then_inc(S("silu"), 1)
                project(f"out{L}", 2, ob)
                evac_done(BLOCKS[f"out{L}"] + 2)
                squares(ob, f"post{L}")
            if stop < 5:
                return
            act.wait_ge(S("angles"), 1)
            af(trig[:, :, :], trig[:, :, :], ACT.Sin).then_inc(S("trig"), 1)
            act.wait_ge(S("x_ready"), 4)
            squares(x, "mix")
            project("qkv", 8, hb)
            one_block(BLOCKS["qkv"] + 8, hb, 8 * N)
            quads(4, 6, DH, lambda n: one_block(BLOCKS["conv_in"] + n, ha, CONV_COLS[n]))
            one_block(BLOCKS["gates"], hb, GC)
            act.wait_ge(S("lse_in"), 1)
            af(lse[:, 0, :], al[:, 4:10, :].rearrange("p n h -> p (n h)"), ACT.Ln).then_inc(S("lse_ln"), 1)
            act.wait_ge(S("lse_m"), 1)
            af(lse[:, 0, :], lse[:, 1, :], ACT.Exp).then_inc(S("lse_e"), 1)
            for i in range(1, 4):
                one_block(BLOCKS["gates"] + i, hb, GC + i * N)
            act.wait_ge(S("gates_in"), 1)
            af(hb[:, :, GC:GC + 2 * D], hb[:, :, GC:GC + 2 * D], ACT.Sigmoid).then_inc(S("gates"), 1)
            act.wait_ge(S("conv_hT"), 1)
            for i in range(2):
                one_block(BLOCKS["conv"] + i, ha, i * N)
            act.wait_ge(S("attn_half"), 2)
            for t in range(T):
                af(ha[:, t, D + N:2 * D], bank[6 + t][:, :], ACT.Copy)
            b = BLOCKS["attn"]
            evac(b, b % 2, lambda t: ha[:, t, D:D + N])
            project("hyb_out", 2, ha[:, :, 2 * D:3 * D])
            if stop < 6:
                return
            act.wait_ge(S("x_ready"), 5)
            squares(x, "ffn")
            for g in range(4):
                act.wait_ge(S("skT"), g + 1)
                last = af(skT[:, 4 * g:4 * g + 4, :].rearrange("p i n -> p (i n)"), bank[2 + g][:, :], ACT.Copy)
            last.then_inc(S("pq_sb"), 1)
            for b in range(4):
                evac(BLOCKS["query"] + b, b % 2, lambda t: qq[:, b % 2, t, :])
                act.wait_ge(S("pqT"), b + 1)
                for i in range(2):
                    last = af(pqT[:, b % 2, 2 * i:2 * i + 2, :].rearrange("p i n -> p (i n)"), bank[6 + i][:, :],
                              ACT.Copy)
                last.then_inc(S("pq_sb"), 1)
                act.wait_ge(S("sc_mm"), b + 1)
                for t in range(T):
                    last = af(sc[:, t, b * N:(b + 1) * N], bank[4 + t][:, :], ACT.Copy)
                last.then_inc(S("sc_sb"), 1)
            if stop < 7:
                return
            for t in range(T):
                def two_heads(i):
                    for half in range(2):
                        h = i * 2 + half + t * PH
                        act.wait_ge(S("choice"), h * LINKS + BEST)
                        af(pex[:, half, :], pbest[:, half, :], ACT.Exp, bias=pneg[:, half, :],
                           accum_out=psm[:, half, :]).then_inc(S("pexp"), 1)
                        act.wait_ge(S(f"dn_used{SLOTS - 1}"), h * 2 + 3)
                        af(pa[:, half, :], pa[:, half, :], ACT.Gelu).then_inc(S("gelu"), 1)
                        act.wait_ge(S("coef"), h + 1)
                        for e in range(TOPK):
                            act.wait_ge(S(f"up_used{(e - 4) % SLOTS}"),
                                        h * 2 + (e - 4) // SLOTS + 2)
                            af(diag[:, e % 4, :], ident[:, :], ACT.Copy, scale=pcoef[:, half, e:e + 1]) \
                                .then_inc(S("diag"), 1)
                with act.Fori(0, PH // 2) as i:
                    two_heads(i)
            for t in range(T):
                act.wait_ge(S("peer_done"), t + 1)
                for c in range(2):
                    last = af(at(t * D + c * N, N), bank[2 * t + c][:, :], ACT.Square,
                              accum_out=sqf[:, 2 * t + c:2 * t + c + 1])
                last.then_inc(S("sq_final"), 1)
            root("final", T, D)

        @block.vector
        def _(dve):
            v = nc.vector
            link = orderer(dve, "dve_order")

            def copy_banks(dst, tag, done, n=4, base=0):
                for i in range(n):
                    dve.wait_ge(S(tag), base + i + 1)
                    last = v.tensor_copy(dst[:, 2 * i:2 * i + 2, :].rearrange("p k n -> p (k n)"), bank[2 + i][:, :])
                last.then_inc(S(done), 1)

            def mod_sums(L, thirds=(0, 1, 2)):
                dve.wait_ge(S("acc_init"), (L + 1) * 16)
                if L == 0:
                    dve.wait_ge(S("cond"), 1)
                for third in thirds:
                    a = acc[:, third * D:(third + 1) * D]
                    for k in range(KC):
                        n = (L * 3 + third) * KC + k
                        if n:
                            dve.wait_ge(S("mod_sum"), n)
                        dve.wait_ge(S(f"mod_landed{k % 4}"), (n // 4 + 1) * 16)
                        v.scalar_tensor_tensor(out=a, in0=mring[:, k % 4, :], scalar=cond[:, k:k + 1], in1=a,
                                               op0=ALU.mult, op1=ALU.add).then_inc(S("mod_sum"), 1)

            def mod_columns(L):
                dve.wait_ge(S("mod_cols"), L + 1)
                v.tensor_copy(modc[:, L % 2, 0, :], bank[2][:, 0:KC])
                v.scalar_tensor_tensor(out=modc[:, L % 2, 1, :], in0=bank[2][:, KC:2 * KC], scalar=1.0,
                                       in1=cols[:, L * KC:(L + 1) * KC], op0=ALU.add, op1=ALU.mult) \
                    .then_inc(S("mod_cols_sb"), 1)

            def mod_gate(L):
                dve.wait_ge(S("mod_read"), L + 1)
                dve.wait_ge(S("gpost_in"), 16 * (L + 1))
                for i in range(2):
                    last = v.tensor_tensor(gateb[:, L % 2, i * N:(i + 1) * N], bank[3 + i][:, :],
                                           gpost[:, i * N:(i + 1) * N], ALU.mult)
                last.then_inc(S("mod_ready"), 1)

            def root(tag, n, width, scale=None):
                dve.wait_ge(S("ssq"), nth(tag))
                var, y, w = ssq[:, 0:n], rstd[:, 0:n], newton[:, 0:n]
                dve.wait_ge(S("root"), nth(tag))
                v.tensor_scalar(var, var, 1.0 / width, EPS, ALU.mult, ALU.add)
                link(v.tensor_tensor(w, y, y, ALU.mult))
                link(v.tensor_tensor(w, w, var, ALU.mult))
                link(v.tensor_scalar(w, w, -0.5, 1.5, ALU.mult, ALU.add))
                link(v.tensor_tensor(y, y, w, ALU.mult))
                if scale is not None:
                    link(v.tensor_scalar(rstd[:, 0:scale[0]], rstd[:, 0:scale[0]], scale[1], None, ALU.mult))

            def normalize(tag, done):
                root(tag, T, D)
                for t in range(T):
                    last = v.tensor_scalar(xn[:, t, :], x[:, t, :], rstd[:, t:t + 1], None, ALU.mult)
                last.then_inc(S(done), 1)

            def quads(first, count, mask, out_of):
                aqT, akT, aS, aPT = bufs(first)
                kd = DH + 2 if first < 4 else DH

                def k_in(n):
                    dve.wait_ge(S("att_T"), 2 * n + 2)
                    for i in range(2):
                        last = v.tensor_copy(akT[0:kd, 2 * i:2 * i + 2, :].rearrange("p h n -> p (h n)"),
                                             bank[3 + i][0:kd, :])
                    last.then_inc(S("att_kT"), 1)

                k_in(first)
                for i in range(count):
                    n, m, o = first + i, mask(i), out_of(i)
                    dve.wait_ge(S("att_s"), n + 1)
                    v.tensor_tensor(aS[:, :, 0:P], bank[5][:, :].rearrange("p (h n) -> p h n", h=4),
                                    amask[:, m, 0:P].unsqueeze(1).to_broadcast([P, 4, P]), ALU.add)
                    for j in range(2):
                        last = v.tensor_tensor(aS[:, 2 * j:2 * j + 2, P:3 * P],
                                               bank[6 + j][:, :].rearrange("p (h n) -> p h n", h=2),
                                               amask[:, m, P:3 * P].unsqueeze(1).to_broadcast([P, 2, 2 * P]), ALU.add)
                    link(last)
                    nm = anm[:, n, :].rearrange("p (h t) -> p h t", t=T)
                    v.tensor_reduce(nm[:, :, 0:1], aS[:, :, 0:P], X, ALU.max)
                    link(v.tensor_reduce(nm[:, :, 1:2], aS[:, :, P:3 * P], X, ALU.max))
                    v.tensor_scalar(anm[:, n, :], anm[:, n, :], -1.0, None, ALU.mult).then_inc(S("att_m"), 1)
                    dve.wait_ge(S("att_pt"), 3 * n + 2)
                    v.tensor_copy(aPT[:, 1, :, :].rearrange("p h n -> p (h n)"), bank[3][:, :]).then_inc(S("att_ptv"), 1)
                    if i + 1 < count:
                        k_in(n + 1)
                    dve.wait_ge(S("att_pv"), n + 1)
                    link(v.reciprocal(arl[:, :], al[:, n, :]))
                    pv_ = bank[5][:, :].rearrange("p (t h d) -> p t h d", t=T, h=4)
                    rl = arl[:, :].rearrange("p (h t) -> p t h", t=T)
                    for t in range(T):
                        last = v.tensor_tensor(o[:, t, :].rearrange("p (h d) -> p h d", h=4), pv_[:, t, :, :],
                                               rl[:, t, :].unsqueeze(2).to_broadcast([P, 4, DH]), ALU.mult)
                    last.then_inc(S("att_o"), 1)

            def gla(L):
                dve.wait_ge(S("low"), 3 if L else 1)
                v.tensor_copy(low[:, :, :].rearrange("p t n -> p (t n)"), bank[6][:, 0:T * RANK]) \
                    .then_inc(S("low_sb"), 1)
                dve.wait_ge(S("ones_set"), 1)
                if L + 1 < DEPTH:
                    mod_columns(L + 1)
                    mod_gate(L + 1)
                dve.wait_ge(S("lowT"), L // 3 + 1)
                v.tensor_copy(alT[0:RANK, :], bank[7][0:RANK, 0:T * P]).then_inc(S("alT"), 1)
                for b in (Q[0], Q[1], K[0], K[1], AT[:, 0, :], AT[:, 1, :]):
                    link(v.memset(b, 0.0), wait=False)
                dve.wait_ge(S("dve_order"), ORDER["dve_order"])
                bfl = b_.rearrange("p h n -> p (h n)")
                dve.wait_ge(S("lnd"), L // 3 + 1)
                for i in range(2):
                    link(v.scalar_tensor_tensor(out=bfl[:, i * N:(i + 1) * N], in0=bank[6 + i][:, :], scalar=0.0,
                                                in1=Dd[0][:, i * N:(i + 1) * N], op0=ALU.min, op1=ALU.subtract))
                link(v.tensor_scalar(bfl, bfl, 1.0 / 16.0, None, ALU.mult))
                for h in range(GH):
                    last = v.tensor_tensor_scan(b_[:, h, :], ones[:, 0:1].to_broadcast([P, T * P]), b_[:, h, :], 0.0,
                                                ALU.mult, ALU.add)
                last.then_inc(S("logd"), 1)
                dve.wait_ge(S("logd"), L // 3 + 1)
                dve.wait_ge(S("qkT_sb"), L // 3 + 1)

                def halves(a, lv):
                    return a.rearrange("p (n two l) -> p n two l", two=2, l=1 << (lv - 1))

                def exponents(lv):
                    if lv >= 3:
                        dve.wait_ge(S("lvl_qk"), L // 3 * (LEVELS + 1) + lv - 2)
                    size = 1 << (lv - 1)
                    n = GH * T * P // (2 * size)
                    bv, dv = halves(bfl, lv), halves(Dd[lv % 2], lv)
                    ref = bv[:, :, 0, size - 1:size].to_broadcast([P, n, size])
                    v.tensor_tensor(dv[:, :, 1, :], bv[:, :, 1, :], ref, ALU.subtract)
                    v.tensor_tensor(dv[:, :, 0, :], ref, bv[:, :, 0, :], ALU.subtract).then_inc(S("lvl_d"), 1)

                def decayed(lv):
                    dve.wait_ge(S("lvl_e"), L // 3 * (LEVELS + 1) + lv)
                    if lv >= 2:
                        dve.wait_ge(S("lvl"), L // 3 * (LEVELS + 2) + lv - 1)
                    e = halves(Dd[lv % 2], lv)
                    v.tensor_tensor(halves(Q[lv % 2], lv)[:, :, 1, :],
                                    halves(qT.rearrange("p h n -> p (h n)"), lv)[:, :, 1, :], e[:, :, 1, :], ALU.mult)
                    v.tensor_tensor(halves(K[lv % 2], lv)[:, :, 0, :],
                                    halves(kT.rearrange("p h n -> p (h n)"), lv)[:, :, 0, :], e[:, :, 0, :], ALU.mult) \
                        .then_inc(S("lvl_qk"), 1)

                def take(lv):
                    dve.wait_ge(S("lvl"), L // 3 * (LEVELS + 2) + lv + 1)
                    if lv:
                        dve.wait_ge(S("lvl_read"), L // 3 * (LEVELS + 1) + lv)
                    b0 = (6, 2)[lv % 2]
                    if lv <= LEVELS:
                        for t in range(T):
                            last = v.copy_predicated(AT[:, t, :].rearrange("p (h n) -> p h n", h=GH),
                                                     gmask[:, lv, :].unsqueeze(1).to_broadcast([P, GH, P]),
                                                     bank[b0 + t][:, :].rearrange("p (h n) -> p h n", h=GH))
                        last.then_inc(S("lvl_read"), 1)
                    else:
                        v.tensor_copy(AX.rearrange("p h n -> p (h n)"), bank[b0][:, :]).then_inc(S("attn_sb"), 1)

                dve.wait_ge(S("consts_in"), CONSTS * 16)
                exponents(1)
                for lv in range(1, LEVELS + 2):
                    if lv <= LEVELS:
                        exponents(lv + 1)
                    decayed(lv)
                    take(lv - 1)
                take(LEVELS + 1)
                root(f"head{L}", T * GH, DV)
                dve.wait_ge(S("ghead_in"), 16 if L == 0 else 32)
                og = at(W0 + 3 * D, T, D)
                for t in range(T):
                    for h in range(GH):
                        last = v.scalar_tensor_tensor(
                            out=og[:, t, h * DV:(h + 1) * DV], in0=bank[2 + 2 * t + h // 2][:, (h % 2) * DV:(h % 2 + 1) * DV],
                            scalar=rstd[:, t * GH + h:t * GH + h + 1], in1=ghead[:, h * DV:(h + 1) * DV],
                            op0=ALU.mult, op1=ALU.mult)
                link(last)
                dve.wait_ge(S("silu"), L + 1)
                z = g_in[:, :, 2 * D:3 * D]
                v.tensor_tensor(z, z, og, ALU.mult).then_inc(S("gated"), 1)
                if L == 0:
                    pass

            def sgu():
                mod_columns(2)
                mod_gate(2)
                dve.wait_ge(S("wsT"), 1)
                link(v.tensor_tensor(wsT, bank[2][:, :].rearrange("p (g n) -> p g n", g=SG),
                                     summ[:, :].unsqueeze(1).to_broadcast([P, SG, P]), ALU.mult), wait=False)
                root("ln", T, D)
                for t in range(T):
                    vt = g_in[:, t, D:2 * D]
                    link(v.scalar_tensor_tensor(out=vt, in0=vt, scalar=rstd[:, t:t + 1], in1=lng[:, :],
                                                op0=ALU.mult, op1=ALU.mult))
                    last = v.tensor_tensor(vt, vt, lnb[:, :], ALU.add)
                last.then_inc(S("ln_done"), 1)
                dve.wait_ge(S("mixed"), 1)
                dve.wait_ge(S("silu"), 2)
                su = at(W0 + 2 * D, T, D)
                for t in range(T):
                    for g in range(SG):
                        last = v.scalar_tensor_tensor(
                            out=su[:, t, g * 256:(g + 1) * 256], in0=bank[2 + 2 * t + g // 2][:, (g % 2) * 256:(g % 2 + 1) * 256],
                            scalar=bs[:, g:g + 1], in1=g_in[:, t, g * 256:(g + 1) * 256], op0=ALU.add, op1=ALU.mult)
                link(last)
                z = g_in[:, :, 2 * D:3 * D]
                v.tensor_tensor(z, z, su, ALU.mult).then_inc(S("gated"), 1)

            def fox():
                dve.wait_ge(S("sq_qk"), 1)
                v.tensor_reduce(ssq[:, 0:64], sqs.rearrange("p i (h d) -> p (i h) d", d=DH), X, ALU.add) \
                    .then_inc(S("ssq"), 1)
                dve.wait_ge(S("low"), 2)
                v.tensor_tensor(low[:, :, :], bank[6][:, 0:T * AH].rearrange("p (t n) -> p t n", t=T),
                                bf[:, :].unsqueeze(1).to_broadcast([P, T, AH]), ALU.add).then_inc(S("f_sb"), 1)
                mod_columns(3)
                mod_gate(3)
                dve.wait_ge(S("lnf"), 1)
                v.scalar_tensor_tensor(out=low2[:, :, :], in0=low[:, :, :], scalar=0.0, in1=low2[:, :, :],
                                       op0=ALU.min, op1=ALU.subtract).then_inc(S("logf"), 1)
                v.memset(qa[:, :, :, DH:DH + 1], 1.0)
                v.memset(ka[:, :, :, DH + 1:DH + 2], 1.0)
                dve.wait_ge(S("fsum"), 1)
                F = bank[7][:, 0:T * AH].rearrange("p (t h) -> p t h", t=T).unsqueeze(3)
                v.tensor_copy(qa[:, :, :, DH + 1:DH + 2], F)
                v.tensor_scalar(ka[:, :, :, DH:DH + 1], F, -1.0, None, ALU.mult)
                root("qk", 4 * AH, DH, scale=(2 * AH, DH ** -0.5))
                for i, dst in ((0, qa), (1, ka)):
                    for t in range(T):
                        src = f_in[:, t, i * D:(i + 1) * D].rearrange("p (h d) -> p h d", d=DH)
                        r = rstd[:, (i * T + t) * AH:(i * T + t + 1) * AH].unsqueeze(2).to_broadcast([P, AH, DH])
                        link(v.tensor_tensor(src, src, r, ALU.mult))
                        last = v.tensor_tensor(dst[:, t, :, 0:DH], src, gqk[:, i, :].unsqueeze(1).to_broadcast([P, AH, DH]),
                                               ALU.mult)
                last.then_inc(S("qka"), 1)
                quads(0, 4, lambda i: 0, lambda i: fo[:, :, i * 256:(i + 1) * 256])
                dve.wait_ge(S("att_o"), 4)
                dve.wait_ge(S("silu"), 3)
                v.tensor_tensor(fo, fo, f_in[:, :, 3 * D:4 * D], ALU.mult).then_inc(S("gated"), 1)

            for t in range(T):
                v.memset(bank[t][:, 0:1], 0.0).then_inc(S(f"evac{t}"), 1)
            dve.wait_ge(S("colsT"), 1)
            v.tensor_copy(cols[:, :], bank[7][:, 0:64]).then_inc(S("colsT_sb"), 1)
            dve.wait_ge(S("colsT_sb"), 1)
            mod_sums(0, (0, 1))
            mod_columns(0)
            for L in range(DEPTH):
                if stop < L + 1:
                    return
                normalize(f"norm{L}", "xn")
                dve.wait_ge(S("mod_cols_sb"), L + 1)
                for k in range(KC):
                    dve.wait_ge(S("xT"), 4 * L + k // 2 + 1)
                    last = v.tensor_scalar(hT[:, k, :], bank[2 + k // 2][:, (k % 2) * 256:(k % 2 + 1) * 256],
                                           modc[:, L % 2, 1, k:k + 1], modc[:, L % 2, 0, k:k + 1], ALU.mult, ALU.add)
                last.then_inc(S("hT"), 1)
                if L == 0:
                    mod_sums(0, (2,))
                    mod_gate(0)
                if L + 1 < DEPTH:
                    mod_sums(L + 1)
                if L in (0, 3):
                    gla(L)
                elif L == 1:
                    sgu()
                else:
                    fox()
                copy_banks(hT, "gT", "ghT", base=4 * L)
                root(f"post{L}", T, D)
                for t in range(T):
                    link(v.scalar_tensor_tensor(out=ob[:, t, :], in0=ob[:, t, :], scalar=rstd[:, t:t + 1],
                                                in1=gateb[:, L % 2, :], op0=ALU.mult, op1=ALU.mult))
                v.tensor_tensor(x[:, :, :], x[:, :, :], ob, ALU.add).then_inc(S("x_ready"), 1)
                dve.wait_ge(S("x_ready"), L + 1)
            if stop < 5:
                return
            link(v.tensor_copy(posf[:, :], posi[:, :]))
            ang = acc[:, 0:16].rearrange("p (t r) -> p t r", t=T)
            for t in range(T):
                link(v.tensor_scalar(ang[:, t, :], freq[:, :], posf[:, t:t + 1], None, ALU.mult))
            for i, (turn, shift) in enumerate(((0.25, np.pi / 2), (0.0, 0.0))):
                a, r, n = acc[:, 0:16], trig[:, i, :], acc[:, 32:48]
                link(v.tensor_scalar(n, a, float(1 / (2 * np.pi)), turn, ALU.mult, ALU.add))
                link(v.tensor_scalar(n, n, MAGIC, None, ALU.add))
                link(v.tensor_scalar(n, n, MAGIC, None, ALU.subtract))
                link(v.scalar_tensor_tensor(out=r, in0=n, scalar=-TWO_PI[0], in1=a, op0=ALU.mult, op1=ALU.add))
                for c in TWO_PI[1:]:
                    link(v.scalar_tensor_tensor(out=r, in0=n, scalar=-c, in1=r, op0=ALU.mult, op1=ALU.add))
                link(v.tensor_scalar(r, r, float(shift), None, ALU.add))
                link(v.tensor_scalar(r, r, PI_SAFE, -PI_SAFE, ALU.min, ALU.max), wait=False)
            dve.wait_ge(S("dve_order"), ORDER["dve_order"])
            v.memset(acc[:, 64:65], 0.0).then_inc(S("angles"), 1)
            normalize("mix", "xn")
            for k in range(KC):
                dve.wait_ge(S("xT"), 4 * DEPTH + k // 2 + 1)
                last = v.tensor_scalar(hT[:, k, :], bank[2 + k // 2][:, (k % 2) * 256:(k % 2 + 1) * 256],
                                       cols[:, 32 + k:33 + k], None, ALU.mult)
            last.then_inc(S("hT"), 1)
            for t in range(T):
                dve.wait_ge(S(f"evac{t}"), BLOCKS["qkv"] + 7)
            dve.wait_ge(S("trig"), 1)
            HB = 2 * NG * GHD
            for t in range(T):
                qk = hb[:, t, 0:HB * DH].rearrange("p (h d) -> p h d", d=DH)
                t1, t2 = qk[:, :, 0:ROT], qk[:, :, ROT:2 * ROT]
                cs = trig[:, 0, t * ROT:(t + 1) * ROT].unsqueeze(1).to_broadcast([P, HB, ROT])
                sn = trig[:, 1, t * ROT:(t + 1) * ROT].unsqueeze(1).to_broadcast([P, HB, ROT])
                tmp = [acc[:, t * 1536 + i * 384:t * 1536 + (i + 1) * 384].rearrange("p (h r) -> p h r", r=ROT) for i in range(4)]
                for o, a, b in ((tmp[0], t1, cs), (tmp[1], t2, sn), (tmp[2], t2, cs), (tmp[3], t1, sn)):
                    last = v.tensor_tensor(o, a, b, ALU.mult)
                link(last)
                v.tensor_tensor(t1, tmp[0], tmp[1], ALU.subtract)
                last = v.tensor_tensor(t2, tmp[2], tmp[3], ALU.add)
            link(last)
            v.tensor_scalar(hb[:, :, 0:1536], hb[:, :, 0:1536], DH ** -0.5, None, ALU.mult).then_inc(S("rotated"), 1)
            quads(4, 6, lambda i: 1 + i // 2, lambda i: od[:, :, i // 2, (i % 2) * 256:(i % 2 + 1) * 256])
            for t in range(T):
                dve.wait_ge(S(f"evac{t}"), BLOCKS["gates"] + 1)
            v.tensor_tensor(ha[:, :, D:2 * D], ha[:, :, D:2 * D], ha[:, :, 2 * D:3 * D], ALU.mult) \
                .then_inc(S("z_conv"), 1)
            dve.wait_ge(S("att_o"), 10)
            v.memset(lsm[:, :], 0.0).then_inc(S("lse_in"), 1)
            dve.wait_ge(S("lse_ln"), 1)
            l0, l1 = lse[:, 0, :], lse[:, 1, :]
            link(v.tensor_tensor(l1, l0, anm[:, 4:10, :].rearrange("p n h -> p (n h)"), ALU.subtract))
            link(v.tensor_tensor(lsm[:, :], l1[:, 0:16], l1[:, 16:32], ALU.max))
            link(v.tensor_tensor(lsm[:, :], lsm[:, :], l1[:, 32:48], ALU.max))
            l3 = l1.rearrange("p (g h) -> p g h", g=NG)
            v.tensor_tensor(l3, l3, lsm[:, :].unsqueeze(1).to_broadcast([P, NG, 16]), ALU.subtract) \
                .then_inc(S("lse_m"), 1)
            dve.wait_ge(S("lse_e"), 1)
            link(v.tensor_tensor(lsm[:, :], l0[:, 0:16], l0[:, 16:32], ALU.add))
            link(v.tensor_tensor(lsm[:, :], lsm[:, :], l0[:, 32:48], ALU.add))
            link(v.reciprocal(lsm[:, :], lsm[:, :]))
            link(v.tensor_tensor(l3, l0.rearrange("p (g h) -> p g h", g=NG),
                                 lsm[:, :].unsqueeze(1).to_broadcast([P, NG, 16]), ALU.mult))
            for t in range(T):
                w = l1.rearrange("p (h t) -> p t h", t=T)[:, t, :].unsqueeze(2).to_broadcast([P, NG * GHD, DH])
                o = od[:, t, :, :].rearrange("p g (h d) -> p (g h) d", d=DH)
                last = v.tensor_tensor(o, o, w, ALU.mult)
            link(last)
            link(v.tensor_tensor(od[:, :, 0, :], od[:, :, 0, :], od[:, :, 1, :], ALU.add))
            v.tensor_tensor(od[:, :, 0, :], od[:, :, 0, :], od[:, :, 2, :], ALU.add).then_inc(S("att_merged"), 1)
            v.memset(zT[:, :, 0:2], 0.0)
            for i in range(4):
                dve.wait_ge(S("zT"), i + 1)
                last = v.tensor_copy(zT[:, 2 * i:2 * i + 2, 2:258], bank[2 + i][:, :].rearrange("p (k n) -> p k n", k=2))
            last.then_inc(S("zT_sb"), 1)
            dve.wait_ge(S("zT_sb"), 1)
            for i in range(3):
                for k in range(KC):
                    w = cols[:, 40 + i * KC + k:41 + i * KC + k]
                    if i == 0:
                        last = v.tensor_scalar(cT[:, k, :], zT[:, k, 0:256], w, None, ALU.mult)
                    else:
                        last = v.scalar_tensor_tensor(out=cT[:, k, :], in0=zT[:, k, i:i + 256], scalar=w,
                                                      in1=cT[:, k, :], op0=ALU.mult, op1=ALU.add)
                link(last)
            for t in range(T):
                dve.wait_ge(S(f"evac{t}"), BLOCKS["gates"] + 5)
            for t in range(T):
                last = v.tensor_tensor(hb[:, t, GC:GC + 2 * D], hb[:, t, GC:GC + 2 * D],
                                       gbias[:, :, :].rearrange("p a d -> p (a d)"), ALU.add)
            last.then_inc(S("gates_in"), 1)
            for i in range(4):
                dve.wait_ge(S("bT"), i + 1)
                last = v.tensor_tensor(hT[:, 2 * i:2 * i + 2, :].rearrange("p k n -> p (k n)"),
                                       cT[:, 2 * i:2 * i + 2, :].rearrange("p k n -> p (k n)"), bank[2 + i][:, :], ALU.mult)
            last.then_inc(S("conv_hT"), 1)
            copy_banks(hT, "oT", "oT_sb", n=2)
            for t in range(T):
                dve.wait_ge(S(f"evac{t}"), BLOCKS["attn"] + 2)
            dve.wait_ge(S("gates"), 1)
            v.tensor_tensor(ha[:, :, 0:D], ha[:, :, 0:D], hb[:, :, GC:GC + D], ALU.mult)
            link(v.tensor_tensor(ha[:, :, D:2 * D], ha[:, :, D:2 * D], hb[:, :, GA:GA + D], ALU.mult))
            v.tensor_tensor(ha[:, :, 0:D], ha[:, :, 0:D], ha[:, :, D:2 * D], ALU.add).then_inc(S("merged"), 1)
            copy_banks(hT, "mT", "mT_sb")
            for t in range(T):
                dve.wait_ge(S(f"evac{t}"), BLOCKS["hyb_out"] + 3)
            v.tensor_tensor(x[:, :, :], x[:, :, :], ha[:, :, 2 * D:3 * D], ALU.add).then_inc(S("x_ready"), 1)
            if stop < 6:
                return
            root("ffn", T, D)
            dve.wait_ge(S("last_rows_in"), 32)
            for t in range(T):
                last = v.scalar_tensor_tensor(out=u[:, t, :], in0=x[:, t, :], scalar=rstd[:, t:t + 1], in1=nffn[:, :],
                                              op0=ALU.mult, op1=ALU.mult)
            last.then_inc(S("u_ready"), 1)
            copy_banks(hT, "uT", "uT_sb")
            if stop < 7:
                return
            link(v.memset(zero, 0.0), wait=False)

            def best16(vals, pos, src, src2, put):
                dve.nop(nofuse=True)
                for w in range(len(src)):
                    last = v.max(vals[w][:, 0:8], src[w])
                put(last)
                dve.nop(nofuse=True)
                for w in range(len(src)):
                    v.max_index(pos[w][:, 0:8], vals[w][:, 0:8], src[w])
                    last = v.match_replace(src2[w], vals[w][:, 0:8], src[w], -3.0e38)
                put(last)
                dve.nop(nofuse=True)
                for w in range(len(src)):
                    last = v.max(vals[w][:, 8:16], src2[w])
                put(last)
                dve.nop(nofuse=True)
                for w in range(len(src)):
                    last = v.max_index(pos[w][:, 8:16], vals[w][:, 8:16], src2[w])
                put(last)

            def choose(h, par):
                n = [0]

                def put(ins):
                    n[0] += 1
                    ins.then_inc(S("choice"), 1)
                    dve.wait_ge(S("choice"), h * LINKS + n[0])

                put(v.tensor_copy(pk, sc.rearrange("p t n -> p (t n)")[:, ds(h * 256, 256)]))
                best16([pv[:, c, :] for c in range(2)], [pix[:, c, :] for c in range(2)],
                       [pk[:, c * P:(c + 1) * P] for c in range(2)], [pk2[:, c * P:(c + 1) * P] for c in range(2)], put)
                v.tensor_copy(pixf[:, :, :], pix[:, :, :])
                put(v.tensor_tensor(cand, pv[:, 0, :].unsqueeze(2).to_broadcast([P, TOPK, TOPK]),
                                    pv[:, 1, :].unsqueeze(1).to_broadcast([P, TOPK, TOPK]), ALU.add))
                best16([pbest[:, par, :]], [ppos[:, :]], [cand.rearrange("p a b -> p (a b)")], [cand2], put)
                put(v.tensor_scalar(pneg[:, par, :], pbest[:, par, 0:1], -1.0, None, ALU.mult))
                assert n[0] == BEST
                v.tensor_single_scalar(pab[:, 0, :], ppos[:, :], 4, ALU.logical_shift_right)
                put(v.tensor_single_scalar(pab[:, 1, :], ppos[:, :], 15, ALU.bitwise_and))
                put(v.tensor_copy(pabf[:, :, :], pab[:, :, :]))
                for c in range(2):
                    put(v.tensor_tensor(hot[:, c, :, :], iota[:, :].unsqueeze(1).to_broadcast([P, TOPK, TOPK]),
                                        pabf[:, c, :].unsqueeze(2).to_broadcast([P, TOPK, TOPK]), ALU.is_equal))
                for c in range(2):
                    put(v.tensor_tensor(hot[:, c, :, :], hot[:, c, :, :],
                                        pixf[:, c, :].unsqueeze(1).to_broadcast([P, TOPK, TOPK]), ALU.mult))
                for c in range(2):
                    put(v.tensor_reduce(psel[:, c, :], hot[:, c, :, :], X, ALU.add))
                put(v.scalar_tensor_tensor(out=pidf[:, :], in0=psel[:, 0, :], scalar=float(NK), in1=psel[:, 1, :],
                                           op0=ALU.mult, op1=ALU.add))
                assert n[0] == LINKS, n[0]

            def dots(h, par, t):
                for e in range(TOPK):
                    s = e % SLOTS
                    dve.wait_ge(S(f"dn_landed{s}"), (h * 2 + e // SLOTS + 1) * 16)
                    v.tensor_tensor_reduce(out=dn[s], in0=dn[s], in1=u[:, t, :], scale=1.0, scalar=0.0,
                                           op0=ALU.mult, op1=ALU.add, accum_out=pa[:, par, e:e + 1]) \
                        .then_inc(S(f"dn_used{s}"), 1)

            def weights(h, par):
                dve.wait_ge(S("pexp"), h + 1)
                v.reciprocal(psm[:, par, :], psm[:, par, :]).then_inc(S("coef_step"), 1)
                dve.wait_ge(S("gelu"), h + 1)
                dve.wait_ge(S("coef_step"), h + 1)
                v.scalar_tensor_tensor(out=pcoef[:, par, :], in0=pa[:, par, :], scalar=psm[:, par, :],
                                       in1=pex[:, par, :], op0=ALU.mult, op1=ALU.mult).then_inc(S("coef"), 1)

            def pick_dn(par):
                v.tensor_copy(idx[:, par, :], pidf[:, :]).then_inc(S("dn_picks"), 1)

            def pick_up(h, par):
                dve.wait_ge(S("dn_picks"), h + 1)
                v.tensor_copy(idxu[:, par, :], idx[:, par, :]).then_inc(S("up_picks"), 1)

            for s in range(SLOTS):
                v.memset(dn[s][:, 0:1], 0.0).then_inc(S(f"dn_used{s}"), 1)
            dve.wait_ge(S("sc_sb"), 1)
            for h in range(2):
                choose(h, h)
                pick_dn(h)
            pick_up(0, 0)
            dots(0, 0, 0)
            dve.wait_ge(S("sc_sb"), 4)
            for s in range(SLOTS):
                v.memset(up[:, s, 0:1], 0.0).then_inc(S(f"up_used{s}"), 1)
            for t in range(T):
                def two_heads(h, cross=False):
                    final = cross and t == T - 1
                    for half in range(2):
                        if not (final and half):
                            dots(h + half + 1, 1 - half, t + (cross and half))
                        weights(h + half, half)
                        if not final:
                            choose(h + half + 2, half)
                            pick_dn(half)
                        if not (final and half):
                            dve.wait_ge(S(f"up_used{SLOTS - 1}"), (h + half) * 2 + 1)
                            pick_up(h + half + 1, 1 - half)
                with dve.Fori(0, PH // 2 - 1) as i:
                    two_heads(i * 2 + t * PH)
                two_heads((t + 1) * PH - 2, cross=True)
            for t in range(T):
                dve.wait_ge(S("sq_final"), t + 1)
                last = v.tensor_tensor(ssq[:, t:t + 1], sqf[:, 2 * t:2 * t + 1], sqf[:, 2 * t + 1:2 * t + 2], ALU.add)
            last.then_inc(S("ssq"), 1)
            root("final", T, D)
            for t in range(T):
                for c in range(2):
                    last = v.scalar_tensor_tensor(out=at(t * D + c * N, N), in0=bank[2 * t + c][:, :],
                                                  scalar=rstd[:, t:t + 1], in1=fin[:, c * N:(c + 1) * N],
                                                  op0=ALU.mult, op1=ALU.mult)
                last.then_inc(S("out_ready"), 1)


_INS = ["x", "c", "norm_pre_g", "norm_post_g", "w_mod", "b_mod", "gla_w_in", "gla_w_a2", "gla_b_a",
        "gla_g_head", "gla_w_out", "sgu_w_in", "sgu_ln_g", "sgu_ln_b", "sgu_w_s", "sgu_b_s",
        "sgu_w_out", "fox_w_in", "fox_b_f", "fox_g_q", "fox_g_k", "fox_w_out", "positions_2",
        "norm_mix_2", "w_in_2", "conv_w_2", "w_conv_out_2", "w_attn_out_2", "gate_bias_2", "w_out_2",
        "norm_ffn_2", "peer_w_query_2", "peer_sub_keys_2", "peer_down_2", "peer_up_2", "final_norm_2"]


def kernel(**inputs):
    import concourse.bacc as bacc
    from concourse.bass_utils import run_bass_kernel_spmd

    nc = bacc.Bacc("TRN2", target_bir_lowering=False, num_devices=1)
    data = {name: np.ascontiguousarray(inputs[name]) for name in _INS}
    data.update(constants())
    arrays, views = {}, {}
    for name, a in data.items():
        arrays[f"in_{name}"] = a
        views[name] = nc.dram_tensor(f"in_{name}", a.shape, mybir.dt.from_np(a.dtype), kind="ExternalInput").ap()
    out = nc.dram_tensor("out_0", (1, T * P, D), F32, kind="ExternalOutput").ap()
    build(nc, views, out)
    r = run_bass_kernel_spmd(nc, [arrays], core_ids=[0])
    return r.results[0]["out_0"]
```

```python
from contextlib import ExitStack

import numpy as np
import concourse.bass as bass
from concourse import mybir

F32 = mybir.dt.float32
I32 = mybir.dt.int32
U32 = mybir.dt.uint32
ALU = mybir.AluOpType
ACT = mybir.ActivationFunctionType
X = mybir.AxisListType.X
ds = bass.ds

P = 128
T = 2
D = 1024
KC = D // P
N = 512
EPS = 1e-6
DEPTH = 4
GH, DK, DV = 4, 128, 256
RANK = 16
LEVELS = 7
SG = 4
AH, DH = 16, 64
NG, GHD = 3, 8
ROT = 8
PH, TOPK, NK = 8, 16, 128
SLOTS = 8
MAGIC = 1.5 * 2.0 ** 23
TWO_PI = (6.28125, 1.9340515136718750e-3, 1.2556659146e-6)
PI_SAFE = 3.1415925

BLOCKS = {}
_at = 0
for _name, _n in (("in0", 6), ("out0", 2), ("in1", 6), ("out1", 2), ("in2", 8), ("out2", 2),
                  ("in3", 6), ("out3", 2), ("qkv", 9), ("conv_in", 6), ("gates", 4), ("attn", 1),
                  ("conv", 2), ("hyb_out", 2), ("query", 4)):
    BLOCKS[_name] = _at
    _at += _n


CONV_COLS = [D, 2 * D, D + N, 2 * D + N, 0, N]
GATE_COLS = [3 * D + 4608 + i * N for i in range(4)]


def constants():
    i = np.arange(P)
    row, col = i[:, None], i[None, :]
    ident = np.eye(P, dtype=np.float32)
    sum_mask = (row <= col).astype(np.float32)
    gla = np.zeros((P, LEVELS + 1, P), np.int32)
    gla[:, 0] = row == col
    for l in range(LEVELS):
        size = 1 << l
        same = row // (2 * size) == col // (2 * size)
        gla[:, l + 1] = same & (row // size % 2 == 0) & (col // size % 2 == 1)
    att = np.zeros((P, 4, 2, P), np.float32)
    for n, (steps, dil) in enumerate(((10 ** 6, 1), (128, 1), (128, 4), (128, 16))):
        own, back = row - col, row + P - col
        for part, dist in enumerate((back, own)):
            ok = (dist >= 0) & (dist <= steps * dil) & (dist % dil == 0)
            att[:, n, part] = np.where(ok, 0.0, -1e30)
    inv = (np.float32(500000.0) ** (-np.arange(ROT, dtype=np.float32) * np.float32(2.0 / 16)))
    return {
        "k_ident": ident, "k_sum": sum_mask, "k_gla": gla, "k_att": att.reshape(P, 4 * 2 * P),
        "k_freq": inv.astype(np.float32).reshape(1, ROT),
        "k_iota": np.arange(TOPK, dtype=np.float32).reshape(1, TOPK),
    }


def build(nc, A, out, stop=99):
    with ExitStack() as ctx:
        def sb(name, shape, dt=F32):
            return ctx.enter_context(nc.sbuf_tensor(name, shape, dt))

        sems = {}

        def S(name):
            if name not in sems:
                sems[name] = ctx.enter_context(nc.semaphore(name))
            return sems[name]

        ring = sb("ring", [P, 2, KC * N])
        mring = sb("mring", [P, 4, D])
        acc = sb("acc", [P, 3 * D])
        x = sb("x", [P, T, D])
        hT = sb("hT", [P, KC, T * P])
        gateb = sb("gateb", [P, 2, D])
        gpost = sb("gpost", [P, D])
        ghead = sb("ghead", [P, D])
        lng = sb("lng", [P, D])
        lnb = sb("lnb", [P, D])
        gbias = sb("gbias", [P, 2, D])
        nffn, fin = lng, lnb
        big = sb("big", [P, 19584])
        ident = sb("ident", [P, P])
        ones = sb("ones", [P, P])
        summ = sb("summ", [P, P])
        gmask = sb("gmask", [P, LEVELS + 1, P], I32)
        amask = sb("amask", [P, 4, 2 * P])
        rows = sb("rows", [64, P])
        cols = sb("cols", [P, 64])
        cond = sb("cond", [P, KC])
        modc = sb("modc", [P, 2, 2, KC])
        wlow = sb("wlow", [P, 3, KC, RANK])
        wa2 = sb("wa2", [RANK + 1, 2, GH * DK])
        alT = sb("alT", [RANK + 1, T * P])
        low = sb("low", [P, T, RANK])
        low2 = sb("low2", [P, T, RANK])
        bs = sb("bs", [P, SG])
        bf = sb("bf", [P, AH])
        gqk = sb("gqk", [P, 2, DH])
        freq = sb("freq", [P, ROT])
        iota = sb("iota", [P, TOPK])
        posi = sb("posi", [P, T], I32)
        posf = sb("posf", [P, T])
        ssq = sb("ssq", [P, 104])
        var = sb("var", [P, 104])
        rstd = sb("rstd", [P, 104])
        newton = sb("newton", [P, 104])
        half_ssq = sb("half_ssq", [P, T * DEPTH])
        small = sb("small", [P, 8])
        trig = sb("trig", [P, 2, T * ROT])
        anm = sb("anm", [P, 10, 8])
        al = sb("al", [P, 10, 8])
        arl = sb("arl", [P, 8])
        lse = sb("lse", [P, 2, NG * 16])
        lsm = sb("lsm", [P, 16])
        pv = sb("pv", [P, 2, TOPK])
        pix = sb("pix", [P, 2, TOPK], U32)
        pixf = sb("pixf", [P, 2, TOPK])
        pbest = sb("pbest", [P, 2, TOPK])
        pneg = sb("pneg", [P, 2, 1])
        ppos = sb("ppos", [P, TOPK], U32)
        pab = sb("pab", [P, 2, TOPK], U32)
        pabf = sb("pabf", [P, 2, TOPK])
        psel = sb("psel", [P, 2, TOPK])
        pidf = sb("pidf", [P, TOPK])
        idx = sb("idx", [P, 2, TOPK], U32)
        idxu = sb("idxu", [P, 2, TOPK], U32)

        pex = gpost[:, 0:32].rearrange("p (a b) -> p a b", a=2)
        pa = gpost[:, 32:64].rearrange("p (a b) -> p a b", a=2)
        pcoef = gpost[:, 64:96].rearrange("p (a b) -> p a b", a=2)
        psm = gpost[:, 96:98].rearrange("p (a b) -> p a b", a=2)
        sqf = gpost[:, 100:100 + 2 * T]

        bank = [ctx.enter_context(nc.psum_tensor(f"bank{i}", [P, N], F32)) for i in range(8)]

        def at(off, *shape):
            size = int(np.prod(shape))
            v = big[:, off:off + size]
            if len(shape) == 2:
                return v.rearrange("p (a b) -> p a b", b=shape[1])
            if len(shape) == 3:
                return v.rearrange("p (a b c) -> p a b c", b=shape[1], c=shape[2])
            if len(shape) == 4:
                return v.rearrange("p (a b c d) -> p a b c d", b=shape[1], c=shape[2], d=shape[3])
            return v

        ob = at(0, T, D)
        xn = at(2 * D, T, D)
        g_in = at(0, T, 3 * D)
        W0 = 6 * D
        b_ = at(W0, GH, T * P)
        qT = at(W0 + D, GH, T * P)
        kT = at(W0 + 2 * D, GH, T * P)
        Q = [at(W0 + 3 * D + i * D, GH * T * P) for i in (0, 1)]
        K = [at(W0 + 5 * D + i * D, GH * T * P) for i in (0, 1)]
        Dd = [at(W0 + 7 * D + i * D, GH * T * P) for i in (0, 1)]
        AT = at(W0 + 9 * D, T, GH * P)
        AX = at(W0 + 10 * D, GH, P)
        ws = at(W0, SG, P)
        wsT = at(W0 + N, SG, P)
        f_in = at(0, T, 4 * D)
        qa = at(8 * D, T, AH, DH + 2)
        ka = at(8 * D + T * AH * (DH + 2), T, AH, DH + 2)
        WF = 8 * D + 2 * T * AH * (DH + 2)
        fo = at(WF + 5 * D, T, D)
        sqs = at(WF, 2, T * D)
        ha = at(0, T, 3 * D)
        hb = at(6 * D, T, 6656)
        QO, KO, VO, GC, GA = 0, 1536, 3072, 4608, 5632
        mflat = mring[:, :, :].rearrange("p a n -> p (a n)")
        zT = mflat[:, 0:KC * 258].rearrange("p (k n) -> p k n", n=258)
        cT = gateb[:, :, :].rearrange("p a (k n) -> p (a k) n", n=T * P)
        od = acc[:, :].rearrange("p (t g n) -> p t g n", t=T, g=NG)
        fox_bufs = (at(WF, 4, T * P), at(WF + D, 4, T * P), at(WF + 2 * D, 4, 3 * P),
                    at(WF + 2 * D + 12 * P, 3, 4, P))
        hyb_bufs = (mflat[:, 0:D].rearrange("p (h n) -> p h n", h=4),
                    mflat[:, D:2 * D].rearrange("p (h n) -> p h n", h=4),
                    gateb[:, :, :].rearrange("p a n -> p (a n)")[:, 0:12 * P].rearrange("p (h n) -> p h n", h=4),
                    mflat[:, 2 * D:2 * D + 12 * P].rearrange("p (b h n) -> p b h n", b=3, h=4))

        def bufs(n):
            return fox_bufs if n < 4 else hyb_bufs
        pk = at(2 * D, 2 * P)
        pk2 = at(2 * D + 256, 2 * P)
        cand = at(2 * D + 512, TOPK, TOPK)
        cand2 = at(2 * D + 768, TOPK * TOPK)
        hot = at(3 * D, 2, TOPK, TOPK)
        diag = ghead[:, 0:4 * P].rearrange("p (s n) -> p s n", n=P)
        zero = ghead[:, 4 * P:5 * P]
        u = at(4 * D, T, D)
        up = at(6 * D, SLOTS, D)
        qq = at(6 * D, 2, T, N)
        pqT = at(8 * D, 2, 4, T * P)
        skT = at(10 * D, 2 * PH, P)
        skr = at(12 * D, 2 * PH, P)
        sc = at(14 * D, T, 2 * D)
        dn = [mring[:, i, :] for i in range(4)] + [acc[:, i * D:(i + 1) * D] for i in range(3)] + [gateb[:, 0, :]]

        block = ctx.enter_context(nc.Block())

        CONSTS = 10 + SG + T + 2
        LINKS, BEST = 20, 11
        ORDER = {}

        def orderer(eng, name):
            ORDER[name] = 0

            def link(ins, wait=True):
                ORDER[name] += 1
                ins.then_inc(S(name), 1)
                if wait:
                    eng.wait_ge(S(name), ORDER[name])
            return link

        NORMS = ["norm0.0", "norm0.1"]
        for L in range(DEPTH):
            NORMS += {1: ["ln"], 2: ["qk.0", "qk.1"]}.get(L, [f"head{L}.0", f"head{L}.1"])
            NORMS += [f"post{L}.0", f"norm{L + 1}.0", f"post{L}.1", f"norm{L + 1}.1"]
        NORMS += ["ffn.0", "ffn.1", "final"]
        COL = {"qk.0": 0, "qk.1": 2 * AH, "ln": 0, "final": 0}
        for n, tag in enumerate(tag for tag in NORMS if tag[:4] in ("norm", "post", "ffn.")):
            COL[tag] = 64 + n
        for n in range(4):
            COL[f"head{n // 2 * 3}.{n % 2}"] = 88 + 4 * n
        PIECES = DEPTH * 3 * KC
        ON_DVE = 3 * KC + 12
        trash = at(4 * D, T, D)

        def nth(tag):
            return NORMS.index(tag) + 1

        @block.sync
        def _(sp):
            def load(dst, src, sem):
                sp.dma_start(dst, src).then_inc(S(sem), 16)

            load(rows[0:32, :], A["norm_pre_g"].rearrange("l (k p) -> (l k) p", p=P), "rows_in")
            load(rows[32:40, :], A["norm_mix_2"].rearrange("l (k p) -> (l k) p", p=P), "rows_in")
            load(rows[40:64, :], A["conv_w_2"][0].rearrange("i (k p) -> (i k) p", p=P), "rows_in")
            load(cond[:, :], A["c"].rearrange("b (p k) -> (b p) k", k=KC), "cond_in")
            load(ident[:, :], A["k_ident"], "rows_in")
            load(x[:, :, :], A["x"][0].rearrange("(t p) d -> p t d", p=P), "x_in")

            def src_of(w, col):
                return w.rearrange("(k p) n -> p k n", p=P)[:, :, ds(col, N)]

            def put(slot, src):
                sp.dma_start(ring[:, slot, :].rearrange("p (k n) -> p k n", n=src.shape[2]), src) \
                    .then_inc(S(f"w_landed{slot}"), 16)

            def stream(name, n, w):
                b0 = BLOCKS[name]
                start = 1 if b0 == 0 else 0

                def pair(i):
                    for slot in range(2):
                        sp.wait_ge(S("proj_done1"), b0 + 2 * i + slot - 1)
                        put(slot, src_of(w, i * (2 * N) + slot * N))

                if n // 2 - start > 1:
                    with sp.Fori(start, n // 2) as i:
                        pair(i)
                elif n // 2 - start == 1:
                    pair(start)

            def one(b, src):
                sp.wait_ge(S("proj_done1"), b - 1)
                put(b % 2, src)

            for i in range(2):
                sp.wait_ge(S(f"mod_landed{2 * i}"), 4 * 16)
                put(i, src_of(A["gla_w_in"][0], i * N))
            for n, (name, w, c0) in enumerate((("gla_w_in", 0, 3072), ("gla_w_in", 1, 3072),
                                               ("fox_w_in", 0, 4096))):
                load(wlow[:, n, :, :], A[name][w].rearrange("(k p) n -> p k n", p=P)[:, :, c0:c0 + RANK],
                     "wlow_in")
            for j in range(2):
                load(wa2[0:RANK, j, :], A["gla_w_a2"][j], "wlow_in")
                load(wa2[RANK:RANK + 1, j, :], A["gla_b_a"][j:j + 1, :], "wlow_in")
            load(gmask[:, :, :], A["k_gla"], "consts_in")
            load(summ[:, :], A["k_sum"], "consts_in")
            load(amask[:, :, :], A["k_att"].rearrange("p (a b) -> p a b", a=4), "consts_in")
            load(ghead[:, :], A["gla_g_head"][0:1].rearrange("a h v -> a (h v)").to_broadcast([P, D]), "ghead_in")
            load(lng[:, :], A["sgu_ln_g"].to_broadcast([P, D]), "consts_in")
            load(lnb[:, :], A["sgu_ln_b"].to_broadcast([P, D]), "consts_in")
            load(gqk[:, 0, :], A["fox_g_q"].to_broadcast([P, DH]), "consts_in")
            load(gqk[:, 1, :], A["fox_g_k"].to_broadcast([P, DH]), "consts_in")
            load(bf[:, :], A["fox_b_f"].to_broadcast([P, AH]), "consts_in")
            load(freq[:, :], A["k_freq"].to_broadcast([P, ROT]), "consts_in")
            load(iota[:, :], A["k_iota"].to_broadcast([P, TOPK]), "consts_in")
            for g in range(SG):
                load(bs[:, g:g + 1], A["sgu_b_s"][0, g:g + 1, :].rearrange("a p -> p a"), "consts_in")
            for t in range(T):
                load(posi[:, t:t + 1], A["positions_2"][:, t * P:(t + 1) * P].rearrange("a p -> p a"),
                     "consts_in")
            for i in range(2):
                load(gbias[:, i, :], A["gate_bias_2"][0, i:i + 1, :].to_broadcast([P, D]), "consts_in")
            if stop < 1:
                return
            stream("in0", 6, A["gla_w_in"][0])
            stream("out0", 2, A["gla_w_out"][0])
            if stop < 2:
                return
            stream("in1", 6, A["sgu_w_in"][0])
            sp.wait_ge(S("x_ready"), T)
            load(ws, A["sgu_w_s"][0].rearrange("g t s -> t g s"), "ws_in")
            stream("out1", 2, A["sgu_w_out"][0])
            if stop < 3:
                return
            stream("in2", 8, A["fox_w_in"][0])
            sp.wait_ge(S("x_ready"), 2 * T)
            load(nffn[:, :], A["norm_ffn_2"].to_broadcast([P, D]), "last_rows_in")
            load(fin[:, :], A["final_norm_2"].rearrange("(a d) -> a d", a=1).to_broadcast([P, D]), "last_rows_in")
            stream("out2", 2, A["fox_w_out"][0])
            if stop < 4:
                return
            sp.wait_ge(S("gated"), T)
            load(ghead[:, :], A["gla_g_head"][1:2].rearrange("a h v -> a (h v)").to_broadcast([P, D]), "ghead_in")
            stream("in3", 6, A["gla_w_in"][1])
            stream("out3", 2, A["gla_w_out"][1])
            if stop < 5:
                return
            b0 = BLOCKS["qkv"]
            with sp.Fori(0, 4) as i:
                for slot in range(2):
                    sp.wait_ge(S("proj_done1"), b0 + 2 * i + slot - 1)
                    put(slot, src_of(A["w_in_2"][0], i * (2 * N) + (3 * D + slot * N)))
            one(b0 + 8, src_of(A["w_in_2"][0], 3 * D + 8 * N))
            for i, col in enumerate(CONV_COLS + GATE_COLS):
                one(BLOCKS["conv_in"] + i, src_of(A["w_in_2"][0], col))
            one(BLOCKS["attn"], A["w_attn_out_2"][0].rearrange("(k p) n -> p k n", p=P))
            for name, w in (("conv", "w_conv_out_2"), ("hyb_out", "w_out_2")):
                for i in range(2):
                    one(BLOCKS[name] + i, src_of(A[w][0], i * N))
            if stop < 6:
                return
            sp.wait_ge(S("merged"), T)
            load(skr, A["peer_sub_keys_2"][0].rearrange("h c k d -> k (h c) d"), "sk_in")
            stream("query", 4, A["peer_w_query_2"][0])
            if stop < 7:
                return
            for t in range(T):
                sp.wait_ge(S("out_ready"), t + 1)
                sp.dma_start(out[0, t * P:(t + 1) * P, :], at(t * D, D)).then_inc(S("out_stored"), 16)
            sp.wait_ge(S("out_stored"), 16 * T)

        @block.gpsimd
        def _(pool):
            link = orderer(pool, "pool_order")
            link(nc.gpsimd.memset(ones[:, :], 1.0), wait=False)
            nc.gpsimd.memset(alT[:, :], 1.0).then_inc(S("ones_set"), 1)

            def piece(n):
                L, third, k = n // (3 * KC), n // KC % 3, n % KC
                if n >= 4:
                    pool.wait_ge(S("mod_sum"), n - 3)
                w = A["w_mod"][L].rearrange("(p k) n -> p k n", k=KC)
                pool.dma_start(mring[:, n % 4, :], w[:, k, third * D:(third + 1) * D]) \
                    .then_inc(S(f"mod_landed{n % 4}"), 16)

            def start_sums(L):
                if L:
                    pool.wait_ge(S("mod_read"), L)
                link(nc.gpsimd.memset(acc[:, :], 0.0))
                pool.dma_start(acc[0:1, :], A["b_mod"][L:L + 1, :]).then_inc(S("acc_init"), 16)
                if L:
                    pool.wait_ge(S("mod_ready"), L)
                pool.dma_start(gpost[:, :], A["norm_post_g"][L:L + 1, :].to_broadcast([P, D])) \
                    .then_inc(S("gpost_in"), 16)

            for n in range(4):
                piece(n)
            start_sums(0)
            for n in range(4, ON_DVE + 4):
                if n == 3 * KC + 4:
                    start_sums(1)
                piece(n)
            for n in range(ON_DVE, PIECES):
                if n % (3 * KC) == 0:
                    start_sums(n // (3 * KC))
                    pool.wait_ge(S("acc_init"), (n // (3 * KC) + 1) * 16)
                third, k = n // KC % 3, n % KC
                a = acc[:, third * D:(third + 1) * D]
                pool.wait_ge(S(f"mod_landed{n % 4}"), (n // 4 + 1) * 16)
                w = mring[:, n % 4, :]
                link(nc.gpsimd.tensor_tensor(w, w, cond[:, k:k + 1].to_broadcast([P, D]), ALU.mult))
                nc.gpsimd.tensor_tensor(a, a, w, ALU.add).then_inc(S("mod_sum"), 1)
                if n + 4 < PIECES:
                    piece(n + 4)
                else:
                    pool.wait_ge(S("mod_sum"), n + 1)
            if stop < 7:
                return
            def gather(h, par, kind, tab, index):
                pool.wait_ge(S(f"{kind}_picks"), h + 1)
                for e in range(TOPK):
                    s = e % SLOTS
                    pool.wait_ge(S(f"{kind}_used{s}"), h * 2 + e // SLOTS + 1)
                    pool.nop(nofuse=True)
                    pool.indirect_dma_start(
                        out=dn[s] if kind == "dn" else up[:, s, :], out_offset=None, in_=A[tab][0],
                        in_offset=bass.IndirectOffsetOnAxis(ap=index[:, par, e:e + 1], axis=0)
                    ).then_inc(S(f"{kind}_landed{s}"), 16)

            def two_heads(h, final=False):
                for half in range(2):
                    if not (final and half):
                        gather(h + half + 1, 1 - half, "dn", "peer_down_2", idx)
                    gather(h + half, half, "up", "peer_up_2", idxu)

            gather(0, 0, "dn", "peer_down_2", idx)
            pool.wait_ge(S("sc_sb"), 4)
            with pool.Fori(0, PH - 1) as i:
                two_heads(i * 2)
            two_heads(2 * PH - 2, final=True)

        @block.tensor
        def _(pe):
            mm, tr = nc.tensor.matmul, nc.tensor.transpose

            def transpose_in(src, tag, chunks=KC, banks=(2, 3, 4, 5)):
                for k in range(chunks):
                    for t in range(T):
                        last = tr(bank[banks[k // 2]][:, (k % 2) * 256 + t * P:(k % 2) * 256 + (t + 1) * P],
                                  src(t, k), ident[:, :])
                    if k % 2:
                        last.then_inc(S(tag), 1)

            def transpose_tile(src, t, tag):
                for k in range(KC):
                    last = tr(bank[2 + 2 * t + k // 4][:, (k % 4) * P:(k % 4 + 1) * P], src(k), ident[:, :])
                    if k % 4 == 3:
                        last.then_inc(S(tag), 1)

            def half_block(b, slot, t, lhs=hT):
                if t == 0:
                    pe.wait_ge(S(f"w_landed{slot}"), (b - slot) * 8 + 16)
                pe.wait_ge(S(f"evac{t}"), b + 1)
                for k in range(KC):
                    last = mm(bank[t][:, :], lhs[:, k, t * P:(t + 1) * P], ring[:, slot, k * N:(k + 1) * N],
                              start=(k == 0), stop=(k == KC - 1))
                last.then_inc(S(f"proj_done{t}"), 1)

            def block_products(b, slot, lhs=hT):
                for t in range(T):
                    half_block(b, slot, t, lhs)

            def one_block(b, lhs=hT):
                block_products(b, b % 2, lhs)

            def project(name, n, src, ready, tag, done, uses, first_gate=False):
                b0 = BLOCKS[name]
                for t in range(T):
                    pe.wait_ge(S(ready), uses + t + 1)
                    transpose_tile(lambda k: src(t, k), t, tag)
                    pe.wait_ge(S(done), uses + t + 1)
                    half_block(b0, b0 % 2, t)
                if first_gate:
                    gate_reduce(0, 1)
                    pe.wait_ge(S("mod_ready"), 1)
                if n > 1:
                    one_block(b0 + 1)

                def pair(i):
                    for slot in range(2):
                        block_products(b0 + 2 * i + slot, slot)
                if n > 4:
                    with pe.Fori(1, n // 2) as i:
                        pair(i)
                elif n == 4:
                    pair(1)

            def low_columns(n, tag):
                pe.wait_ge(S("wlow_in"), 7 * 16)
                for t in range(T):
                    for k in range(KC):
                        last = mm(bank[6][:, t * RANK:(t + 1) * RANK], hT[:, k, t * P:(t + 1) * P],
                                  wlow[:, n, k, :], start=(k == 0), stop=(k == KC - 1))
                last.then_inc(S(tag), 1)

            def mod_reduce(L):
                pe.wait_ge(S("acc_init"), (L + 1) * 16)
                for third in range(2):
                    pe.wait_ge(S("mod_sum"), (L * 3 + third + 1) * KC)
                    for j in range(third * KC, (third + 1) * KC):
                        last = mm(bank[7][:, j:j + 1], acc[:, j * P:(j + 1) * P], ones[:, 0:1], start=True, stop=True)
                last.then_inc(S("mod_cols"), 1)

            def gate_reduce(L, b):
                pe.wait_ge(S("mod_sum"), (L + 1) * 3 * KC)
                for i in range(2):
                    pe.wait_ge(S(f"evac{i}"), b + 1)
                    last = mm(bank[i][:, :], ones[:, :], acc[:, 2 * D + i * N:2 * D + (i + 1) * N],
                              start=True, stop=True)
                last.then_inc(S("mod_read"), 1)

            def quads(first, count, q, k, v, kd, between):
                paired = kd == DH

                def transposed(n, src, bk):
                    if paired:
                        for j in range(2):
                            for t in range(T):
                                last = tr(bank[bk][:, j * 256 + t * P:j * 256 + (t + 1) * P], src(n, j, t), ident[:, :])
                        last.then_inc(S("att_T"), 1)
                        return
                    for h in range(4):
                        for t in range(T):
                            last = tr(bank[bk + h // 2][0:kd, (h % 2) * 256 + t * P:(h % 2) * 256 + (t + 1) * P],
                                      src(n, h, t), ident[:, :])
                    last.then_inc(S("att_T"), 1)

                aqT, akT, aS, aPT = bufs(first)
                transposed(0, q, 6)
                transposed(0, k, 3)
                for i in range(count):
                    n = first + i
                    pe.wait_ge(S("att_qT"), n + 1)
                    pe.wait_ge(S("att_kT"), n + 1)
                    if n:
                        pe.wait_ge(S("att_o"), n)
                    for h in range(4):
                        if paired:
                            e, j = h % 2, h // 2
                            q_, k_ = (a[e * kd:(e + 1) * kd, j, :] for a in (aqT, akT))
                            s0, s1 = bank[(5, 2)[e]][:, j * P:(j + 1) * P], bank[6 + e][:, j * 256:(j + 1) * 256]
                        else:
                            q_, k_ = aqT[0:kd, h, :], akT[0:kd, h, :]
                            s0 = bank[5][:, h * P:(h + 1) * P]
                            s1 = bank[6 + h // 2][:, (h % 2) * 256:(h % 2 + 1) * 256]
                        mm(s0, q_[:, 0:P], k_[:, 0:P], start=True, stop=True)
                        last = mm(s1, q_[:, P:2 * P], k_, start=True, stop=True)
                    last.then_inc(S("att_s"), 1)
                    between(i)
                    pe.wait_ge(S("att_p"), n + 1)
                    for b in range(3):
                        for h in range(4):
                            last = tr(bank[2 + b][:, h * P:(h + 1) * P], aS[:, h, b * P:(b + 1) * P], ident[:, :])
                        last.then_inc(S("att_pt"), 1)
                    if i + 1 < count:
                        transposed(i + 1, q, 6)
                    pe.wait_ge(S("att_pta"), n + 1)
                    pe.wait_ge(S("att_ptv"), n + 1)
                    if i + 1 < count:
                        transposed(i + 1, k, 3)
                    for h in range(4):
                        mm(bank[5][:, h * DH:(h + 1) * DH], aPT[:, 0, h, :], v(i, h, 0), start=True, stop=True)
                    for h in range(4):
                        o = bank[5][:, 256 + h * DH:256 + (h + 1) * DH]
                        mm(o, aPT[:, 1, h, :], v(i, h, 0), start=True, stop=False)
                        last = mm(o, aPT[:, 2, h, :], v(i, h, 1), start=False, stop=True)
                    last.then_inc(S("att_pv"), 1)

            def gla(L, j):
                b0 = BLOCKS[f"in{L}"]
                low_columns(j, "low")
                one_block(b0 + 2)
                pe.wait_ge(S("low_sb"), L // 3 + 1)
                for t in range(T):
                    last = mm(bank[7][0:RANK, t * P:(t + 1) * P], low[:, t, :], ident[:, :], start=True, stop=True)
                last.then_inc(S("lowT"), 1)
                pe.wait_ge(S("alT"), L // 3 + 1)
                for h in range(GH):
                    last = mm(bank[6 + h // 2][:, (h % 2) * 256:(h % 2 + 1) * 256],
                              wa2[:, j, h * DK:(h + 1) * DK], alT[:, :], start=True, stop=True)
                last.then_inc(S("decay"), 1)
                for t in range(T):
                    pe.wait_ge(S(f"evac{t}"), b0 + 3)
                for i in range(2):
                    for h in range(GH):
                        for t in range(T):
                            last = tr(bank[2 + 2 * i + h // 2][:, (h % 2) * 256 + t * P:(h % 2) * 256 + (t + 1) * P],
                                      g_in[:, t, i * N + h * DK:i * N + (h + 1) * DK], ident[:, :])
                last.then_inc(S("qkT"), 1)
                one_block(b0 + 3)
                pe.wait_ge(S("qkT_sb"), L // 3 + 1)
                pe.wait_ge(S("logd"), L // 3 + 1)
                for lv in range(LEVELS + 2):
                    q_, k_ = (qT, kT) if lv == 0 else (
                        Q[lv % 2].rearrange("p (h n) -> p h n", h=GH), K[lv % 2].rearrange("p (h n) -> p h n", h=GH))
                    if lv:
                        pe.wait_ge(S("lvl_qk"), L // 3 * (LEVELS + 1) + lv)
                    if lv >= 2:
                        pe.wait_ge(S("lvl_read"), L // 3 * (LEVELS + 1) + lv - 1)
                    bk = (6, 2)[lv % 2]
                    if lv <= LEVELS:
                        for t in range(T):
                            for h in range(GH):
                                last = mm(bank[bk + t][:, h * P:(h + 1) * P], k_[:, h, t * P:(t + 1) * P],
                                          q_[:, h, t * P:(t + 1) * P], start=True, stop=True)
                    else:
                        for h in range(GH):
                            last = mm(bank[bk][:, h * P:(h + 1) * P], k_[:, h, 0:P], q_[:, h, P:2 * P],
                                      start=True, stop=True)
                    last.then_inc(S("lvl"), 1)
                    if lv % 2:
                        half_block(b0 + 4 + lv // 4, (b0 + lv // 4) % 2, lv // 2 % 2)
                if L + 1 < DEPTH:
                    mod_reduce(L + 1)
                    gate_reduce(L + 1, b0 + 6)
                pe.wait_ge(S("attn_sb"), L // 3 + 1)
                for t in range(T):
                    for h in range(GH):
                        o = bank[2 + 2 * t + h // 2][:, (h % 2) * 256:(h % 2 + 1) * 256]
                        last = mm(o, AT[:, t, h * P:(h + 1) * P], g_in[:, t, D + h * DV:D + (h + 1) * DV],
                                  start=True, stop=(t == 0))
                        if t:
                            last = mm(o, AX[:, h, :], g_in[:, 0, D + h * DV:D + (h + 1) * DV],
                                      start=False, stop=True)
                    last.then_inc(S("gla_o"), 1)

            def sgu():
                pe.wait_ge(S("ws_in"), 16)
                for g in range(SG):
                    last = tr(bank[2][:, g * P:(g + 1) * P], ws[:, g, :], ident[:, :])
                last.then_inc(S("wsT"), 1)
                mod_reduce(2)
                gate_reduce(2, BLOCKS["in1"] + 6)
                pe.wait_ge(S("ln_done"), 1)
                for t in range(T):
                    for g in range(SG):
                        last = mm(bank[2 + 2 * t + g // 2][:, (g % 2) * 256:(g % 2 + 1) * 256],
                                  wsT[:, g, :], g_in[:, t, D + g * 256:D + (g + 1) * 256],
                                  start=True, stop=True)
                    last.then_inc(S("mixed"), 1)

            def fox():
                b0 = BLOCKS["in2"]
                low_columns(2, "low")
                half_block(b0 + 4, (b0 + 4) % 2, 0)
                pe.wait_ge(S("logf"), 1)
                pe.wait_ge(S("consts_in"), CONSTS * 16)
                mm(bank[7][:, 0:AH], summ[:, :], low2[:, 0, :], start=True, stop=True)
                mm(bank[7][:, AH:2 * AH], ones[:, :], low2[:, 0, :], start=True, stop=False)
                mm(bank[7][:, AH:2 * AH], summ[:, :], low2[:, 1, :], start=False, stop=True) \
                    .then_inc(S("fsum"), 1)
                half_block(b0 + 4, (b0 + 4) % 2, 1)
                pe.wait_ge(S("qka"), 1)

                def between(n):
                    if n < 2:
                        one_block(b0 + 5 + n)
                    else:
                        half_block(b0 + 7, (b0 + 7) % 2, n - 2)

                quads(0, 4, lambda n, h, t: qa[:, t, 4 * n + h, :], lambda n, h, t: ka[:, t, 4 * n + h, :],
                      lambda n, h, t: f_in[:, t, 2 * D + (4 * n + h) * DH:2 * D + (4 * n + h + 1) * DH],
                      DH + 2, between)
                mod_reduce(3)
                gate_reduce(3, b0 + 8)

            pe.wait_ge(S("rows_in"), 4 * 16)
            tr(bank[7][:, 0:64], rows[:, :], ident[0:64, 0:64]).then_inc(S("colsT"), 1)
            pe.wait_ge(S("ones_set"), 1)
            pe.wait_ge(S("pool_order"), 1)
            mod_reduce(0)
            for L in range(DEPTH):
                if stop < L + 1:
                    return
                if L:
                    pe.wait_ge(S("mod_ready"), L + 1)
                else:
                    pe.wait_ge(S("mod_cols_sb"), 1)
                project(f"in{L}", (2, 6, 4, 2)[L], lambda t, k: xn[:, t, k * P:(k + 1) * P], "xn", "xT", "hT", T * L, first_gate=(L == 0))
                if L in (0, 3):
                    gla(L, L // 3)
                elif L == 1:
                    sgu()
                else:
                    fox()
                src = fo if L == 2 else g_in[:, :, 2 * D:3 * D]
                if L + 1 < DEPTH:
                    pe.wait_ge(S("mod_ready"), L + 2)
                project(f"out{L}", 2, lambda t, k: src[:, t, k * P:(k + 1) * P], "gated", "gT", "ghT", T * L)
            if stop < 5:
                return
            b0 = BLOCKS["qkv"]
            project("qkv", 8, lambda t, k: xn[:, t, k * P:(k + 1) * P], "xn", "xT", "hT", T * DEPTH)
            one_block(b0 + 8)
            pe.wait_ge(S("rotated"), 1)

            def head(c0, heads=1):
                return lambda n, h, t: hb[:, t, c0 + (4 * n + heads * h) * DH:c0 + (4 * n + heads * (h + 1)) * DH]

            quads(4, 6, head(QO, 2), head(KO, 2), head(VO), DH, lambda n: one_block(BLOCKS["conv_in"] + n))
            pe.wait_ge(S("z_conv"), 1)
            one_block(BLOCKS["gates"])
            transpose_in(lambda t, k: ha[:, t, D + k * P:D + (k + 1) * P], "zT")
            one_block(BLOCKS["gates"] + 1)
            one_block(BLOCKS["gates"] + 2)
            one_block(BLOCKS["gates"] + 3)
            pe.wait_ge(S("zT_sb"), 1)
            pe.wait_ge(S("att_merged"), 1)
            transpose_in(lambda t, k: od[:, t, 0, k * P:(k + 1) * P], "oT", chunks=4)
            pe.wait_ge(S("oT_sb"), 1)
            transpose_in(lambda t, k: ha[:, t, k * P:(k + 1) * P], "bT")
            b = BLOCKS["attn"]
            pe.wait_ge(S(f"w_landed{b % 2}"), (b // 2 + 1) * 16)
            wv = ring[:, b % 2, :].rearrange("p (k n) -> p k n", n=D)
            for half in (1, 0):
                for t in range(T):
                    if half == 0:
                        pe.wait_ge(S(f"evac{t}"), b + 1)
                    for k in range(4):
                        last = mm(bank[t + 6 * half][:, :], hT[:, k, t * P:(t + 1) * P],
                                  wv[:, k, half * N:(half + 1) * N], start=(k == 0), stop=(k == 3))
                    last.then_inc(S("attn_half") if half else S(f"proj_done{t}"), 1)
            pe.wait_ge(S("conv_in"), 1)
            for i in range(2):
                one_block(BLOCKS["conv"] + i, cT)
            project("hyb_out", 1, lambda t, k: ha[:, t, k * P:(k + 1) * P], "merged", "mT", "mT_sb", 0)
            pe.wait_ge(S("sk_in"), 16)
            for g in range(4):
                for i in range(4):
                    last = tr(bank[2 + g][:, i * P:(i + 1) * P], skr[:, 4 * g + i, :], ident[:, :])
                last.then_inc(S("skT"), 1)
            one_block(BLOCKS["hyb_out"] + 1)
            if stop < 6:
                return
            project("query", 1, lambda t, k: u[:, t, k * P:(k + 1) * P], "u_ready", "uT", "uT_sb", 0)
            for b in range(4):
                if b:
                    one_block(BLOCKS["query"] + b)
                for t in range(T):
                    pe.wait_ge(S(f"evac{t}"), BLOCKS["query"] + b + 2)
                pe.wait_ge(S("pq_sb"), b + 1)
                for i in range(4):
                    for t in range(T):
                        last = tr(bank[6 + i // 2][:, (i % 2) * 256 + t * P:(i % 2) * 256 + (t + 1) * P],
                                  qq[:, b % 2, t, i * P:(i + 1) * P], ident[:, :])
                last.then_inc(S("pqT"), 1)
                pe.wait_ge(S("pq_sb"), b + 2)
                if b:
                    pe.wait_ge(S("sc_sb"), b)
                for t in range(T):
                    for i in range(4):
                        last = mm(bank[4 + t][:, i * P:(i + 1) * P], pqT[:, b % 2, i, t * P:(t + 1) * P],
                                  skT[:, 4 * b + i, :], start=True, stop=True)
                last.then_inc(S("sc_mm"), 1)
            if stop < 7:
                return
            for t in range(T):
                for i in range(2):
                    mm(bank[2 * t + i][:, :], ident[:, :], x[:, t, i * N:(i + 1) * N], start=True, stop=False,
                       skip_group_check=True)

                def two_heads(i):
                    for half in range(2):
                        h = i * 2 + half + t * PH
                        for e in range(TOPK):
                            s = e % SLOTS
                            pe.wait_ge(S("diag"), h * TOPK + e + 1)
                            pe.wait_ge(S(f"up_landed{s}"), (h * 2 + e // SLOTS + 1) * 16)
                            for c in range(2):
                                last = mm(bank[2 * t + c][:, :], diag[:, e % 4, :], up[:, s, c * N:(c + 1) * N],
                                          start=False, stop=False, skip_group_check=True)
                            last.then_inc(S(f"up_used{s}"), 1)
                with pe.Fori(0, PH // 2) as i:
                    two_heads(i)
                for c in range(2):
                    last = mm(bank[2 * t + c][:, :], zero[:, :], x[:, t, c * N:(c + 1) * N],
                              start=False, stop=True, skip_group_check=True)
                last.then_inc(S("peer_done"), 1)

        @block.scalar
        def _(act):
            link = orderer(act, "act_order")
            af = nc.scalar.activation

            def half(b, t, dst, f=ACT.Copy, **more):
                act.wait_ge(S(f"proj_done{t}"), b + 1)
                return af(dst, bank[t][:, :], f, **more).then_inc(S(f"evac{t}"), 1)

            def evac(b, slot, dst):
                for t in range(T):
                    half(b, t, dst(t))

            def one_block(b, buf, col):
                evac(b, b % 2, lambda t: buf[:, t, col:col + N])

            def project(name, n, dst):
                b0 = BLOCKS[name]

                def pair(i):
                    for slot in range(2):
                        evac(b0 + 2 * i + slot, slot, lambda t: dst[:, t, ds(i * (2 * N) + slot * N, N)])
                if n > 2:
                    with act.Fori(0, n // 2) as i:
                        pair(i)
                else:
                    pair(0)

            def evac_done(b):
                for t in range(T):
                    act.wait_ge(S(f"evac{t}"), b + 1)

            def root(tag, n, width, bias=EPS):
                r = rstd[:, COL[tag]:COL[tag] + n]
                act.wait_ge(S("ssq"), nth(tag))
                link(af(r, ssq[:, COL[tag]:COL[tag] + n], ACT.Ln, scale=1.0 / width, bias=bias))
                af(r, r, ACT.Exp, scale=-0.5).then_inc(S("root"), 1)

            def squares(src, tag, t):
                af(trash[:, t, 0:src.shape[1]], src, ACT.Square, accum_out=ssq[:, COL[tag]:COL[tag] + 1]) \
                    .then_inc(S("ssq"), 1)

            def output(L):
                b = BLOCKS[f"out{L}"]
                for t in range(T):
                    act.wait_ge(S(f"proj_done{t}"), b + 1)
                    af(trash[:, t, 0:N], bank[t][:, :], ACT.Square, accum_out=half_ssq[:, T * L + t:T * L + t + 1])
                    half(b, t, ob[:, t, 0:N])
                for t in range(T):
                    act.wait_ge(S(f"proj_done{t}"), b + 2)
                    squares(bank[t][:, :], f"post{L}.{t}", t)
                    act.wait_ge(S("half_var"), T * L + t + 1)
                    root(f"post{L}.{t}", 1, D, bias=half_ssq[:, T * L + t:T * L + t + 1])
                    act.wait_ge(S("x_ready"), T * L + t + 1)
                    squares(x[:, t, :], f"norm{L + 1}.{t}", t)
                    root(f"norm{L + 1}.{t}", 1, D)

            def quads(first, count, kd, between):
                aqT, akT, aS, aPT = bufs(first)

                def q_in(n):
                    act.wait_ge(S("att_T"), 2 * n + 1)
                    for i in range(1 if kd == DH else 2):
                        rows_ = slice(0, P if kd == DH else kd)
                        last = af(aqT[rows_, 2 * i:2 * i + 2, :].rearrange("p h n -> p (h n)"),
                                  bank[6 + i][rows_, :], ACT.Copy)
                    last.then_inc(S("att_qT"), 1)

                q_in(first)
                for i in range(count):
                    n = first + i
                    act.wait_ge(S("att_m"), n + 1)
                    for h in range(4):
                        for t in range(T):
                            part = aS[:, h, 0:P] if t == 0 else aS[:, h, P:3 * P]
                            last = af(part, part, ACT.Exp, bias=anm[:, n, 2 * h + t:2 * h + t + 1],
                                      accum_out=al[:, n, 2 * h + t:2 * h + t + 1])
                    last.then_inc(S("att_p"), 1)
                    between(i)
                    act.wait_ge(S("att_pt"), 3 * n + 1)
                    af(aPT[:, 0, :, :].rearrange("p h n -> p (h n)"), bank[2][:, :], ACT.Copy)
                    act.wait_ge(S("att_pt"), 3 * n + 3)
                    af(aPT[:, 2, :, :].rearrange("p h n -> p (h n)"), bank[4][:, :], ACT.Copy) \
                        .then_inc(S("att_pta"), 1)
                    if i + 1 < count:
                        q_in(n + 1)

            act.wait_ge(S("cond_in"), 16)
            af(cond[:, :], cond[:, :], ACT.Silu).then_inc(S("cond"), 1)
            act.wait_ge(S("x_in"), 16)
            for t in range(T):
                squares(x[:, t, :], f"norm0.{t}", t)
                root(f"norm0.{t}", 1, D)
            for L in range(DEPTH):
                if stop < L + 1:
                    return
                b0 = BLOCKS[f"in{L}"]
                if L in (0, 3):
                    project(f"in{L}", 2, g_in)
                if L in (0, 3):
                    one_block(b0 + 2, g_in, 2 * N)
                    act.wait_ge(S("decay"), L // 3 + 1)
                    ya = Dd[0]
                    for i in range(2):
                        link(af(ya[:, i * N:(i + 1) * N], bank[6 + i][:, :], ACT.Abs))
                    link(af(ya, ya, ACT.Exp, scale=-1.0))
                    af(ya, ya, ACT.Ln, bias=1.0).then_inc(S("lnd"), 1)
                    act.wait_ge(S("qkT"), L // 3 + 1)
                    for i in range(2):
                        af(qT[:, 2 * i:2 * i + 2, :].rearrange("p h n -> p (h n)"), bank[2 + i][:, :],
                           ACT.Copy, scale=DK ** -0.5)
                        last = af(kT[:, 2 * i:2 * i + 2, :].rearrange("p h n -> p (h n)"),
                                  bank[4 + i][:, :], ACT.Copy)
                    last.then_inc(S("qkT_sb"), 1)
                    for lv in range(1, LEVELS + 2):
                        act.wait_ge(S("lvl_d"), L // 3 * (LEVELS + 1) + lv)
                        af(Dd[lv % 2], Dd[lv % 2], ACT.Exp).then_inc(S("lvl_e"), 1)
                        if lv == 2:
                            one_block(b0 + 3, g_in, 3 * N)
                        if lv % 2 == 0 and lv >= 4:
                            hf = lv // 2 - 2
                            half(b0 + 4 + hf // 2, hf % 2, g_in[:, hf % 2, (4 + hf // 2) * N:(5 + hf // 2) * N])
                    half(b0 + 5, 1, g_in[:, 1, 5 * N:6 * N])
                    evac_done(b0 + 6)
                    for t in range(T):
                        af(g_in[:, t, 2 * D:3 * D], g_in[:, t, 2 * D:3 * D], ACT.Silu).then_inc(S("silu"), 1)
                    for t in range(T):
                        act.wait_ge(S("gla_o"), L // 3 * T + t + 1)
                        c0 = COL[f"head{L}.{t}"]
                        for h in range(GH):
                            last = af(at(W0 + 7 * D + (t * GH + h) * DV, DV), bank[2 + 2 * t + h // 2][:, (h % 2) * DV:(h % 2 + 1) * DV],
                                      ACT.Square, accum_out=ssq[:, c0 + h:c0 + h + 1])
                        last.then_inc(S("ssq"), 1)
                        root(f"head{L}.{t}", GH, DV)
                elif L == 1:
                    for c in range(4):
                        for t in range(T):
                            dst = g_in[:, t, c * N:(c + 1) * N]
                            if c < 2:
                                half(b0 + c, t, dst, ACT.Gelu_apprx_tanh)
                            else:
                                half(b0 + c, t, dst, ACT.Gelu_apprx_tanh, accum_out=small[:, (c - 2) * T + t:(c - 2) * T + t + 1])
                    evac_done(b0 + 4)
                    link(af(small[:, 4:4 + T], small[:, 0:T], ACT.Copy, scale=-1.0 / D))
                    for t in range(T):
                        link(af(small[:, 6 + t:7 + t], small[:, T + t:T + t + 1], ACT.Identity, scale=-1.0 / D,
                                bias=small[:, 4 + t:5 + t]))
                    for t in range(T):
                        half(b0 + 4, t, g_in[:, t, 4 * N:5 * N], ACT.Silu)
                        link(af(g_in[:, t, D:2 * D], g_in[:, t, D:2 * D], ACT.Identity, bias=small[:, 6 + t:7 + t]))
                        last = af(at(W0 + (2 + t) * D, D), g_in[:, t, D:2 * D], ACT.Square, accum_out=ssq[:, t:t + 1])
                    last.then_inc(S("ssq"), 1)
                    root("ln", T, D)
                    for t in range(T):
                        half(b0 + 5, t, g_in[:, t, 5 * N:6 * N], ACT.Silu)
                else:
                    for i in range(2):
                        one_block(b0 + 2 * i, f_in, 2 * i * N)
                        if i:
                            root("qk.0", 2 * AH, DH)
                        one_block(b0 + 2 * i + 1, f_in, (2 * i + 1) * N)
                        evac_done(b0 + 2 * i + 2)
                        af(sqs[:, i, :].rearrange("p (t d) -> p t d", t=T), f_in[:, :, i * D:(i + 1) * D],
                           ACT.Square).then_inc(S("sq_qk"), 1)
                    act.wait_ge(S("f_sb"), 1)
                    link(af(low2[:, :, :], low[:, :, :], ACT.Abs))
                    link(af(low2[:, :, :], low2[:, :, :], ACT.Exp, scale=-1.0))
                    af(low2[:, :, :], low2[:, :, :], ACT.Ln, bias=1.0).then_inc(S("lnf"), 1)
                    root("qk.1", 2 * AH, DH)
                    one_block(b0 + 4, f_in, 4 * N)

                    def between(n):
                        if n < 2:
                            one_block(b0 + 5 + n, f_in, (5 + n) * N)
                        else:
                            half(b0 + 7, n - 2, f_in[:, n - 2, 7 * N:8 * N])

                    quads(0, 4, DH + 2, between)
                    evac_done(b0 + 8)
                    for t in range(T):
                        af(f_in[:, t, 3 * D:4 * D], f_in[:, t, 3 * D:4 * D], ACT.Silu).then_inc(S("silu_fox"), 1)
                output(L)
            if stop < 5:
                return
            act.wait_ge(S("angles"), 1)
            af(trig[:, :, :], trig[:, :, :], ACT.Sin).then_inc(S("trig"), 1)
            project("qkv", 8, hb)
            one_block(BLOCKS["qkv"] + 8, hb, 8 * N)
            quads(4, 6, DH, lambda n: one_block(BLOCKS["conv_in"] + n, ha, CONV_COLS[n]))
            one_block(BLOCKS["gates"], hb, GC)
            act.wait_ge(S("lse_in"), 1)
            af(lse[:, 0, :], al[:, 4:10, :].rearrange("p n h -> p (n h)"), ACT.Ln).then_inc(S("lse_ln"), 1)
            act.wait_ge(S("lse_m"), 1)
            af(lse[:, 0, :], lse[:, 1, :], ACT.Exp).then_inc(S("lse_e"), 1)
            for i in range(1, 4):
                one_block(BLOCKS["gates"] + i, hb, GC + i * N)
            act.wait_ge(S("gates_in"), 1)
            af(hb[:, :, GC:GC + 2 * D], hb[:, :, GC:GC + 2 * D], ACT.Sigmoid).then_inc(S("gates"), 1)
            act.wait_ge(S("attn_half"), 2)
            for t in range(T):
                af(ha[:, t, D + N:2 * D], bank[6 + t][:, :], ACT.Copy)
            b = BLOCKS["attn"]
            evac(b, b % 2, lambda t: ha[:, t, D:D + N])
            one_block(BLOCKS["conv"], ha, 0)
            b = BLOCKS["hyb_out"]
            evac(b, b % 2, lambda t: ha[:, t, 2 * D:2 * D + N])
            for g in range(4):
                act.wait_ge(S("skT"), g + 1)
                last = af(skT[:, 4 * g:4 * g + 4, :].rearrange("p i n -> p (i n)"), bank[2 + g][:, :], ACT.Copy)
            last.then_inc(S("pq_sb"), 1)
            if stop < 6:
                return
            for t in range(T):
                act.wait_ge(S("x_ready"), T * DEPTH + t + 1)
                squares(x[:, t, :], f"ffn.{t}", t)
                root(f"ffn.{t}", 1, D)
            evac(BLOCKS["query"], BLOCKS["query"] % 2, lambda t: qq[:, 0, t, :])
            for b in range(4):
                if b:
                    evac(BLOCKS["query"] + b, b % 2, lambda t: qq[:, b % 2, t, :])
                act.wait_ge(S("pqT"), b + 1)
                for i in range(2):
                    last = af(pqT[:, b % 2, 2 * i:2 * i + 2, :].rearrange("p i n -> p (i n)"), bank[6 + i][:, :],
                              ACT.Copy)
                last.then_inc(S("pq_sb"), 1)
                act.wait_ge(S("sc_mm"), b + 1)
                for t in range(T):
                    last = af(sc[:, t, b * N:(b + 1) * N], bank[4 + t][:, :], ACT.Copy)
                last.then_inc(S("sc_sb"), 1)
            if stop < 7:
                return
            for t in range(T):
                def two_heads(i):
                    for half in range(2):
                        h = i * 2 + half + t * PH
                        act.wait_ge(S("choice"), h * LINKS + BEST)
                        af(pex[:, half, :], pbest[:, half, :], ACT.Exp, bias=pneg[:, half, :],
                           accum_out=psm[:, half, :]).then_inc(S("pexp"), 1)
                        act.wait_ge(S(f"dn_used{SLOTS - 1}"), h * 2 + 3)
                        af(pa[:, half, :], pa[:, half, :], ACT.Gelu).then_inc(S("gelu"), 1)
                        act.wait_ge(S("coef"), h + 1)
                        for e in range(TOPK):
                            act.wait_ge(S(f"up_used{(e - 4) % SLOTS}"),
                                        h * 2 + (e - 4) // SLOTS + 2)
                            af(diag[:, e % 4, :], ident[:, :], ACT.Copy, scale=pcoef[:, half, e:e + 1]) \
                                .then_inc(S("diag"), 1)
                with act.Fori(0, PH // 2) as i:
                    two_heads(i)
            for t in range(T):
                act.wait_ge(S("peer_done"), t + 1)
                for c in range(2):
                    last = af(at(t * D + c * N, N), bank[2 * t + c][:, :], ACT.Square,
                              accum_out=sqf[:, 2 * t + c:2 * t + c + 1])
                last.then_inc(S("sq_final"), 1)
            root("final", T, D)

        @block.vector
        def _(dve):
            v = nc.vector
            link = orderer(dve, "dve_order")

            def copy_banks(dst, tag, done, n=4, base=0):
                for i in range(n):
                    dve.wait_ge(S(tag), base + i + 1)
                    last = v.tensor_copy(dst[:, 2 * i:2 * i + 2, :].rearrange("p k n -> p (k n)"), bank[2 + i][:, :])
                last.then_inc(S(done), 1)

            def mod_sums(first, last):
                dve.wait_ge(S("acc_init"), (first // (3 * KC) + 1) * 16)
                dve.wait_ge(S("cond"), 1)
                for n in range(first, last):
                    third, k = n // KC % 3, n % KC
                    a = acc[:, third * D:(third + 1) * D]
                    if n:
                        dve.wait_ge(S("mod_sum"), n)
                    dve.wait_ge(S(f"mod_landed{n % 4}"), (n // 4 + 1) * 16)
                    v.scalar_tensor_tensor(out=a, in0=mring[:, n % 4, :], scalar=cond[:, k:k + 1], in1=a,
                                           op0=ALU.mult, op1=ALU.add).then_inc(S("mod_sum"), 1)

            def mod_columns(L):
                dve.wait_ge(S("mod_cols"), L + 1)
                v.tensor_copy(modc[:, L % 2, 0, :], bank[7][:, 0:KC])
                v.scalar_tensor_tensor(out=modc[:, L % 2, 1, :], in0=bank[7][:, KC:2 * KC], scalar=1.0,
                                       in1=cols[:, L * KC:(L + 1) * KC], op0=ALU.add, op1=ALU.mult) \
                    .then_inc(S("mod_cols_sb"), 1)

            def mod_gate(L):
                dve.wait_ge(S("mod_read"), L + 1)
                dve.wait_ge(S("gpost_in"), 16 * (L + 1))
                for i in range(2):
                    last = v.tensor_tensor(gateb[:, L % 2, i * N:(i + 1) * N], bank[i][:, :],
                                           gpost[:, i * N:(i + 1) * N], ALU.mult)
                last.then_inc(S("mod_ready"), 1)

            def root(tag, n, width, scale=None, half=None):
                c = slice(COL[tag], COL[tag] + n)
                q, y, w = var[:, c], rstd[:, c], newton[:, c]
                dve.wait_ge(S("ssq"), nth(tag))
                if half is None:
                    link(v.tensor_scalar(q, ssq[:, c], 1.0 / width, EPS, ALU.mult, ALU.add), wait=False)
                else:
                    link(v.scalar_tensor_tensor(out=q, in0=ssq[:, c], scalar=1.0 / width, in1=half,
                                                op0=ALU.mult, op1=ALU.add), wait=False)
                dve.wait_ge(S("dve_order"), ORDER["dve_order"])
                dve.wait_ge(S("root"), nth(tag))
                if n == 1:
                    link(v.scalar_tensor_tensor(out=w, in0=y, scalar=y, in1=q, op0=ALU.mult, op1=ALU.mult))
                else:
                    link(v.tensor_tensor(w, y, y, ALU.mult))
                    link(v.tensor_tensor(w, w, q, ALU.mult))
                link(v.tensor_scalar(w, w, -0.5, 1.5, ALU.mult, ALU.add))
                link(v.tensor_tensor(y, y, w, ALU.mult))
                if scale is not None:
                    link(v.tensor_scalar(rstd[:, 0:scale[0]], rstd[:, 0:scale[0]], scale[1], None, ALU.mult))
                return rstd[:, COL[tag]:COL[tag] + 1]

            def copy_tile(t, tag, done, base=0):
                for i in range(2):
                    dve.wait_ge(S(tag), base + 2 * t + i + 1)
                    last = v.tensor_copy(hT[:, 4 * i:4 * i + 4, t * P:(t + 1) * P],
                                         bank[2 + 2 * t + i][:, :].rearrange("p (k n) -> p k n", k=4))
                last.then_inc(S(done), 1)

            def normalized(L, t):
                r = root(f"norm{L}.{t}", 1, D)
                v.tensor_scalar(xn[:, t, :], x[:, t, :], r, None, ALU.mult).then_inc(S("xn"), 1)

            def modulated(L, t):
                if L < DEPTH:
                    dve.wait_ge(S("mod_cols_sb"), L + 1)
                for k in range(KC):
                    dve.wait_ge(S("xT"), 4 * L + 2 * t + k // 4 + 1)
                    src, dst = bank[2 + 2 * t + k // 4][:, (k % 4) * P:(k % 4 + 1) * P], hT[:, k, t * P:(t + 1) * P]
                    if L < DEPTH:
                        last = v.tensor_scalar(dst, src, modc[:, L % 2, 1, k:k + 1], modc[:, L % 2, 0, k:k + 1],
                                               ALU.mult, ALU.add)
                    else:
                        last = v.tensor_scalar(dst, src, cols[:, 32 + k:33 + k], None, ALU.mult)
                last.then_inc(S("hT"), 1)

            def output(L):
                b, gate = BLOCKS[f"out{L}"], gateb[:, L % 2, :]
                for t in range(T):
                    hs = half_ssq[:, T * L + t:T * L + t + 1]
                    dve.wait_ge(S(f"evac{t}"), b + 2)
                    v.tensor_tensor(ob[:, t, 0:N], ob[:, t, 0:N], gate[:, 0:N], ALU.mult)
                    v.tensor_scalar(hs, hs, 1.0 / D, EPS, ALU.mult, ALU.add).then_inc(S("half_var"), 1)

                def second(t):
                    dve.wait_ge(S("ssq"), nth(f"post{L}.{t}"))
                    v.tensor_tensor(ob[:, t, N:D], bank[t][:, :], gate[:, N:D], ALU.mult).then_inc(S(f"evac{t}"), 1)

                def update(t):
                    dve.wait_ge(S("half_var"), T * L + t + 1)
                    r = root(f"post{L}.{t}", 1, D, half=half_ssq[:, T * L + t:T * L + t + 1])
                    dve.wait_ge(S(f"evac{t}"), b + 3)
                    v.scalar_tensor_tensor(out=x[:, t, :], in0=ob[:, t, :], scalar=r, in1=x[:, t, :],
                                           op0=ALU.mult, op1=ALU.add).then_inc(S("x_ready"), 1)
                    dve.wait_ge(S("x_ready"), T * L + t + 1)
                    normalized(L + 1, t)

                second(0)
                update(0)
                second(1)
                modulated(L + 1, 0)
                update(1)
                modulated(L + 1, 1)

            def quads(first, count, mask, out_of):
                aqT, akT, aS, aPT = bufs(first)
                kd = DH + 2 if first < 4 else DH

                def k_in(n):
                    dve.wait_ge(S("att_T"), 2 * n + 2)
                    for i in range(1 if kd == DH else 2):
                        rows_ = slice(0, P if kd == DH else kd)
                        last = v.tensor_copy(akT[rows_, 2 * i:2 * i + 2, :].rearrange("p h n -> p (h n)"),
                                             bank[3 + i][rows_, :])
                    last.then_inc(S("att_kT"), 1)

                k_in(first)
                for i in range(count):
                    n, m, o = first + i, mask(i), out_of(i)
                    dve.wait_ge(S("att_s"), n + 1)
                    if kd == DH:
                        for e in range(2):
                            hs = aS.rearrange("p (j e) n -> p e j n", e=2)[:, e, :, :]
                            v.tensor_tensor(hs[:, :, 0:P], bank[(5, 2)[e]][:, 0:256].rearrange("p (h n) -> p h n", h=2),
                                            amask[:, m, P:2 * P].unsqueeze(1).to_broadcast([P, 2, P]), ALU.add)
                            last = v.tensor_tensor(hs[:, :, P:3 * P], bank[6 + e][:, :].rearrange("p (h n) -> p h n", h=2),
                                                   amask[:, m, :].unsqueeze(1).to_broadcast([P, 2, 2 * P]), ALU.add)
                    else:
                        v.tensor_tensor(aS[:, :, 0:P], bank[5][:, :].rearrange("p (h n) -> p h n", h=4),
                                        amask[:, m, P:2 * P].unsqueeze(1).to_broadcast([P, 4, P]), ALU.add)
                        for j in range(2):
                            last = v.tensor_tensor(aS[:, 2 * j:2 * j + 2, P:3 * P],
                                                   bank[6 + j][:, :].rearrange("p (h n) -> p h n", h=2),
                                                   amask[:, m, :].unsqueeze(1).to_broadcast([P, 2, 2 * P]), ALU.add)
                    link(last)
                    nm = anm[:, n, :].rearrange("p (h t) -> p h t", t=T)
                    v.tensor_reduce(nm[:, :, 0:1], aS[:, :, 0:P], X, ALU.max)
                    link(v.tensor_reduce(nm[:, :, 1:2], aS[:, :, P:3 * P], X, ALU.max))
                    v.tensor_scalar(anm[:, n, :], anm[:, n, :], -1.0, None, ALU.mult).then_inc(S("att_m"), 1)
                    dve.wait_ge(S("att_pt"), 3 * n + 2)
                    v.tensor_copy(aPT[:, 1, :, :].rearrange("p h n -> p (h n)"), bank[3][:, :]).then_inc(S("att_ptv"), 1)
                    if i + 1 < count:
                        k_in(n + 1)
                    dve.wait_ge(S("att_pv"), n + 1)
                    link(v.reciprocal(arl[:, :], al[:, n, :]))
                    pv_ = bank[5][:, :].rearrange("p (t h d) -> p t h d", t=T, h=4)
                    rl = arl[:, :].rearrange("p (h t) -> p t h", t=T)
                    for t in range(T):
                        last = v.tensor_tensor(o[:, t, :].rearrange("p (h d) -> p h d", h=4), pv_[:, t, :, :],
                                               rl[:, t, :].unsqueeze(2).to_broadcast([P, 4, DH]), ALU.mult)
                    last.then_inc(S("att_o"), 1)

            def gla(L):
                dve.wait_ge(S("low"), 3 if L else 1)
                v.tensor_copy(low[:, :, :].rearrange("p t n -> p (t n)"), bank[6][:, 0:T * RANK]) \
                    .then_inc(S("low_sb"), 1)
                dve.wait_ge(S("ones_set"), 1)
                dve.wait_ge(S("lowT"), L // 3 + 1)
                v.tensor_copy(alT[0:RANK, :], bank[7][0:RANK, 0:T * P]).then_inc(S("alT"), 1)
                for b in (Q[0], Q[1], K[0], K[1], AT[:, 0, :], AT[:, 1, :]):
                    link(v.memset(b, 0.0), wait=False)
                dve.wait_ge(S("dve_order"), ORDER["dve_order"])
                bfl = b_.rearrange("p h n -> p (h n)")
                dve.wait_ge(S("lnd"), L // 3 + 1)
                for i in range(2):
                    link(v.scalar_tensor_tensor(out=bfl[:, i * N:(i + 1) * N], in0=bank[6 + i][:, :], scalar=0.0,
                                                in1=Dd[0][:, i * N:(i + 1) * N], op0=ALU.min, op1=ALU.subtract))
                link(v.tensor_scalar(bfl, bfl, 1.0 / 16.0, None, ALU.mult))
                for h in range(GH):
                    last = v.tensor_tensor_scan(b_[:, h, :], ones[:, 0:1].to_broadcast([P, T * P]), b_[:, h, :], 0.0,
                                                ALU.mult, ALU.add)
                last.then_inc(S("logd"), 1)
                dve.wait_ge(S("logd"), L // 3 + 1)
                dve.wait_ge(S("qkT_sb"), L // 3 + 1)

                def halves(a, lv):
                    return a.rearrange("p (n two l) -> p n two l", two=2, l=1 << (lv - 1))

                def exponents(lv):
                    if lv >= 3:
                        dve.wait_ge(S("lvl_qk"), L // 3 * (LEVELS + 1) + lv - 2)
                    size = 1 << (lv - 1)
                    n = GH * T * P // (2 * size)
                    bv, dv = halves(bfl, lv), halves(Dd[lv % 2], lv)
                    ref = bv[:, :, 0, size - 1:size].to_broadcast([P, n, size])
                    v.tensor_tensor(dv[:, :, 1, :], bv[:, :, 1, :], ref, ALU.subtract)
                    v.tensor_tensor(dv[:, :, 0, :], ref, bv[:, :, 0, :], ALU.subtract).then_inc(S("lvl_d"), 1)

                def decayed(lv):
                    dve.wait_ge(S("lvl_e"), L // 3 * (LEVELS + 1) + lv)
                    if lv >= 2:
                        dve.wait_ge(S("lvl"), L // 3 * (LEVELS + 2) + lv - 1)
                    e = halves(Dd[lv % 2], lv)
                    v.tensor_tensor(halves(Q[lv % 2], lv)[:, :, 1, :],
                                    halves(qT.rearrange("p h n -> p (h n)"), lv)[:, :, 1, :], e[:, :, 1, :], ALU.mult)
                    v.tensor_tensor(halves(K[lv % 2], lv)[:, :, 0, :],
                                    halves(kT.rearrange("p h n -> p (h n)"), lv)[:, :, 0, :], e[:, :, 0, :], ALU.mult) \
                        .then_inc(S("lvl_qk"), 1)

                def take(lv):
                    dve.wait_ge(S("lvl"), L // 3 * (LEVELS + 2) + lv + 1)
                    if lv:
                        dve.wait_ge(S("lvl_read"), L // 3 * (LEVELS + 1) + lv)
                    b0 = (6, 2)[lv % 2]
                    if lv <= LEVELS:
                        for t in range(T):
                            last = v.copy_predicated(AT[:, t, :].rearrange("p (h n) -> p h n", h=GH),
                                                     gmask[:, lv, :].unsqueeze(1).to_broadcast([P, GH, P]),
                                                     bank[b0 + t][:, :].rearrange("p (h n) -> p h n", h=GH))
                        last.then_inc(S("lvl_read"), 1)
                    else:
                        v.tensor_copy(AX.rearrange("p h n -> p (h n)"), bank[b0][:, :]).then_inc(S("attn_sb"), 1)

                dve.wait_ge(S("consts_in"), CONSTS * 16)
                exponents(1)
                for lv in range(1, LEVELS + 2):
                    if lv <= LEVELS:
                        exponents(lv + 1)
                    decayed(lv)
                    take(lv - 1)
                take(LEVELS + 1)
                if L + 1 < DEPTH:
                    mod_columns(L + 1)
                    mod_gate(L + 1)
                dve.wait_ge(S("ghead_in"), 16 if L == 0 else 32)
                z = g_in[:, :, 2 * D:3 * D]
                for t in range(T):
                    dve.wait_ge(S("silu"), L // 3 * T + t + 1)
                    last = v.tensor_tensor(z[:, t, :], z[:, t, :], ghead[:, :], ALU.mult)
                link(last)
                for t in range(T):
                    root(f"head{L}.{t}", GH, DV)
                    c = COL[f"head{L}.{t}"]
                    for h in range(GH):
                        zh = z[:, t, h * DV:(h + 1) * DV]
                        last = v.scalar_tensor_tensor(
                            out=zh, in0=bank[2 + 2 * t + h // 2][:, (h % 2) * DV:(h % 2 + 1) * DV],
                            scalar=rstd[:, c + h:c + h + 1], in1=zh, op0=ALU.mult, op1=ALU.mult)
                    last.then_inc(S("gated"), 1)

            def sgu():
                dve.wait_ge(S("wsT"), 1)
                link(v.tensor_tensor(wsT, bank[2][:, :].rearrange("p (g n) -> p g n", g=SG),
                                     summ[:, :].unsqueeze(1).to_broadcast([P, SG, P]), ALU.mult), wait=False)
                root("ln", T, D)
                for t in range(T):
                    vt = g_in[:, t, D:2 * D]
                    link(v.scalar_tensor_tensor(out=vt, in0=vt, scalar=rstd[:, t:t + 1], in1=lng[:, :],
                                                op0=ALU.mult, op1=ALU.mult))
                    last = v.tensor_tensor(vt, vt, lnb[:, :], ALU.add)
                last.then_inc(S("ln_done"), 1)
                mod_columns(2)
                mod_gate(2)
                z = g_in[:, :, 2 * D:3 * D]
                for t in range(T):
                    dve.wait_ge(S(f"evac{t}"), BLOCKS["in1"] + 7)
                    last = v.tensor_tensor(z[:, t, :], z[:, t, :], g_in[:, t, 0:D], ALU.mult)
                link(last)
                for t in range(T):
                    dve.wait_ge(S("mixed"), t + 1)
                    for g in range(SG):
                        zg = z[:, t, g * 256:(g + 1) * 256]
                        last = v.scalar_tensor_tensor(
                            out=zg, in0=bank[2 + 2 * t + g // 2][:, (g % 2) * 256:(g % 2 + 1) * 256],
                            scalar=bs[:, g:g + 1], in1=zg, op0=ALU.add, op1=ALU.mult)
                    last.then_inc(S("gated"), 1)

            def fox():
                def head_sums(i):
                    dve.wait_ge(S("sq_qk"), i + 1)
                    v.tensor_reduce(ssq[:, 2 * AH * i:2 * AH * (i + 1)],
                                    sqs[:, i, :].rearrange("p (h d) -> p h d", d=DH), X, ALU.add).then_inc(S("ssq"), 1)

                def normal_heads(i, dst):
                    root(f"qk.{i}", 2 * AH, DH, scale=None if i else (2 * AH, DH ** -0.5))
                    for t in range(T):
                        src = f_in[:, t, i * D:(i + 1) * D].rearrange("p (h d) -> p h d", d=DH)
                        r = rstd[:, (i * T + t) * AH:(i * T + t + 1) * AH].unsqueeze(2).to_broadcast([P, AH, DH])
                        link(v.tensor_tensor(src, src, r, ALU.mult))
                        last = v.tensor_tensor(dst[:, t, :, 0:DH], src, gqk[:, i, :].unsqueeze(1).to_broadcast([P, AH, DH]),
                                               ALU.mult)
                    return last

                head_sums(0)
                normal_heads(0, qa)
                head_sums(1)
                dve.wait_ge(S("low"), 2)
                v.tensor_tensor(low[:, :, :], bank[6][:, 0:T * AH].rearrange("p (t n) -> p t n", t=T),
                                bf[:, :].unsqueeze(1).to_broadcast([P, T, AH]), ALU.add).then_inc(S("f_sb"), 1)
                dve.wait_ge(S("lnf"), 1)
                v.scalar_tensor_tensor(out=low2[:, :, :], in0=low[:, :, :], scalar=0.0, in1=low2[:, :, :],
                                       op0=ALU.min, op1=ALU.subtract).then_inc(S("logf"), 1)
                v.memset(qa[:, :, :, DH:DH + 1], 1.0)
                v.memset(ka[:, :, :, DH + 1:DH + 2], 1.0)
                normal_heads(1, ka)
                dve.wait_ge(S("fsum"), 1)
                F = bank[7][:, 0:T * AH].rearrange("p (t h) -> p t h", t=T).unsqueeze(3)
                v.tensor_copy(qa[:, :, :, DH + 1:DH + 2], F)
                v.tensor_scalar(ka[:, :, :, DH:DH + 1], F, -1.0, None, ALU.mult).then_inc(S("qka"), 1)
                quads(0, 4, lambda i: 0, lambda i: fo[:, :, i * 256:(i + 1) * 256])
                mod_columns(3)
                mod_gate(3)
                dve.wait_ge(S("att_o"), 4)
                for t in range(T):
                    dve.wait_ge(S("silu_fox"), t + 1)
                    v.tensor_tensor(fo[:, t, :], fo[:, t, :], f_in[:, t, 3 * D:4 * D], ALU.mult) \
                        .then_inc(S("gated"), 1)

            def angles():
                link(v.tensor_copy(posf[:, :], posi[:, :]))
                ang = acc[:, 0:16].rearrange("p (t r) -> p t r", t=T)
                for t in range(T):
                    link(v.tensor_scalar(ang[:, t, :], freq[:, :], posf[:, t:t + 1], None, ALU.mult))
                for i, (turn, shift) in enumerate(((0.25, np.pi / 2), (0.0, 0.0))):
                    a, r, n = acc[:, 0:16], trig[:, i, :], acc[:, 32:48]
                    link(v.tensor_scalar(n, a, float(1 / (2 * np.pi)), turn, ALU.mult, ALU.add))
                    link(v.tensor_scalar(n, n, MAGIC, None, ALU.add))
                    link(v.tensor_scalar(n, n, MAGIC, None, ALU.subtract))
                    link(v.scalar_tensor_tensor(out=r, in0=n, scalar=-TWO_PI[0], in1=a, op0=ALU.mult, op1=ALU.add))
                    for c in TWO_PI[1:]:
                        link(v.scalar_tensor_tensor(out=r, in0=n, scalar=-c, in1=r, op0=ALU.mult, op1=ALU.add))
                    link(v.tensor_scalar(r, r, float(shift), None, ALU.add))
                    link(v.tensor_scalar(r, r, PI_SAFE, -PI_SAFE, ALU.min, ALU.max), wait=False)
                dve.wait_ge(S("dve_order"), ORDER["dve_order"])
                v.memset(acc[:, 64:65], 0.0).then_inc(S("angles"), 1)

            for t in range(T):
                v.memset(bank[t][:, 0:1], 0.0).then_inc(S(f"evac{t}"), 1)
            dve.wait_ge(S("colsT"), 1)
            v.tensor_copy(cols[:, :], bank[7][:, 0:64]).then_inc(S("colsT_sb"), 1)
            dve.wait_ge(S("colsT_sb"), 1)
            mod_sums(0, 2 * KC)
            mod_columns(0)
            for t in range(T):
                normalized(0, t)
            for t in range(T):
                modulated(0, t)
            for L in range(DEPTH):
                if stop < L + 1:
                    return
                if L == 0:
                    mod_sums(2 * KC, 3 * KC)
                    mod_gate(0)
                    mod_sums(3 * KC, ON_DVE)
                if L == 3:
                    angles()
                if L in (0, 3):
                    gla(L)
                elif L == 1:
                    sgu()
                else:
                    fox()
                for t in range(T):
                    copy_tile(t, "gT", "ghT", base=4 * L)
                output(L)
            if stop < 5:
                return
            for t in range(T):
                dve.wait_ge(S(f"evac{t}"), BLOCKS["qkv"] + 7)
            dve.wait_ge(S("trig"), 1)
            HB = 2 * NG * GHD
            for t in range(T):
                qk = hb[:, t, 0:HB * DH].rearrange("p (h d) -> p h d", d=DH)
                t1, t2 = qk[:, :, 0:ROT], qk[:, :, ROT:2 * ROT]
                cs = trig[:, 0, t * ROT:(t + 1) * ROT].unsqueeze(1).to_broadcast([P, HB, ROT])
                sn = trig[:, 1, t * ROT:(t + 1) * ROT].unsqueeze(1).to_broadcast([P, HB, ROT])
                tmp = [acc[:, t * 1536 + i * 384:t * 1536 + (i + 1) * 384].rearrange("p (h r) -> p h r", r=ROT) for i in range(4)]
                for o, a, b in ((tmp[0], t1, cs), (tmp[1], t2, sn), (tmp[2], t2, cs), (tmp[3], t1, sn)):
                    last = v.tensor_tensor(o, a, b, ALU.mult)
                link(last)
                v.tensor_tensor(t1, tmp[0], tmp[1], ALU.subtract)
                last = v.tensor_tensor(t2, tmp[2], tmp[3], ALU.add)
            link(last)
            v.tensor_scalar(hb[:, :, 0:1536], hb[:, :, 0:1536], DH ** -0.5, None, ALU.mult).then_inc(S("rotated"), 1)
            quads(4, 6, lambda i: 1 + i // 2, lambda i: od[:, :, i // 2, (i % 2) * 256:(i % 2 + 1) * 256])
            for t in range(T):
                dve.wait_ge(S(f"evac{t}"), BLOCKS["gates"] + 1)
            v.tensor_tensor(ha[:, :, D:2 * D], ha[:, :, D:2 * D], ha[:, :, 2 * D:3 * D], ALU.mult) \
                .then_inc(S("z_conv"), 1)
            dve.wait_ge(S("att_o"), 10)
            v.memset(lsm[:, :], 0.0).then_inc(S("lse_in"), 1)
            dve.wait_ge(S("lse_ln"), 1)
            l0, l1 = lse[:, 0, :], lse[:, 1, :]
            link(v.tensor_tensor(l1, l0, anm[:, 4:10, :].rearrange("p n h -> p (n h)"), ALU.subtract))
            link(v.tensor_tensor(lsm[:, :], l1[:, 0:16], l1[:, 16:32], ALU.max))
            link(v.tensor_tensor(lsm[:, :], lsm[:, :], l1[:, 32:48], ALU.max))
            l3 = l1.rearrange("p (g h) -> p g h", g=NG)
            v.tensor_tensor(l3, l3, lsm[:, :].unsqueeze(1).to_broadcast([P, NG, 16]), ALU.subtract) \
                .then_inc(S("lse_m"), 1)
            dve.wait_ge(S("lse_e"), 1)
            link(v.tensor_tensor(lsm[:, :], l0[:, 0:16], l0[:, 16:32], ALU.add))
            link(v.tensor_tensor(lsm[:, :], lsm[:, :], l0[:, 32:48], ALU.add))
            link(v.reciprocal(lsm[:, :], lsm[:, :]))
            link(v.tensor_tensor(l3, l0.rearrange("p (g h) -> p g h", g=NG),
                                 lsm[:, :].unsqueeze(1).to_broadcast([P, NG, 16]), ALU.mult))
            for t in range(T):
                w = l1.rearrange("p (h t) -> p t h", t=T)[:, t, :].unsqueeze(2).to_broadcast([P, NG * GHD, DH])
                o = od[:, t, :, :].rearrange("p g (h d) -> p (g h) d", d=DH)
                last = v.tensor_tensor(o, o, w, ALU.mult)
            link(last)
            link(v.tensor_tensor(od[:, :, 0, :], od[:, :, 0, :], od[:, :, 1, :], ALU.add))
            v.tensor_tensor(od[:, :, 0, :], od[:, :, 0, :], od[:, :, 2, :], ALU.add).then_inc(S("att_merged"), 1)
            v.memset(zT[:, :, 0:2], 0.0)
            for i in range(4):
                dve.wait_ge(S("zT"), i + 1)
                last = v.tensor_copy(zT[:, 2 * i:2 * i + 2, 2:258], bank[2 + i][:, :].rearrange("p (k n) -> p k n", k=2))
            last.then_inc(S("zT_sb"), 1)
            dve.wait_ge(S("zT_sb"), 1)
            for i in range(3):
                for k in range(KC):
                    w = cols[:, 40 + i * KC + k:41 + i * KC + k]
                    if i == 0:
                        last = v.tensor_scalar(cT[:, k, :], zT[:, k, 0:256], w, None, ALU.mult)
                    else:
                        last = v.scalar_tensor_tensor(out=cT[:, k, :], in0=zT[:, k, i:i + 256], scalar=w,
                                                      in1=cT[:, k, :], op0=ALU.mult, op1=ALU.add)
                link(last)
            copy_banks(hT, "oT", "oT_sb", n=2)
            for i in range(4):
                dve.wait_ge(S("bT"), i + 1)
                c = cT[:, 2 * i:2 * i + 2, :].rearrange("p k n -> p (k n)")
                last = v.tensor_tensor(c, c, bank[2 + i][:, :], ALU.mult)
            last.then_inc(S("conv_in"), 1)
            for t in range(T):
                dve.wait_ge(S(f"evac{t}"), BLOCKS["gates"] + 5)
            for t in range(T):
                last = v.tensor_tensor(hb[:, t, GC:GC + 2 * D], hb[:, t, GC:GC + 2 * D],
                                       gbias[:, :, :].rearrange("p a d -> p (a d)"), ALU.add)
            last.then_inc(S("gates_in"), 1)
            dve.wait_ge(S("gates"), 1)
            for t in range(T):
                dve.wait_ge(S(f"evac{t}"), BLOCKS["attn"] + 2)
                last = v.tensor_tensor(ha[:, t, D:2 * D], ha[:, t, D:2 * D], hb[:, t, GA:GA + D], ALU.mult)
            link(last)
            for c in range(2):
                for t in range(T):
                    part = ha[:, t, c * N:(c + 1) * N]
                    g = hb[:, t, GC + c * N:GC + (c + 1) * N]
                    if c == 0:
                        dve.wait_ge(S(f"evac{t}"), BLOCKS["conv"] + 2)
                        link(v.tensor_tensor(part, part, g, ALU.mult))
                    else:
                        dve.wait_ge(S(f"proj_done{t}"), BLOCKS["conv"] + 2)
                        v.tensor_tensor(part, bank[t][:, :], g, ALU.mult).then_inc(S(f"evac{t}"), 1)
                        dve.wait_ge(S(f"evac{t}"), BLOCKS["conv"] + 3)
                    last = v.tensor_tensor(part, part, ha[:, t, D + c * N:D + (c + 1) * N], ALU.add)
                    if c:
                        last.then_inc(S("merged"), 1)
            for t in range(T):
                copy_tile(t, "mT", "mT_sb")
            for t in range(T):
                dve.wait_ge(S(f"evac{t}"), BLOCKS["hyb_out"] + 2)
                v.tensor_tensor(x[:, t, 0:N], x[:, t, 0:N], ha[:, t, 2 * D:2 * D + N], ALU.add)
            for t in range(T):
                dve.wait_ge(S(f"proj_done{t}"), BLOCKS["hyb_out"] + 2)
                v.tensor_tensor(x[:, t, N:D], x[:, t, N:D], bank[t][:, :], ALU.add).then_inc(S("x_ready"), 1)
                dve.wait_ge(S("x_ready"), T * DEPTH + t + 1)
                v.memset(var[:, 0:1], 0.0).then_inc(S(f"evac{t}"), 1)
            if stop < 6:
                return
            dve.wait_ge(S("last_rows_in"), 32)
            for t in range(T):
                r = root(f"ffn.{t}", 1, D)
                v.scalar_tensor_tensor(out=u[:, t, :], in0=x[:, t, :], scalar=r, in1=nffn[:, :],
                                       op0=ALU.mult, op1=ALU.mult).then_inc(S("u_ready"), 1)
            for t in range(T):
                copy_tile(t, "uT", "uT_sb")
            if stop < 7:
                return
            link(v.memset(zero, 0.0), wait=False)

            def best16(vals, pos, src, src2, put):
                dve.nop(nofuse=True)
                for w in range(len(src)):
                    last = v.max(vals[w][:, 0:8], src[w])
                put(last)
                dve.nop(nofuse=True)
                for w in range(len(src)):
                    v.max_index(pos[w][:, 0:8], vals[w][:, 0:8], src[w])
                    last = v.match_replace(src2[w], vals[w][:, 0:8], src[w], -3.0e38)
                put(last)
                dve.nop(nofuse=True)
                for w in range(len(src)):
                    last = v.max(vals[w][:, 8:16], src2[w])
                put(last)
                dve.nop(nofuse=True)
                for w in range(len(src)):
                    last = v.max_index(pos[w][:, 8:16], vals[w][:, 8:16], src2[w])
                put(last)

            def choose(h, par):
                n = [0]

                def put(ins):
                    n[0] += 1
                    ins.then_inc(S("choice"), 1)
                    dve.wait_ge(S("choice"), h * LINKS + n[0])

                put(v.tensor_copy(pk, sc.rearrange("p t n -> p (t n)")[:, ds(h * 256, 256)]))
                best16([pv[:, c, :] for c in range(2)], [pix[:, c, :] for c in range(2)],
                       [pk[:, c * P:(c + 1) * P] for c in range(2)], [pk2[:, c * P:(c + 1) * P] for c in range(2)], put)
                v.tensor_copy(pixf[:, :, :], pix[:, :, :])
                put(v.tensor_tensor(cand, pv[:, 0, :].unsqueeze(2).to_broadcast([P, TOPK, TOPK]),
                                    pv[:, 1, :].unsqueeze(1).to_broadcast([P, TOPK, TOPK]), ALU.add))
                best16([pbest[:, par, :]], [ppos[:, :]], [cand.rearrange("p a b -> p (a b)")], [cand2], put)
                put(v.tensor_scalar(pneg[:, par, :], pbest[:, par, 0:1], -1.0, None, ALU.mult))
                assert n[0] == BEST
                v.tensor_single_scalar(pab[:, 0, :], ppos[:, :], 4, ALU.logical_shift_right)
                put(v.tensor_single_scalar(pab[:, 1, :], ppos[:, :], 15, ALU.bitwise_and))
                put(v.tensor_copy(pabf[:, :, :], pab[:, :, :]))
                for c in range(2):
                    put(v.tensor_tensor(hot[:, c, :, :], iota[:, :].unsqueeze(1).to_broadcast([P, TOPK, TOPK]),
                                        pabf[:, c, :].unsqueeze(2).to_broadcast([P, TOPK, TOPK]), ALU.is_equal))
                for c in range(2):
                    put(v.tensor_tensor(hot[:, c, :, :], hot[:, c, :, :],
                                        pixf[:, c, :].unsqueeze(1).to_broadcast([P, TOPK, TOPK]), ALU.mult))
                for c in range(2):
                    put(v.tensor_reduce(psel[:, c, :], hot[:, c, :, :], X, ALU.add))
                put(v.scalar_tensor_tensor(out=pidf[:, :], in0=psel[:, 0, :], scalar=float(NK), in1=psel[:, 1, :],
                                           op0=ALU.mult, op1=ALU.add))
                assert n[0] == LINKS, n[0]

            def dots(h, par, t):
                for e in range(TOPK):
                    s = e % SLOTS
                    dve.wait_ge(S(f"dn_landed{s}"), (h * 2 + e // SLOTS + 1) * 16)
                    v.tensor_tensor_reduce(out=dn[s], in0=dn[s], in1=u[:, t, :], scale=1.0, scalar=0.0,
                                           op0=ALU.mult, op1=ALU.add, accum_out=pa[:, par, e:e + 1]) \
                        .then_inc(S(f"dn_used{s}"), 1)

            def weights(h, par):
                dve.wait_ge(S("pexp"), h + 1)
                v.reciprocal(psm[:, par, :], psm[:, par, :]).then_inc(S("coef_step"), 1)
                dve.wait_ge(S("gelu"), h + 1)
                dve.wait_ge(S("coef_step"), h + 1)
                v.scalar_tensor_tensor(out=pcoef[:, par, :], in0=pa[:, par, :], scalar=psm[:, par, :],
                                       in1=pex[:, par, :], op0=ALU.mult, op1=ALU.mult).then_inc(S("coef"), 1)

            def pick_dn(par):
                v.tensor_copy(idx[:, par, :], pidf[:, :]).then_inc(S("dn_picks"), 1)

            def pick_up(h, par):
                dve.wait_ge(S("dn_picks"), h + 1)
                v.tensor_copy(idxu[:, par, :], idx[:, par, :]).then_inc(S("up_picks"), 1)

            for s in range(SLOTS):
                v.memset(dn[s][:, 0:1], 0.0).then_inc(S(f"dn_used{s}"), 1)
            dve.wait_ge(S("sc_sb"), 1)
            for h in range(2):
                choose(h, h)
                pick_dn(h)
            pick_up(0, 0)
            dots(0, 0, 0)
            dve.wait_ge(S("sc_sb"), 4)
            for s in range(SLOTS):
                v.memset(up[:, s, 0:1], 0.0).then_inc(S(f"up_used{s}"), 1)
            for t in range(T):
                def two_heads(h, cross=False):
                    final = cross and t == T - 1
                    for half in range(2):
                        if not (final and half):
                            dots(h + half + 1, 1 - half, t + (cross and half))
                        weights(h + half, half)
                        if not final:
                            choose(h + half + 2, half)
                            pick_dn(half)
                        if not (final and half):
                            dve.wait_ge(S(f"up_used{SLOTS - 1}"), (h + half) * 2 + 1)
                            pick_up(h + half + 1, 1 - half)
                with dve.Fori(0, PH // 2 - 1) as i:
                    two_heads(i * 2 + t * PH)
                two_heads((t + 1) * PH - 2, cross=True)
            for t in range(T):
                dve.wait_ge(S("sq_final"), t + 1)
                last = v.tensor_tensor(ssq[:, t:t + 1], sqf[:, 2 * t:2 * t + 1], sqf[:, 2 * t + 1:2 * t + 2], ALU.add)
            last.then_inc(S("ssq"), 1)
            root("final", T, D)
            for t in range(T):
                for c in range(2):
                    last = v.scalar_tensor_tensor(out=at(t * D + c * N, N), in0=bank[2 * t + c][:, :],
                                                  scalar=rstd[:, t:t + 1], in1=fin[:, c * N:(c + 1) * N],
                                                  op0=ALU.mult, op1=ALU.mult)
                last.then_inc(S("out_ready"), 1)


_INS = ["x", "c", "norm_pre_g", "norm_post_g", "w_mod", "b_mod", "gla_w_in", "gla_w_a2", "gla_b_a",
        "gla_g_head", "gla_w_out", "sgu_w_in", "sgu_ln_g", "sgu_ln_b", "sgu_w_s", "sgu_b_s",
        "sgu_w_out", "fox_w_in", "fox_b_f", "fox_g_q", "fox_g_k", "fox_w_out", "positions_2",
        "norm_mix_2", "w_in_2", "conv_w_2", "w_conv_out_2", "w_attn_out_2", "gate_bias_2", "w_out_2",
        "norm_ffn_2", "peer_w_query_2", "peer_sub_keys_2", "peer_down_2", "peer_up_2", "final_norm_2"]


def kernel(**inputs):
    import concourse.bacc as bacc
    from concourse.bass_utils import run_bass_kernel_spmd

    nc = bacc.Bacc("TRN2", target_bir_lowering=False, num_devices=1)
    data = {name: np.ascontiguousarray(inputs[name]) for name in _INS}
    data.update(constants())
    arrays, views = {}, {}
    for name, a in data.items():
        arrays[f"in_{name}"] = a
        views[name] = nc.dram_tensor(f"in_{name}", a.shape, mybir.dt.from_np(a.dtype), kind="ExternalInput").ap()
    out = nc.dram_tensor("out_0", (1, T * P, D), F32, kind="ExternalOutput").ap()
    build(nc, views, out)
    r = run_bass_kernel_spmd(nc, [arrays], core_ids=[0])
    return r.results[0]["out_0"]
```
